# Optimizing a Trainium2 kernel written in Bass

```python
import jax
import jax.numpy as jnp
from jax import lax
import numpy as np
import math
import jax, jax.numpy as jnp

D_MODEL = 1024
BATCH = 1
SEQ = 512
DEPTH = 1

HEAD_DIM = 64
ROPE_THETA = 10000.0
RMS_EPS = 1e-6
NEG_INF = -1e30
Q_BLOCK = 64

A_HEADS = 8
IDX_HEADS = 8
IDX_DIM = 32
DSA_TOPK_MAX = 256

B_HEADS = 8
B_KV_HEADS = 2
B_GROUP = B_HEADS // B_KV_HEADS
CMP_LEN = 32
CMP_STRIDE = 16
CMP_HIDDEN = 128
SLC_LEN = 64
SLC_TOPN = 16
WINDOW = 512

N_GROUPS = 4
EXPERTS_PER_GROUP = 8
N_EXPERTS = N_GROUPS * EXPERTS_PER_GROUP
TOP_K_INNER = 2
D_EXPERT = 256
MOE_BLOCK = 256

IN_SPLITS = (A_HEADS * HEAD_DIM, HEAD_DIM, HEAD_DIM, IDX_HEADS * IDX_DIM, IDX_DIM, IDX_HEADS,
             B_HEADS * HEAD_DIM, 6 * B_KV_HEADS * HEAD_DIM, 3 * B_HEADS, D_MODEL, D_MODEL)
IN_WIDTH = sum(IN_SPLITS)
SPLIT_POINTS = tuple(int(v) for v in np.cumsum(IN_SPLITS)[:-1])


def rmsnorm(x, g):
    xf = x.astype(jnp.float32)
    y = xf * lax.rsqrt(jnp.mean(xf * xf, axis=-1, keepdims=True) + RMS_EPS)
    return (y * g.astype(jnp.float32)).astype(x.dtype)

def rope(x, pos):
    half = x.shape[-1] // 2
    inv_freq = ROPE_THETA ** (-jnp.arange(half, dtype=jnp.float32) / half)
    ang = pos.astype(jnp.float32)[:, :, None] * inv_freq
    cos = jnp.cos(ang)[:, :, None, :]
    sin = jnp.sin(ang)[:, :, None, :]
    xf = x.astype(jnp.float32)
    x1, x2 = xf[..., :half], xf[..., half:]
    return jnp.concatenate([x1 * cos - x2 * sin, x1 * sin + x2 * cos], axis=-1).astype(x.dtype)

def masked_softmax(s, mask):
    p = jax.nn.softmax(jnp.where(mask, s.astype(jnp.float32), NEG_INF), axis=-1)
    return jnp.where(mask, p, 0.0)

def _rows(a, t0):
    return lax.dynamic_slice_in_dim(a, t0, Q_BLOCK, axis=1)

def dsa_attention(q, k, v, qi, ki, wi):
    bsz, L = q.shape[0], q.shape[1]
    k_sel = min(DSA_TOPK_MAX, L // 4)
    key_pos = jnp.arange(L)
    b_ix = jnp.arange(bsz)[:, None, None]
    scale = HEAD_DIM ** -0.5

    def block(i):
        t0 = i * Q_BLOCK
        qpos = t0 + jnp.arange(Q_BLOCK)
        causal = (key_pos[None, :] <= qpos[:, None])[None]
        idx_logit = jax.nn.relu(jnp.einsum('bthd,bsd->bths', _rows(qi, t0), ki))
        score = jnp.einsum('bth,bths->bts', _rows(wi, t0), idx_logit).astype(jnp.float32)
        score = jnp.where(causal, score, -jnp.inf)
        _, sel = lax.top_k(score, k_sel)
        ks = k[b_ix, sel]
        vs = v[b_ix, sel]
        s = jnp.einsum('bthd,btkd->bthk', _rows(q, t0), ks) * scale
        mask = (sel <= qpos[None, :, None])[:, :, None, :]
        p = masked_softmax(s, mask).astype(vs.dtype)
        return jnp.einsum('bthk,btkd->bthd', p, vs)

    out = lax.map(block, jnp.arange(L // Q_BLOCK))
    return out.transpose(1, 0, 2, 3, 4).reshape(bsz, L, A_HEADS * HEAD_DIM)

def compress_tokens(kv, pe, w1, w2):
    bsz, L, hk, dh = kv.shape
    n_cmp = (L - CMP_LEN) // CMP_STRIDE + 1
    idx = np.arange(n_cmp)[:, None] * CMP_STRIDE + np.arange(CMP_LEN)[None, :]
    blocks = kv[:, idx] + pe[:, None, :]
    z = blocks.transpose(0, 1, 3, 2, 4).reshape(bsz, n_cmp, hk, CMP_LEN * dh)
    return jax.nn.silu(z @ w1) @ w2

def nsa_attention(q_nope, q_rope, k_cmp, v_cmp, k_slc, v_slc, k_win, v_win, gates,
                  pe_k, w1_k, w2_k, pe_v, w1_v, w2_v):
    bsz, L = q_nope.shape[0], q_nope.shape[1]
    scale = HEAD_DIM ** -0.5
    kc = compress_tokens(k_cmp, pe_k, w1_k, w2_k)
    vc = compress_tokens(v_cmp, pe_v, w1_v, w2_v)
    n_cmp = kc.shape[1]
    cmp_start = np.arange(n_cmp) * CMP_STRIDE
    cmp_end = jnp.asarray(cmp_start + CMP_LEN - 1)
    n_slc = L // SLC_LEN
    n_sel = min(SLC_TOPN, n_slc)
    slc_start = np.arange(n_slc) * SLC_LEN
    overlap = (cmp_start[:, None] < slc_start[None, :] + SLC_LEN) & (cmp_start[:, None] + CMP_LEN > slc_start[None, :])
    cmp_to_slc = jnp.asarray(overlap.astype(np.float32))
    k_blk = k_slc.reshape(bsz, n_slc, SLC_LEN, B_KV_HEADS, HEAD_DIM).transpose(0, 3, 1, 2, 4)
    v_blk = v_slc.reshape(bsz, n_slc, SLC_LEN, B_KV_HEADS, HEAD_DIM).transpose(0, 3, 1, 2, 4)
    k_pad = jnp.pad(k_win, ((0, 0), (WINDOW, 0), (0, 0), (0, 0)))
    v_pad = jnp.pad(v_win, ((0, 0), (WINDOW, 0), (0, 0), (0, 0)))
    b_ix = jnp.arange(bsz)[:, None, None, None]
    h_ix = jnp.arange(B_KV_HEADS)[None, None, :, None]
    j_ix = jnp.arange(n_slc)

    def block(i):
        t0 = i * Q_BLOCK
        qpos = t0 + jnp.arange(Q_BLOCK)
        qn = _rows(q_nope, t0).reshape(bsz, Q_BLOCK, B_KV_HEADS, B_GROUP, HEAD_DIM)
        qr = _rows(q_rope, t0).reshape(bsz, Q_BLOCK, B_KV_HEADS, B_GROUP, HEAD_DIM)
        g = _rows(gates, t0)
        s = jnp.einsum('btkgd,bnkd->btkgn', qn, kc) * scale
        m_cmp = (cmp_end[None, :] <= qpos[:, None])[None, :, None, None, :]
        p_cmp = masked_softmax(s, m_cmp)
        o_cmp = jnp.einsum('btkgn,bnkd->btkgd', p_cmp.astype(vc.dtype), vc)
        imp = jnp.einsum('btkgn,nj->btkj', p_cmp, cmp_to_slc)
        admiss = j_ix[None, :] * SLC_LEN <= qpos[:, None]
        cur = qpos[:, None] // SLC_LEN
        forced = admiss & ((j_ix[None, :] == 0) | (j_ix[None, :] == cur) | (j_ix[None, :] == cur - 1))
        score = jnp.where(admiss[None, :, None, :], imp, -jnp.inf)
        score = jnp.where(forced[None, :, None, :], jnp.inf, score)
        _, sel = lax.top_k(score, n_sel)
        ks = k_blk[b_ix, h_ix, sel].reshape(bsz, Q_BLOCK, B_KV_HEADS, n_sel * SLC_LEN, HEAD_DIM)
        vs = v_blk[b_ix, h_ix, sel].reshape(bsz, Q_BLOCK, B_KV_HEADS, n_sel * SLC_LEN, HEAD_DIM)
        tok = (sel[..., None] * SLC_LEN + jnp.arange(SLC_LEN)).reshape(bsz, Q_BLOCK, B_KV_HEADS, n_sel * SLC_LEN)
        m_sel = (tok <= qpos[None, :, None, None])[:, :, :, None, :]
        s = jnp.einsum('btkgd,btksd->btkgs', qr, ks) * scale
        p = masked_softmax(s, m_sel).astype(vs.dtype)
        o_slc = jnp.einsum('btkgs,btksd->btkgd', p, vs)
        kw = lax.dynamic_slice_in_dim(k_pad, t0, WINDOW + Q_BLOCK, axis=1)
        vw = lax.dynamic_slice_in_dim(v_pad, t0, WINDOW + Q_BLOCK, axis=1)
        kpos = t0 - WINDOW + jnp.arange(WINDOW + Q_BLOCK)
        rel = qpos[:, None] - kpos[None, :]
        m_win = ((rel >= 0) & (rel < WINDOW) & (kpos[None, :] >= 0))[None, :, None, None, :]
        s = jnp.einsum('btkgd,bskd->btkgs', qr, kw) * scale
        p = masked_softmax(s, m_win).astype(vw.dtype)
        o_win = jnp.einsum('btkgs,bskd->btkgd', p, vw)
        gc = g[:, :, 0].reshape(bsz, Q_BLOCK, B_KV_HEADS, B_GROUP, 1)
        gs = g[:, :, 1].reshape(bsz, Q_BLOCK, B_KV_HEADS, B_GROUP, 1)
        gw = g[:, :, 2].reshape(bsz, Q_BLOCK, B_KV_HEADS, B_GROUP, 1)
        o = gc * o_cmp + gs * o_slc + gw * o_win
        return o.reshape(bsz, Q_BLOCK, B_HEADS * HEAD_DIM)

    out = lax.map(block, jnp.arange(L // Q_BLOCK))
    return out.transpose(1, 0, 2, 3).reshape(bsz, L, B_HEADS * HEAD_DIM)

def mixer_layer(h, positions, w_in, pe_k, w1_k, w2_k, pe_v, w1_v, w2_v, w_br_a, w_br_b, w_out):
    bsz, L, _ = h.shape
    proj = jnp.einsum('bsd,dc->bsc', h, w_in)
    qa, ka, va, qi, ki, wi, qb, kvb, gb, gate_a, gate_b = jnp.split(proj, SPLIT_POINTS, axis=-1)
    qa = rope(qa.reshape(bsz, L, A_HEADS, HEAD_DIM), positions)
    ka = rope(ka[:, :, None, :], positions)[:, :, 0]
    qi = rope(qi.reshape(bsz, L, IDX_HEADS, IDX_DIM), positions)
    ki = rope(ki[:, :, None, :], positions)[:, :, 0]
    o_a = dsa_attention(qa, ka, va, qi, ki, wi)
    qb = qb.reshape(bsz, L, B_HEADS, HEAD_DIM)
    kvb = kvb.reshape(bsz, L, 6, B_KV_HEADS, HEAD_DIM)
    k_cmp, v_cmp = kvb[:, :, 0], kvb[:, :, 1]
    k_slc, v_slc = rope(kvb[:, :, 2], positions), kvb[:, :, 3]
    k_win, v_win = rope(kvb[:, :, 4], positions), kvb[:, :, 5]
    nsa_gates = jax.nn.sigmoid(gb.reshape(bsz, L, 3, B_HEADS))
    o_b = nsa_attention(qb, rope(qb, positions), k_cmp, v_cmp, k_slc, v_slc, k_win, v_win, nsa_gates,
                        pe_k, w1_k, w2_k, pe_v, w1_v, w2_v)
    merged = jax.nn.sigmoid(gate_a) * (o_a @ w_br_a) + jax.nn.sigmoid(gate_b) * (o_b @ w_br_b)
    return merged @ w_out

def hier_moe(h, w_group, b_group, w_expert, b_expert, w_gate_up, w_down):
    bsz, L, d = h.shape
    n_tok = bsz * L
    tok = h.reshape(n_tok, d)
    g_logit = jnp.einsum('nd,dg->ng', tok, w_group).astype(jnp.float32) + b_group.astype(jnp.float32)
    g_prob = jax.nn.softmax(g_logit, axis=-1)
    g_sel = jnp.argmax(g_logit, axis=-1)
    e_logit = jnp.einsum('nd,de->ne', tok, w_expert).astype(jnp.float32) + b_expert.astype(jnp.float32)
    e_in = jnp.take_along_axis(e_logit.reshape(n_tok, N_GROUPS, EXPERTS_PER_GROUP), g_sel[:, None, None], axis=1)[:, 0]
    top_val, top_idx = lax.top_k(e_in, TOP_K_INNER)
    weight = jnp.take_along_axis(g_prob, g_sel[:, None], axis=1) * jax.nn.softmax(top_val, axis=-1)
    expert = g_sel[:, None] * EXPERTS_PER_GROUP + top_idx
    n_asg = n_tok * TOP_K_INNER
    e_flat = expert.reshape(n_asg)
    tok_flat = jnp.repeat(jnp.arange(n_tok), TOP_K_INNER)
    w_flat = weight.reshape(n_asg)
    order = jnp.argsort(e_flat)
    e_s, tok_s, w_s = e_flat[order], tok_flat[order], w_flat[order]
    counts = jnp.bincount(e_flat, length=N_EXPERTS)
    starts = jnp.cumsum(counts) - counts
    padded = (counts + MOE_BLOCK - 1) // MOE_BLOCK * MOE_BLOCK
    pad_end = jnp.cumsum(padded)
    pad_start = pad_end - padded
    dest = pad_start[e_s] + jnp.arange(n_asg) - starts[e_s]
    n_blocks = -(-n_asg // MOE_BLOCK) + N_EXPERTS
    buf = jnp.zeros((n_blocks * MOE_BLOCK, d), h.dtype).at[dest].set(tok[tok_s])
    blk_expert = jnp.minimum(jnp.searchsorted(pad_end, jnp.arange(n_blocks) * MOE_BLOCK, side='right'), N_EXPERTS - 1)

    def run(args):
        xb, e = args
        gate, up = jnp.split(xb @ w_gate_up[e], 2, axis=-1)
        return (jax.nn.silu(gate) * up) @ w_down[e]

    y_buf = lax.map(run, (buf.reshape(n_blocks, MOE_BLOCK, d), blk_expert)).reshape(n_blocks * MOE_BLOCK, d)
    y = jax.ops.segment_sum(y_buf[dest] * w_s[:, None].astype(h.dtype), tok_s, num_segments=n_tok)
    return y.reshape(bsz, L, d)

def first_inputs(seed: int = 0) -> dict:
    key = jax.random.key(seed)
    ks = jax.random.split(key, 24)

    def nrm(k, shape, scale):
        return jax.random.normal(k, shape, jnp.float32) * scale

    cmp_in = CMP_LEN * HEAD_DIM
    a_w = A_HEADS * HEAD_DIM
    b_w = B_HEADS * HEAD_DIM
    offs = jax.random.randint(ks[1], (BATCH, 1), 0, 1024, dtype=jnp.int32)
    return {
        "x": nrm(ks[0], (BATCH, SEQ, D_MODEL), 1.0),
        "positions": offs + jnp.arange(SEQ, dtype=jnp.int32)[None, :],
        "norm_mix": 1.0 + nrm(ks[2], (DEPTH, D_MODEL), 0.02),
        "w_in": nrm(ks[3], (DEPTH, D_MODEL, IN_WIDTH), D_MODEL ** -0.5),
        "pe_k": nrm(ks[4], (DEPTH, CMP_LEN, HEAD_DIM), 0.1),
        "w1_k": nrm(ks[5], (DEPTH, cmp_in, CMP_HIDDEN), cmp_in ** -0.5),
        "w2_k": nrm(ks[6], (DEPTH, CMP_HIDDEN, HEAD_DIM), CMP_HIDDEN ** -0.5),
        "pe_v": nrm(ks[7], (DEPTH, CMP_LEN, HEAD_DIM), 0.1),
        "w1_v": nrm(ks[8], (DEPTH, cmp_in, CMP_HIDDEN), cmp_in ** -0.5),
        "w2_v": nrm(ks[9], (DEPTH, CMP_HIDDEN, HEAD_DIM), CMP_HIDDEN ** -0.5),
        "w_br_a": nrm(ks[10], (DEPTH, a_w, D_MODEL), a_w ** -0.5),
        "w_br_b": nrm(ks[11], (DEPTH, b_w, D_MODEL), b_w ** -0.5),
        "w_out": nrm(ks[12], (DEPTH, D_MODEL, D_MODEL), D_MODEL ** -0.5),
        "norm_ffn": 1.0 + nrm(ks[13], (DEPTH, D_MODEL), 0.02),
        "w_group": nrm(ks[14], (DEPTH, D_MODEL, N_GROUPS), D_MODEL ** -0.5),
        "b_group": nrm(ks[15], (DEPTH, N_GROUPS), 0.01),
        "w_expert": nrm(ks[16], (DEPTH, D_MODEL, N_EXPERTS), D_MODEL ** -0.5),
        "b_expert": nrm(ks[17], (DEPTH, N_EXPERTS), 0.01),
        "w_gate_up": nrm(ks[18], (DEPTH, N_EXPERTS, D_MODEL, 2 * D_EXPERT), D_MODEL ** -0.5),
        "w_down": nrm(ks[19], (DEPTH, N_EXPERTS, D_EXPERT, D_MODEL), D_EXPERT ** -0.5),
        "norm_final": 1.0 + nrm(ks[20], (D_MODEL,), 0.02),
    }

def first_block(x, positions, norm_mix, w_in, pe_k, w1_k, w2_k, pe_v, w1_v, w2_v, w_br_a, w_br_b,
              w_out, norm_ffn, w_group, b_group, w_expert, b_expert, w_gate_up, w_down, norm_final):
    for l in range(DEPTH):
        h = rmsnorm(x, norm_mix[l])
        x = x + mixer_layer(h, positions, w_in[l], pe_k[l], w1_k[l], w2_k[l], pe_v[l], w1_v[l], w2_v[l],
                            w_br_a[l], w_br_b[l], w_out[l])
        h = rmsnorm(x, norm_ffn[l])
        x = x + hier_moe(h, w_group[l], b_group[l], w_expert[l], b_expert[l], w_gate_up[l], w_down[l])
    return rmsnorm(x, norm_final)


DEPTH_2 = 2

MIX_WIDTH = D_MODEL
ATT_WIDTH = MIX_WIDTH // 2
FOURIER_WIDTH = MIX_WIDTH - ATT_WIDTH
N_HEADS = 8
HEAD_DIM_2 = ATT_WIDTH // (2 * N_HEADS)
V_HEAD_DIM = 2 * HEAD_DIM_2
N_FGROUPS = 4
FGROUP_DIM = FOURIER_WIDTH // N_FGROUPS
IN_COLS = 3 * ATT_WIDTH + FOURIER_WIDTH
D_FF = ((8 * D_MODEL + 3 * 256 - 1) // (3 * 256)) * 256
Q_BLOCK_2 = 128
LN_EPS = 1e-5
SUBLN_EPS = 1e-5
ALPHA = (2.0 * DEPTH_2) ** 0.25
BETA = (8.0 * DEPTH_2) ** -0.25
LAMBDA_STD = 0.1


def layer_norm(x, g, b):
    x32 = x.astype(jnp.float32)
    mu = jnp.mean(x32, axis=-1, keepdims=True)
    var = jnp.mean(jnp.square(x32 - mu), axis=-1, keepdims=True)
    return ((x32 - mu) * lax.rsqrt(var + LN_EPS) * g + b).astype(x.dtype)

def lambda_init_fn(layer_idx):
    return 0.8 - 0.6 * math.exp(-0.3 * layer_idx)

def diff_attention(q, k, v, lam, lam_init, subln_g):
    B, S = q.shape[0], q.shape[1]
    nb = S // Q_BLOCK_2
    slopes = jnp.exp2(-8.0 * jnp.arange(1, N_HEADS + 1, dtype=jnp.float32) / N_HEADS)
    kpos = jnp.arange(S, dtype=jnp.float32)
    scale = HEAD_DIM_2 ** -0.5
    qb = q.reshape(B, nb, Q_BLOCK_2, N_HEADS, 2, HEAD_DIM_2).transpose(1, 0, 2, 3, 4, 5)
    starts = jnp.arange(nb, dtype=jnp.float32) * Q_BLOCK_2

    def block(args):
        qi, start = args
        s = jnp.einsum('bqhcd,bkhcd->bhcqk', qi, k).astype(jnp.float32) * scale
        qpos = start + jnp.arange(Q_BLOCK_2, dtype=jnp.float32)
        dist = jnp.abs(qpos[:, None] - kpos[None, :])
        s = s - slopes[:, None, None, None] * dist[None, None]
        p = jax.nn.softmax(s, axis=-1)
        a = p[:, :, 0] - lam * p[:, :, 1]
        o = jnp.einsum('bhqk,bkhd->bqhd', a.astype(v.dtype), v).astype(jnp.float32)
        o = o * lax.rsqrt(jnp.mean(jnp.square(o), axis=-1, keepdims=True) + SUBLN_EPS)
        o = o * subln_g * (1.0 - lam_init)
        return o.astype(v.dtype)

    out = lax.map(block, (qb, starts))
    return out.transpose(1, 0, 2, 3, 4).reshape(B, S, N_HEADS * V_HEAD_DIM)

def fourier_mix(u, w_f, b_f):
    B, S = u.shape[0], u.shape[1]
    ug = u.reshape(B, S, N_FGROUPS, FGROUP_DIM).astype(jnp.float32)
    f = jnp.fft.fft(ug, axis=3, norm='ortho')
    f = jnp.fft.fft(f, axis=1, norm='ortho').real.astype(u.dtype)
    y = jnp.einsum('bsgc,gcd->bsgd', f, w_f)
    return y.reshape(B, S, FOURIER_WIDTH) + b_f

def swiglu(h, w_gu, w_down):
    gu = jnp.einsum('bsd,df->bsf', h, w_gu)
    g, up = gu[..., :D_FF], gu[..., D_FF:]
    return jnp.einsum('bsf,fd->bsd', jax.nn.silu(g) * up, w_down)

def second_inputs(seed: int = 0) -> dict:
    key = jax.random.key(seed)
    ks = jax.random.split(key, 16)
    f32 = jnp.float32
    nrm = lambda k, shape: jax.random.normal(k, shape, f32)
    return {
        'x': nrm(ks[0], (BATCH, SEQ, D_MODEL)),
        'ln_in_g': 1.0 + 0.01 * nrm(ks[1], (D_MODEL,)),
        'ln_in_b': 0.01 * nrm(ks[2], (D_MODEL,)),
        'w_in': nrm(ks[3], (DEPTH_2, D_MODEL, IN_COLS)) * D_MODEL ** -0.5,
        'lam_params': LAMBDA_STD * nrm(ks[4], (DEPTH_2, 4, HEAD_DIM_2)),
        'subln_g': 1.0 + 0.01 * nrm(ks[5], (DEPTH_2, V_HEAD_DIM)),
        'w_f': nrm(ks[6], (DEPTH_2, N_FGROUPS, FGROUP_DIM, FGROUP_DIM)) * FGROUP_DIM ** -0.5,
        'b_f': 0.01 * nrm(ks[7], (DEPTH_2, FOURIER_WIDTH)),
        'w_o': nrm(ks[8], (DEPTH_2, MIX_WIDTH, D_MODEL)) * (MIX_WIDTH ** -0.5 * BETA),
        'ln1_g': 1.0 + 0.01 * nrm(ks[9], (DEPTH_2, D_MODEL)),
        'ln1_b': 0.01 * nrm(ks[10], (DEPTH_2, D_MODEL)),
        'w_gu': nrm(ks[11], (DEPTH_2, D_MODEL, 2 * D_FF)) * D_MODEL ** -0.5,
        'w_down': nrm(ks[12], (DEPTH_2, D_FF, D_MODEL)) * (D_FF ** -0.5 * BETA),
        'ln2_g': 1.0 + 0.01 * nrm(ks[13], (DEPTH_2, D_MODEL)),
        'ln2_b': 0.01 * nrm(ks[14], (DEPTH_2, D_MODEL)),
    }

def second_block(x, ln_in_g, ln_in_b, w_in, lam_params, subln_g, w_f, b_f, w_o,
              ln1_g, ln1_b, w_gu, w_down, ln2_g, ln2_b):
    B, S = x.shape[0], x.shape[1]
    h = layer_norm(x, ln_in_g, ln_in_b)
    for l in range(DEPTH_2):
        lam_init = lambda_init_fn(l)
        proj = jnp.einsum('bsd,de->bse', h, w_in[l])
        q = proj[..., :ATT_WIDTH].reshape(B, S, N_HEADS, 2, HEAD_DIM_2)
        k = proj[..., ATT_WIDTH:2 * ATT_WIDTH].reshape(B, S, N_HEADS, 2, HEAD_DIM_2)
        v = proj[..., 2 * ATT_WIDTH:3 * ATT_WIDTH].reshape(B, S, N_HEADS, V_HEAD_DIM)
        u = proj[..., 3 * ATT_WIDTH:]
        lp = lam_params[l].astype(jnp.float32)
        lam = jnp.exp(jnp.sum(lp[0] * lp[1])) - jnp.exp(jnp.sum(lp[2] * lp[3])) + lam_init
        a = diff_attention(q, k, v, lam, lam_init, subln_g[l])
        f = fourier_mix(u, w_f[l], b_f[l])
        mix = jnp.einsum('bse,ed->bsd', jnp.concatenate([a, f], axis=-1), w_o[l])
        h = layer_norm(ALPHA * h + mix, ln1_g[l], ln1_b[l])
        h = layer_norm(ALPHA * h + swiglu(h, w_gu[l], w_down[l]), ln2_g[l], ln2_b[l])
    return h


def setup_inputs(seed=0):
    out = dict(first_inputs(seed))
    for name, value in second_inputs(seed + 1).items():
        if name != "x":
            out[name + "_2"] = value
    return out


def reference(
    x, positions, norm_mix, w_in, pe_k, w1_k, w2_k, pe_v, w1_v, w2_v, w_br_a, w_br_b, w_out,
    norm_ffn, w_group, b_group, w_expert, b_expert, w_gate_up, w_down, norm_final, ln_in_g_2,
    ln_in_b_2, w_in_2, lam_params_2, subln_g_2, w_f_2, b_f_2, w_o_2, ln1_g_2, ln1_b_2, w_gu_2,
    w_down_2, ln2_g_2, ln2_b_2,
):
    x = first_block(
        x, positions, norm_mix, w_in, pe_k, w1_k, w2_k, pe_v, w1_v, w2_v, w_br_a, w_br_b, w_out,
        norm_ffn, w_group, b_group, w_expert, b_expert, w_gate_up, w_down, norm_final,
    )
    return second_block(
        x, ln_in_g_2, ln_in_b_2, w_in_2, lam_params_2, subln_g_2, w_f_2, b_f_2, w_o_2, ln1_g_2,
        ln1_b_2, w_gu_2, w_down_2, ln2_g_2, ln2_b_2,
    )


_drawn_inputs = setup_inputs


def setup_inputs(seed=0):
    import zlib

    import numpy as np

    out = dict(_drawn_inputs(seed))
    spreads = {}
    factors = {'pe_k': 8.0,
     'b_group': 8.0,
     'b_expert': 8.0,
     'norm_final': 2.699,
     'ln_in_g_2': 5.126,
     'ln_in_b_2': 3.022,
     'subln_g_2': 38.45,
     'b_f_2': 34.529,
     'ln1_g_2': 3.953,
     'ln1_b_2': 3.587,
     'ln2_g_2': 3.871,
     'ln2_b_2': 10.131}
    for name, (base, spread) in spreads.items():
        noise = np.random.default_rng([zlib.crc32(name.encode()), seed]).standard_normal(out[name].shape)
        drawn = base * np.exp(spread * noise) if base else spread * noise
        out[name] = jnp.asarray(drawn.astype(out[name].dtype))
    for name, factor in factors.items():
        out[name] = (out[name] * factor).astype(out[name].dtype)
    return out
```

```python
from contextlib import ExitStack

import math

import numpy as np

import concourse.bass as bass
from concourse import mybir

F32 = mybir.dt.float32
F32R = mybir.dt.float32r
I32 = mybir.dt.int32
U32 = mybir.dt.uint32
ALU = mybir.AluOpType
ACT = mybir.ActivationFunctionType
AX = mybir.AxisListType.X

P = 128
S = 512
D = 1024
NT = S // P
KD = D // P
HD = 64
TOPK = 128
NEXP = 32
CAP = 128
NOVER = 7
TCOLS = 40
NFF = 22
BIG = 1e30
FAR = 1 << 20
ALPHA = (2.0 * 2) ** 0.25

RAW = 4
HL = 3


class Queue:

    def __init__(self, eng, name):
        self.eng, self.name, self.seen, self.sem, self.n, self.loose = eng, name, {}, None, 0, False

    def wait(self, *toks):
        for t in toks:
            if t is None:
                continue
            if isinstance(t, list):
                self.wait(*t)
            elif self.seen.get(t[0], 0) < t[1]:
                self.seen[t[0]] = t[1]
                self.eng.wait_ge(t[0], t[1])

    def do(self, fn, *toks):
        self.wait(*toks)
        self.n += 1
        self.loose = False
        fn(self.eng).then_inc(self.sem, 1)
        return (self.sem, self.n)

    def go(self, fn, *toks):
        self.wait(*toks)
        self.loose = True
        fn(self.eng)

    def last(self):
        assert not self.loose
        return (self.sem, self.n) if self.n else None


class Slot:

    def __init__(self, key):
        self.key, self.n = key, 0


def dma(q, slot, out, in_, *toks):
    q.wait(*toks)
    slot.n += 16
    q.eng.dma_start(out, in_).then_inc(slot.key, 16)
    return (slot.key, slot.n)


class Memory:

    def __init__(self, nc):
        self.nc, self.n = nc, 0
        self.base = (nc.sbuf_base + 63) // 64 * 64
        self.size = (nc.sbuf_usable_end - self.base) // 32 * 8
        self.pos, self.top = 0, 0

    def place(self, dt, *dims):
        n = int(np.prod(dims))
        t = self.nc.alloc_sbuf_tensor_at(f"m{self.n}", [P, n], dt, offset=self.base + 4 * self.pos)
        self.n += 1
        self.pos += (n + 7) // 8 * 8
        self.top = max(self.top, self.pos)
        assert self.pos <= self.size, (self.pos, self.size)
        ap = t[:, :]
        if len(dims) == 2:
            ap = ap.rearrange("p (a b) -> p a b", a=dims[0])
        elif len(dims) == 3:
            ap = ap.rearrange("p (a b c) -> p a b c", a=dims[0], b=dims[1])
        return ap

    def f(self, *dims):
        return self.place(F32, *dims)

    def r(self, *dims):
        return self.place(F32R, *dims)


def build_program(nc, io):
    ctx = ExitStack()
    with ctx:
        semnames = []

        def newsem(name):
            semnames.append(name)
            return ctx.enter_context(nc.semaphore("s_" + name))

        V, A, T = Queue(nc.vector, "V"), Queue(nc.scalar, "A"), Queue(nc.tensor, "T")
        G, Y = Queue(nc.gpsimd, "G"), Queue(nc.sync, "Y")
        slots = {}

        def slot(name):
            if name not in slots:
                slots[name] = Slot(newsem("d_" + name))
            return slots[name]

        M = Memory(nc)
        ti = M.place(I32, 96)
        bank = [ctx.enter_context(nc.psum_tensor(f"b{i}", [P, 512], F32)) for i in range(8)]
        pf = [None] * 8

        H2 = nc.dram_tensor("s_h2", [S, D], F32).ap()
        GT = nc.dram_tensor("s_gt", [16, P, S], F32).ap()
        TB = nc.dram_tensor("s_tb", [P * TCOLS, 4], I32).ap()
        Y2 = nc.dram_tensor("s_y2", [2 * S, D], F32).ap()

        def phase(name):
            ends = [q.last() for q in (V, A, T, G)]
            for q in (V, A, T, G):
                q.wait(*[t for t in ends if t and t[0] != q.sem], q.last())
                q.sem, q.n = newsem(f"{q.name}_{name}"), 0
            return ends

        def fr(ap):
            return ap.bitcast(F32)

        phase("init")

        ident = M.f(P)
        zeros = M.f(256)
        mneg = M.f(4)
        eps = M.f(4)
        raw = [M.f(1024) for _ in range(RAW)]
        DUP = [M.f(512) for _ in range(2)]
        dupf, ndup = [None, None], [0]

        def doubled(src, n, rep, *toks):
            i = ndup[0] % 2
            ndup[0] += 1
            d = DUP[i][:, 0:4 * rep * n].rearrange("p (t r n) -> p t r n", t=4, r=rep)
            tk = G.do(lambda e: e.tensor_copy(d, src.unsqueeze(2).broadcast_to([P, 4, rep, n])), dupf[i], *toks)
            return i, DUP[i][:, 0:4 * rep * n].rearrange("p (t m) -> p t m", t=4), tk

        ring0 = M.pos
        whi = [M.r(1024) for _ in range(HL)]
        wlo = [M.r(1024) for _ in range(HL)]

        z0 = G.do(lambda e: e.memset(ident, 0.0))
        t_ident = G.do(lambda e: e.affine_select(out=ident, in_=ident, compare_op=ALU.not_equal, fill=1.0, base=0,
                                                 pattern=[[-1, P]], channel_multiplier=1), z0)
        t_zero = G.do(lambda e: e.memset(zeros, 0.0))
        m0 = G.do(lambda e: e.memset(mneg, 0.0))
        m0 = G.do(lambda e: e.memset(mneg[64:128, 0:1], -1.0), m0)
        m0 = G.do(lambda e: e.memset(mneg[32:64, 1:2], -1.0), m0)
        t_mneg = G.do(lambda e: e.memset(mneg[64:96, 2:3], -1.0), m0)
        t_eps = G.do(lambda e: e.memset(eps[:, 0:1], -0.5), t_mneg)

        chunks = []

        class Stream:
            def __init__(self):
                self.dmas = 0
                self.splits = 0
                self.used = 0
                self.rawfree = [None] * RAW
                self.hlfree = [None] * HL
                self.landed = {}
                self.ready = {}
                self.limit = 0
                self.plain = {}
                self.poolhi = False

            def load(self):
                i = self.dmas
                src, a, b = chunks[i]
                dst = raw[i % RAW][:, 0:a * b].rearrange("p (a b) -> p a b", a=a)
                self.landed[i] = dma(Y, slot(f"raw{i % RAW}"), dst, src, self.rawfree[i % RAW])
                self.dmas += 1

            def split(self):
                i = self.splits
                while self.dmas <= i:
                    self.load()
                n = chunks[i][1] * chunks[i][2]
                r, h, l = raw[i % RAW][:, 0:n], whi[i % HL][:, 0:n], wlo[i % HL][:, 0:n]
                if self.poolhi and i % 3 == 2:
                    th = G.do(lambda e: e.tensor_copy(h, r), self.landed[i], self.hlfree[i % HL])
                else:
                    th = A.do(lambda e: e.activation(h, r, ACT.Copy), self.landed[i], self.hlfree[i % HL])
                tl = V.do(lambda e: e.tensor_tensor(l, r, fr(h), ALU.subtract), th)
                self.ready[i] = [th, tl]
                self.rawfree[i % RAW] = [th, tl]
                self.splits += 1
                while self.dmas < min(i + 1 + RAW, len(chunks)):
                    self.load()

            def use(self):
                i = self.used
                while self.splits < min(i + HL, self.limit):
                    self.split()
                a, b = chunks[i][1:]
                view = lambda x: x[:, 0:a * b].rearrange("p (a b) -> p a b", a=a)
                return view(whi[i % HL]), view(wlo[i % HL]), self.ready[i]

            def used_by(self, tok):
                self.hlfree[self.used % HL] = tok
                self.used += 1

        W = Stream()

        def wchunks(w, kt, ks, cols, cw):
            v = w.rearrange("(k p) n -> p k n", p=P)
            for c in cols:
                for k in range(0, kt, ks):
                    chunks.append((v[:, k:k + ks, c:c + cw], ks, cw))

        wchunks(io["w_in"], 8, 2, range(0, 2240, 448), 448)
        wchunks(io["w_in"], 8, 4, range(2240, 4288, 256), 256)
        for c in range(0, 1024, 256):
            wchunks(io["w_br_a"], 4, 4, [c], 256)
            wchunks(io["w_br_b"], 4, 4, [c], 256)
        wchunks(io["w_out"], 8, 2, (0, 512), 512)
        for e in range(NEXP):
            wchunks(io["w_gate_up"][e], 8, 2, [0], 512)
            wchunks(io["w_down"][e], 2, 1, [0], 1024)
        for l in range(2):
            wchunks(io["w_in_2"][l], 8, 4, (1536, 1792), 256)
            wchunks(io["c_cos"], 4, 2, [0], 512)
            wchunks(io["c_sin"], 4, 2, [0], 512)
            wchunks(io["w_in_2"][l], 8, 2, (0, 512, 1024), 512)
            wchunks(io["w_o_2"][l], 8, 2, (0, 512), 512)
            for f in range(0, 2816, 256):
                wchunks(io["w_gu_2"][l], 8, 4, [f], 256)
                wchunks(io["w_gu_2"][l], 8, 4, [2816 + f], 256)
            wchunks(io["w_down_2"][l], 22, 2, (0, 512), 512)

        def mm3(b, pairs, start, stop, *toks):
            (xh, xl), (yh, yl) = pairs
            T.wait(*toks)
            T.go(lambda e: e.matmul(b, xh, yh, start=start, stop=False, skip_group_check=True))
            T.go(lambda e: e.matmul(b, xh, yl, start=False, stop=False, skip_group_check=True))
            return T.do(lambda e: e.matmul(b, xl, yh, start=False, stop=stop, skip_group_check=True))

        def gemm_tok(xhi, xlo, kt, ks, width, nblocks, banks, evac, xready, hook=None):
            for j in range(nblocks):
                bs = banks[j % len(banks)]
                for s in range(kt // ks):
                    hi, lo, ready = W.use()
                    for kk in range(ks):
                        k = s * ks + kk
                        for t in range(NT):
                            sl = slice(t * P, t * P + P)
                            tk = mm3(bank[bs[t]][:, 0:width], ((xhi[:, k, sl], xlo[:, k, sl]), (hi[:, kk, :], lo[:, kk, :])),
                                     k == 0, k == kt - 1, ready, xready, pf[bs[t]] if k == 0 else None)
                            if k == kt - 1:
                                pf[bs[t]] = evac(j, t, bank[bs[t]], tk)
                    W.used_by(tk)
                    if hook:
                        hook()

        def gemm_feat(xhi, xlo, kt, banks, fdone, xready, hook=None):
            for s in range(kt // 4):
                hi, lo, ready = W.use()
                for kk in range(4):
                    k = s * 4 + kk
                    for f in range(2):
                        sl = slice(f * P, f * P + P)
                        tk = mm3(bank[banks[f]][:, :], ((hi[:, kk, sl], lo[:, kk, sl]), (xhi[:, k, :], xlo[:, k, :])),
                                 k == 0, k == kt - 1, ready, xready, pf[banks[f]] if k == 0 else None)
                        fdone[f] = tk
                W.used_by(tk)
                if hook:
                    hook()

        def turn(src, t, hi, lo, bs, *toks):
            for g in range(2):
                b = bs[g]
                T.wait(pf[b], t_ident, *toks)
                for k in range(4):
                    tt = T.do(lambda e, k=k, g=g, b=b: e.transpose(bank[b][:, k * P:k * P + P], src[:, (4 * g + k) * P:(4 * g + k + 1) * P], ident))
                pv = bank[b][:, :].rearrange("p (k n) -> p k n", k=4)
                h, l = hi[:, 4 * g:4 * g + 4, t * P:t * P + P], lo[:, 4 * g:4 * g + 4, t * P:t * P + P]
                th = A.do(lambda e, h=h, pv=pv: e.activation(h, pv, ACT.Copy), tt)
                tl = V.do(lambda e, h=h, l=l, pv=pv: e.tensor_tensor(l, pv, fr(h), ALU.subtract), th)
                pf[b] = tl
            return tt, tl

        def rms_rows(x, st, scr, toks):
            for t in range(NT):
                ta = A.do(lambda e, t=t: e.activation(scr, x[:, t, :], ACT.Square, accum_out=st[:, 8 + t:9 + t]), toks, A.last())
            tv = V.do(lambda e: e.tensor_scalar(st[:, 4:8], st[:, 8:12], 1.0 / D, 1e-6, ALU.mult, ALU.add), ta)
            return G.do(lambda e: e.tensor_tensor(st[:, 0:4], st[:, 4:8], eps[:, 0:1].to_broadcast([P, 4]), ALU.pow), tv, t_eps)

        FX = M.pos
        PJ = M.f(4, 2240)
        RT = M.f(12, 128)
        invf = M.f(32)
        posf = M.f(4)
        M8 = M.f(3, 8)
        Mc = M.f(512)
        DM = M.f(3, 512)
        GNS = M.f(4, 24)
        PTC = [M.f(512) for _ in range(2)]
        BD = M.f(2, 2, 128)
        AT0 = M.pos
        TM = M.f(4, 1024)
        TM1 = M.pos
        HThi, HTlo = M.r(8, 512), M.r(8, 512)
        HT1 = M.pos
        X = M.f(4, 1024)
        XN = [PJ[:, 0, 0:1024], PJ[:, 1, 0:1024]]
        gB = PJ[:, 2, 0:1024]
        st = M.f(16)
        scr = PJ[:, 3, 0:1024]
        tx = dma(A, slot("x"), X, io["x"].rearrange("(t p) n -> p t n", p=P))
        tg = dma(A, slot("g"), gB, io["norm_mix"].partition_broadcast(P))
        W.limit = 20
        for _ in range(RAW):
            W.load()
        tr_ = rms_rows(X, st, scr, [tx])
        xf = [None, None]
        for t in range(NT):
            tn = V.do(lambda e, t=t: e.scalar_tensor_tensor(out=XN[t % 2], in0=X[:, t, :], scalar=st[:, t:t + 1], in1=gB,
                                                            op0=ALU.mult, op1=ALU.mult), tr_, tg, xf[t % 2])
            xf[t % 2], tht = turn(XN[t % 2], t, HThi, HTlo, (2 * (t % 2), 2 * (t % 2) + 1), tn)
        phase("proj")
        M.pos = HT1

        def ev_proj(j, t, b, tk):
            dst = PJ[:, t, 448 * j:448 * j + 448]
            if t % 2:
                return V.do(lambda e: e.tensor_copy(dst, b[:, 0:448]), tk)
            return A.do(lambda e: e.activation(dst, b[:, 0:448], ACT.Copy), tk)

        QA, KA, VA, QI, KI, WI, QB, KVB, GB = 0, 512, 576, 640, 896, 928, 936, 1448, 2216

        RTr = [RT[:, i, :].rearrange("p (t d) -> p t d", t=4) for i in range(12)]
        WK = [M.f(3, 512)]
        tp = dma(A, slot("pos"), ti[:, 0:4], io["c_pos"])
        ti_ = dma(A, slot("invf"), invf, io["c_invf"])
        v = V.do(lambda e: e.tensor_copy(posf, ti[:, 0:4]), tp)
        for t in range(NT):
            v = V.do(lambda e, t=t: e.tensor_scalar(RTr[0][:, t, :], invf, posf[:, t:t + 1], None, ALU.mult), v, ti_)
        MAGIC = 12582912.0
        C1 = 6.28125
        C2 = float(np.float32(2 * math.pi - C1))
        C2 = float(np.frombuffer(np.uint32(np.frombuffer(np.float32(C2).tobytes(), np.uint32)[0] & 0xFFFFF000).tobytes(), np.float32)[0])
        C3 = float(np.float32(2 * math.pi - C1 - C2))
        for which, dst, off, add in (("sin", 2, 0.0, 0.0), ("cos", 3, 0.25, math.pi / 2)):
            v = V.do(lambda e, off=off: e.tensor_scalar(RT[:, 1, :], RT[:, 0, :], 1.0 / (2 * math.pi), off, ALU.mult, ALU.add), v)
            v = V.do(lambda e: e.tensor_scalar(RT[:, 1, :], RT[:, 1, :], MAGIC, None, ALU.add), v)
            v = V.do(lambda e: e.tensor_scalar(RT[:, 1, :], RT[:, 1, :], -MAGIC, None, ALU.add), v)
            v = V.do(lambda e, dst=dst: e.scalar_tensor_tensor(out=RT[:, dst, :], in0=RT[:, 1, :], scalar=-C1, in1=RT[:, 0, :], op0=ALU.mult, op1=ALU.add), v)
            v = V.do(lambda e, dst=dst: e.scalar_tensor_tensor(out=RT[:, dst, :], in0=RT[:, 1, :], scalar=-C2, in1=RT[:, dst, :], op0=ALU.mult, op1=ALU.add), v)
            v = V.do(lambda e, dst=dst: e.scalar_tensor_tensor(out=RT[:, dst, :], in0=RT[:, 1, :], scalar=-C3, in1=RT[:, dst, :], op0=ALU.mult, op1=ALU.add), v)
            v = V.do(lambda e, dst=dst, add=add: e.tensor_scalar(RT[:, dst, :], RT[:, dst, :], add, 3.1415925, ALU.add, ALU.min), v)
            v = V.do(lambda e, dst=dst: e.tensor_scalar(RT[:, dst, :], RT[:, dst, :], -3.1415925, None, ALU.max), v)
        SN, CS, NSN, NCS = RTr[4], RTr[5], RTr[6], RTr[7]
        a = A.do(lambda e: e.activation(RT[:, 4, :], RT[:, 2, :], ACT.Sin), v)
        a = A.do(lambda e: e.activation(RT[:, 5, :], RT[:, 3, :], ACT.Sin), v)
        trt = V.do(lambda e: e.tensor_scalar(RT[:, 6:8, :], RT[:, 4:6, :], -0.125, None, ALU.mult), a)
        c0 = G.do(lambda e: e.memset(Mc, 0.0))
        t_mc = G.do(lambda e: e.affine_select(out=Mc[:, 384:512], in_=Mc[:, 384:512], compare_op=ALU.is_ge, fill=BIG, base=0,
                                              pattern=[[-1, P]], channel_multiplier=1), c0)

        gemm_tok(HThi, HTlo, 8, 2, 448, 5, [(0, 1, 2, 3), (4, 5, 6, 7)], ev_proj, None)
        tproj = [V.last(), A.last()]

        def rope(E, src, dst, nh, half, cs, sn, tm, *toks):
            n = 4 * nh * half
            tmp = [tm[:, i, 0:n].rearrange("p (t h d) -> p t h d", t=4, h=nh) for i in range(4)]
            sv = src.rearrange("p t (h two d) -> p t h two d", h=nh, two=2)
            dv = dst.rearrange("p t (h two d) -> p t h two d", h=nh, two=2)
            c = cs.unsqueeze(2).broadcast_to([P, 4, nh, half])
            s = sn.unsqueeze(2).broadcast_to([P, 4, nh, half])
            x1, x2 = sv[:, :, :, 0, :], sv[:, :, :, 1, :]
            for i, (x, y) in enumerate(((x1, c), (x2, s), (x1, s), (x2, c))):
                tk = E.do(lambda e, i=i, x=x, y=y: e.tensor_tensor(tmp[i], x, y, ALU.mult), *toks)
            E.do(lambda e: e.tensor_tensor(dv[:, :, :, 0, :], tmp[0], tmp[1], ALU.subtract), tk)
            return E.do(lambda e: e.tensor_tensor(dv[:, :, :, 1, :], tmp[2], tmp[3], ALU.add), tk)

        cs16, sn16 = CS[:, :, 0:32:2], SN[:, :, 0:32:2]
        t_ki = rope(V, PJ[:, :, KI:KI + 32], PJ[:, :, KI:KI + 32], 1, 16, cs16, sn16, TM, tproj, trt)
        t_qi = rope(V, PJ[:, :, QI:QI + 256], PJ[:, :, QI:QI + 256], 8, 16, cs16, sn16, TM, t_ki)

        kI = M.r(512)
        qI = [M.r(512) for _ in range(2)]
        hI = [M.r(512) for _ in range(2)]
        RL = [TM[:, 2, 0:512], TM[:, 3, 0:512], TM[:, 2, 512:1024], TM[:, 3, 512:1024]]
        rlf = [t_qi] * 4
        AC = WK[0]

        def stack(src, n, nrow, b, tmp, tmpfree, out, outfree, mcol, *toks):
            di, d, td = doubled(src, n, nrow // n, *toks)
            T.wait(pf[b], t_ident, td)
            for t in range(NT):
                tt = T.do(lambda e, t=t: e.transpose(bank[b][0:nrow, t * P:t * P + P], d[:, t, :], ident))
            dupf[di] = tt
            th = A.do(lambda e: e.activation(tmp[0:nrow, :], bank[b][0:nrow, :], ACT.Copy), tt, tmpfree)
            tl = V.do(lambda e: e.scalar_tensor_tensor(out=out[0:nrow, :], in0=fr(tmp[0:nrow, :]), scalar=mneg[0:nrow, mcol:mcol + 1],
                                                       in1=bank[b][0:nrow, :], op0=ALU.mult, op1=ALU.add), th, outfree, t_mneg)
            pf[b] = tl
            return tt, tl

        _, tk_ki = stack(PJ[:, :, KI:KI + 32], 32, 96, 0, hI[0], None, kI, None, 2, t_ki, tproj)
        hf, qf = [tk_ki, None], [None, None]
        n_rl = 0
        acc = {}
        for h in range(8):
            _, tq = stack(PJ[:, :, QI + 32 * h:QI + 32 * h + 32], 32, 96, 1 + h % 2, hI[(h + 1) % 2], hf[(h + 1) % 2], qI[h % 2], qf[h % 2], 1, t_qi)
            hf[(h + 1) % 2] = tq
            for qt in (1, 2, 3):
                n = (qt + 1) * P
                b = 3 + n_rl % 4
                ts = T.do(lambda e, b=b, n=n, qt=qt, h=h: e.matmul(bank[b][:, 0:n], qI[h % 2][0:96, qt * P:qt * P + P], kI[0:96, 0:n], start=True, stop=True),
                          tq, tk_ki, pf[b])
                r = n_rl % 4
                ta = A.do(lambda e, b=b, n=n, r=r: e.activation(RL[r][:, 0:n], bank[b][:, 0:n], ACT.Relu), ts, rlf[r])
                pf[b] = ta
                wcol = PJ[:, qt, WI + h:WI + h + 1]
                if h == 0:
                    tv = V.do(lambda e, n=n, r=r, qt=qt, wcol=wcol: e.tensor_scalar(AC[:, qt - 1, 0:n], RL[r][:, 0:n], wcol, None, ALU.mult), ta)
                else:
                    tv = V.do(lambda e, n=n, r=r, qt=qt, wcol=wcol: e.scalar_tensor_tensor(out=AC[:, qt - 1, 0:n], in0=RL[r][:, 0:n], scalar=wcol,
                                                                                         in1=AC[:, qt - 1, 0:n], op0=ALU.mult, op1=ALU.add), ta, acc[qt])
                acc[qt] = tv
                rlf[r] = tv
                n_rl += 1
            qf[h % 2] = ts
        for qt in (1, 2, 3):
            d = slice(qt * P, qt * P + P)
            acc[qt] = V.do(lambda e, qt=qt, d=d: e.tensor_tensor(AC[:, qt - 1, d], AC[:, qt - 1, d], Mc[:, 384:512], ALU.subtract), acc[qt], t_mc)

        WA = {qt: AC[:, qt - 1, 0:(qt + 1) * P] for qt in (1, 2, 3)}
        WB = {qt: TM[:, qt - 1, 0:(qt + 1) * P] for qt in (1, 2, 3)}

        def topk_steps():
            tk = dict(acc)
            for r in range(TOPK // 8):
                for qt in (1, 2, 3):
                    src, dst = (WA, WB) if r % 2 == 0 else (WB, WA)
                    tk[qt] = V.do(lambda e, qt=qt, src=src: e.max(M8[:, qt - 1, :], src[qt]), tk[qt])
                for qt in (1, 2, 3):
                    src, dst = (WA, WB) if r % 2 == 0 else (WB, WA)
                    tk[qt] = V.do(lambda e, qt=qt, src=src, dst=dst: e.match_replace(dst[qt], M8[:, qt - 1, :], src[qt], -3e38), tk[qt],
                                  [tk[q] for q in tk])
                yield
            for qt in (1, 2, 3):
                tk[qt] = V.do(lambda e, qt=qt: e.tensor_scalar(DM[:, qt - 1, 0:(qt + 1) * P], WA[qt], -2e38, BIG, ALU.is_gt, ALU.mult), tk[qt])
            yield

        steps = topk_steps()

        GS = [M.f(512) for _ in range(4)]
        gsf = [None] * 4
        W.limit = 20 + 16
        n = 0
        for fp in range(8):
            bs = [(0, 1), (2, 3), (4, 5), (6, 7)][fp % 4]
            fd = [None, None]
            gemm_feat(HThi, HTlo, 8, bs, fd, None, hook=lambda: next(steps, None))
            for f in range(2):
                i = n % 4
                ta = A.do(lambda e, i=i, b=bs[f]: e.activation(GS[i], bank[b][:, :], ACT.Sigmoid), fd[f], gsf[i])
                pf[bs[f]] = ta
                gsf[i] = dma(G, slot(f"gs{i}"), GT[2 * fp + f], GS[i], ta)
                n += 1
        for _ in steps:
            pass
        phase("cmp")
        for q in (A, V, G):
            q.wait(*gsf)

        M.pos = TM1
        VE = [(M.r(4, 192), M.r(4, 192)) for _ in range(3)]
        VE1 = M.pos
        w1v = {"k": TM[:, 0:2, :], "v": TM[:, 2:4, :]}
        KV2 = [M.f(512), M.f(512)]
        Zt = M.f(16, 64)
        hid = M.f(2, 64)
        kcT = M.f(2, 64)
        w2 = M.f(3, 64)
        peT = M.f(2, 16)
        wl = [dma(A, slot("w1k"), w1v["k"].rearrange("p a (b c) -> p (a b) c", c=P), io["w1_k"].rearrange("(j p) c -> p j c", p=P)),
              dma(A, slot("w1v"), w1v["v"].rearrange("p a (b c) -> p (a b) c", c=P), io["w1_v"].rearrange("(j p) c -> p j c", p=P)),
              dma(A, slot("w2"), w2[:, 0, :], io["w2_k"]), dma(A, slot("w2"), w2[:, 1, :], io["w2_k"]), dma(A, slot("w2"), w2[:, 2, :], io["w2_v"]),
              dma(A, slot("pe"), peT[:, 0, :], io["pe_k"]), dma(A, slot("pe"), peT[:, 1, :], io["pe_v"])]
        wl = [wl[0], wl[1], wl[4], wl[6]]
        tsg = A.do(lambda e: e.activation(GNS, PJ[:, :, GB:GB + 24], ACT.Sigmoid))
        for hi_, lo_ in VE:
            for x in (hi_, lo_):
                for c in (0, 128):
                    tz = V.do(lambda e, x=x, c=c: e.tensor_copy(x[:, :, c:c + 64], zeros.rearrange("p (a b) -> p a b", a=4)), t_zero)
        kvf = [None, None]
        zf = None
        tbd = None
        for s_, (nm, col) in enumerate((("k", KVB), ("v", KVB + 128))):
            for kvh in range(2):
                b = kvh
                di, d, td = doubled(PJ[:, :, col + 64 * kvh:col + 64 * kvh + 64], 64, 2)
                T.wait(pf[b], td)
                for t in range(NT):
                    tt = T.do(lambda e, t=t, d=d, b=b: e.transpose(bank[b][:, t * P:t * P + P], d[:, t, :], ident))
                dupf[di] = tt
                x = KV2[kvh]
                V.do(lambda e, x=x, b=b: e.tensor_copy(x[0:64, :], bank[b][0:64, :]), tt, kvf[kvh])
                tv = V.do(lambda e, x=x, b=b: e.tensor_copy(x[64:128, 0:511], bank[b][64:128, 1:512]), tt)
                pf[b] = tv
                z = Zt[:, :, 32 * kvh:32 * kvh + 31]
                pe_b = lambda k: peT[:, s_, k:k + 8].unsqueeze(2).broadcast_to([P, 8, 31])
                s0 = x[:, 0:496].rearrange("p (n j two) -> p j two n", j=8, two=2)[:, :, 0, :]
                s1 = x[:, 16:512].rearrange("p (n j two) -> p j two n", j=8, two=2)[:, :, 0, :]
                V.do(lambda e, z=z, s0=s0, pb=pe_b(0): e.tensor_tensor(z[:, 0:8, :], s0, pb, ALU.add), tv, wl, zf)
                tzv = V.do(lambda e, z=z, s1=s1, pb=pe_b(8): e.tensor_tensor(z[:, 8:16, :], s1, pb, ALU.add), tv)
                kvf[kvh] = tzv
            b = 2
            T.wait(pf[b], tzv, wl)
            for j in range(16):
                wj = w1v[nm].rearrange("p a (b c) -> p (a b) c", c=P)[:, j, :]
                for kvh in range(2):
                    th = T.do(lambda e, j=j, wj=wj, kvh=kvh: e.matmul(bank[3 + kvh][:, 0:31], wj, Zt[:, j, 32 * kvh:32 * kvh + 31], start=j == 0, stop=j == 15,
                                                                      skip_group_check=True), pf[3 + kvh] if j == 0 else None)
            zf = th
            for kvh in range(2):
                ta = A.do(lambda e, s_=s_, kvh=kvh: e.activation(hid[:, s_, 32 * kvh:32 * kvh + 31], bank[3 + kvh][:, 0:31], ACT.Silu), th)
                pf[3 + kvh] = ta
            if nm == "k":
                T.wait(pf[5])
                for kvh in range(2):
                    w2d = w2[:, 0:2, :].rearrange("p a b -> p (a b)")
                    tt = T.do(lambda e, kvh=kvh, w2d=w2d: e.matmul(bank[5][:, 32 * kvh:32 * kvh + 31], w2d, hid[:, 0, 32 * kvh:32 * kvh + 31], start=True, stop=True,
                                                                   skip_group_check=True), ta)
                tk0 = V.do(lambda e: e.memset(kcT, 0.0))
                for kvh in range(2):
                    for r in (0, 64):
                        tkc = V.do(lambda e, kvh=kvh: e.tensor_copy(kcT[r:r + 64, kvh, r // 2:r // 2 + 31], bank[5][r:r + 64, 32 * kvh:32 * kvh + 31]), tt, tk0)
                pf[5] = tkc
            else:
                T.wait(pf[6], ta)
                for kvh in range(2):
                    tt = T.do(lambda e, kvh=kvh: e.matmul(bank[6][0:31, 64 * kvh:64 * kvh + 64], hid[:, 1, 32 * kvh:32 * kvh + 31], w2[:, 2, :], start=True, stop=True,
                                                          skip_group_check=True))
                tb0 = V.do(lambda e: e.memset(BD, 0.0))
                for kvh in range(2):
                    for h in range(4):
                        tbd = V.do(lambda e, kvh=kvh, h=h: e.tensor_copy(BD[32 * h:32 * h + 31, kvh, h // 2, 64 * (h % 2):64 * (h % 2) + 64],
                                                                         bank[6][0:31, 64 * kvh:64 * kvh + 64]), tt, tb0)
                pf[6] = tbd
        CM = TM[:, 0, 0:128]
        c0 = G.do(lambda e: e.memset(CM, 0.0), zf)
        CMv = CM.rearrange("p (t n) -> p t n", t=4)
        t_cm = G.do(lambda e: e.affine_select(out=CMv, in_=CMv, compare_op=ALU.is_ge, fill=BIG, base=-31,
                                              pattern=[[P, 4], [-16, 32]], channel_multiplier=1), c0)
        RV = TM[:, 0, 128:132]
        c0 = G.do(lambda e: e.memset(RV, 1.0), zf)
        t_rv = G.do(lambda e: e.affine_select(out=RV, in_=RV, compare_op=ALU.is_ge, fill=0.0, base=-31,
                                              pattern=[[P, 4]], channel_multiplier=1), c0)
        QN = [TM[:, 1, 0:512], TM[:, 1, 512:1024]]
        SC = TM[:, 2, :].rearrange("p (t h n) -> p t h n", t=4, h=8)
        cst = TM[:, 3, 0:256].rearrange("p (a t h) -> p a t h", a=8, t=4)
        tsc0 = V.do(lambda e: e.memset(SC, 0.0), zf)
        tsc = None
        qnf = [None, None]
        for pr in range(4):
            b = pr % 2
            T.wait(pf[b])
            for t in range(NT):
                tt = T.do(lambda e, t=t, pr=pr, b=b: e.transpose(bank[b][:, t * P:t * P + P], PJ[:, t, QB + P * pr:QB + P * pr + P], ident))
            tq = V.do(lambda e, pr=pr, b=b: e.tensor_scalar(QN[pr % 2], bank[b][:, :], -0.125, None, ALU.mult), tt, qnf[pr % 2], zf)
            pf[b] = tq
            for t in range(NT):
                ts = T.do(lambda e: e.matmul(bank[2 + t][:, 64 * pr:64 * pr + 64], QN[pr % 2][:, t * P:t * P + P], kcT[:, pr // 2, :],
                                             start=True, stop=True, skip_group_check=True), tq, tkc, pf[2 + t] if pr == 0 else None)
            qnf[pr % 2] = ts
        for t in range(NT):
            bv = bank[2 + t][:, 0:256].rearrange("p (h n) -> p h n", h=8)[:, :, 0:31]
            cm = CMv[:, t, 0:31].unsqueeze(1).broadcast_to([P, 8, 31])
            tsc = V.do(lambda e, t=t, bv=bv, cm=cm: e.tensor_tensor(SC[:, t, :, 0:31], bv, cm, ALU.add), ts, tsc0, t_cm)
            pf[2 + t] = tsc
        SCf = SC.rearrange("p t h n -> p (t h) n")[:, :, 0:31]
        cf = lambda i: cst[:, i, :, :].rearrange("p t h -> p (t h)")
        v = V.do(lambda e: e.tensor_reduce(cf(0), SCf, AX, ALU.min), tsc)
        v = V.do(lambda e: e.tensor_tensor(SCf, SCf, cf(0).unsqueeze(2).broadcast_to([P, 32, 31]), ALU.subtract), v)
        a = A.do(lambda e: e.activation(SCf, SCf, ACT.Exp, scale=-1.0), v)
        v = V.do(lambda e: e.tensor_reduce(cf(1), SCf, AX, ALU.add), a)
        v = V.do(lambda e: e.reciprocal(cf(2), cf(1)), v)
        v = V.do(lambda e: e.tensor_tensor(cst[:, 3], cst[:, 2], GNS[:, :, 0:8], ALU.mult), v, tsg)
        v = V.do(lambda e: e.tensor_tensor(cst[:, 4], cst[:, 3], RV.unsqueeze(2).broadcast_to([P, 4, 8]), ALU.mult), v, t_rv)
        v = V.do(lambda e: e.tensor_tensor(SCf, SCf, cf(4).unsqueeze(2).broadcast_to([P, 32, 31]), ALU.mult), v)
        for kvh in range(2):
            b = kvh
            T.wait(pf[b], v)
            for t in range(NT):
                tt = T.do(lambda e, t=t, kvh=kvh, b=b: e.transpose(bank[b][:, t * P:t * P + P], SC[:, t, 4 * kvh:4 * kvh + 4, :].rearrange("p h n -> p (h n)"), ident))
            tptc = V.do(lambda e, kvh=kvh, b=b: e.tensor_copy(PTC[kvh], bank[b][:, :]), tt)
            pf[b] = tptc
        tmdone = [v, tt, qnf[0], qnf[1]]
        t_qa = rope(V, PJ[:, :, QA:QA + 512], PJ[:, :, QA:QA + 512], 8, 32, NCS, NSN, TM, tmdone)
        t_ka = rope(V, PJ[:, :, KA:KA + 64], PJ[:, :, KA:KA + 64], 1, 32, CS, SN, TM, t_qa)
        t_qb = rope(V, PJ[:, :, QB:QB + 512], PJ[:, :, QB:QB + 512], 8, 32, NCS, NSN, TM, t_ka)
        t_k2 = rope(V, PJ[:, :, KVB + 256:KVB + 384], PJ[:, :, KVB + 256:KVB + 384], 2, 32, CS, SN, TM, t_qb)
        t_k4 = rope(V, PJ[:, :, KVB + 512:KVB + 640], PJ[:, :, KVB + 512:KVB + 640], 2, 32, CS, SN, TM, t_k2)
        phase("att")

        M.pos = AT0
        PTb = [(M.r(4, 512), M.r(4, 512))]
        assert M.pos <= TM1
        M.pos = VE1
        KS = [(M.r(512), M.r(512)) for _ in range(3)]
        qH = [M.r(512) for _ in range(2)]
        qS = [M.r(512) for _ in range(3)]
        Ebuf = [M.f(512) for _ in range(4)]
        sm = M.f(3, 8)
        OAB = M.size - 8192
        assert M.pos <= OAB
        M.pos = OAB
        OA = (M.r(4, 512), M.r(4, 512))
        OB = (M.r(4, 512), M.r(4, 512))
        M.pos = ring0
        PTb.append((M.r(4, 512), M.r(4, 512)))
        branches = []
        for h in range(8):
            branches.append(dict(q=("a", h), kv=0, mask="sel", gate=None, par=h % 2, o=OA, pr=h // 2,
                                 first=h % 2 == 0, last=h % 2 == 1, cmp=None))
        for h in range(8):
            for br in range(2):
                branches.append(dict(q=("b", h), kv=1 + 2 * (h // 4) + br, mask="causal", gate=(1 + br) * 8 + h, par=h % 2, o=OB, pr=h // 2,
                                     first=False, last=(h % 2 == 1 and br == 1), cmp=(h // 4, (h % 4) // 2) if (h % 2 == 0 and br == 0) else None))
        kvsrc = [(KA, VA), (KVB + 256, KVB + 384), (KVB + 512, KVB + 640), (KVB + 320, KVB + 448), (KVB + 576, KVB + 704)]
        kvset = [0, 1, 2, 0, 1]
        kvtok, kvfree = {}, [None] * 3
        qtok, qfree, qhf = {}, [None] * 3, [None, None]
        nq = [0]
        PB = [5, 6]
        nb = [0]

        def prep_kv(i):
            s = kvset[i]
            kc, vc = kvsrc[i]
            b = 7
            di, d, td = doubled(PJ[:, :, kc:kc + 64], 64, 2)
            T.wait(pf[b], td)
            for t in range(NT):
                tt = T.do(lambda e, t=t: e.transpose(bank[b][:, t * P:t * P + P], d[:, t, :], ident))
            dupf[di] = tt
            kh, kl = KS[s]
            th = A.do(lambda e: e.activation(kh, bank[b][:, :], ACT.Copy), tt, kvfree[s])
            tl = V.do(lambda e: e.tensor_tensor(kl, bank[b][:, :], fr(kh), ALU.subtract), th)
            pf[b] = tl
            vh, vl = VE[s]
            src = PJ[:, :, vc:vc + 64]
            th = A.do(lambda e: e.activation(vh[:, :, 64:128], src, ACT.Copy), kvfree[s])
            tl = V.do(lambda e: e.tensor_tensor(vl[:, :, 64:128], src, fr(vh[:, :, 64:128]), ALU.subtract), th)
            kvtok[i] = tl

        def prep_q(key):
            i = nq[0]
            nq[0] += 1
            c = (QA if key[0] == "a" else QB) + 64 * key[1]
            _, tq = stack(PJ[:, :, c:c + 64], 64, 128, 7, qH[i % 2], qhf[i % 2], qS[i % 3], qfree[i % 3], 0)
            qhf[i % 2] = tq
            qtok[key] = (i % 3, tq)

        def steps_of(n):
            return [(i, qt) for i in range(n) for qt in range(NT)]

        SBK, TBK, OBK = [0, 1, 2], [3, 4], [5, 6]
        todo = steps_of(len(branches))
        LT, LP = 3, 5
        ef = [None] * 4
        stv = {}
        ptf = [None, None]
        pv_done = {}
        for i in range(len(todo) + LP):
            if i < len(todo):
                bi, qt = todo[i]
                B_ = branches[bi]
                if qt == 0:
                    if B_["kv"] not in kvtok:
                        prep_kv(B_["kv"])
                    if B_["q"] not in qtok:
                        prep_q(B_["q"])
                n = (qt + 1) * P
                sb_ = SBK[i % 3]
                kh, kl = KS[kvset[B_["kv"]]]
                qs, tq = qtok[B_["q"]]
                T.wait(pf[sb_], tq, kvtok[B_["kv"]])
                T.go(lambda e, sb_=sb_, n=n, qs=qs, qt=qt, kh=kh: e.matmul(bank[sb_][:, 0:n], qS[qs][:, qt * P:qt * P + P], kh[:, 0:n], start=True, stop=False))
                ts = T.do(lambda e, sb_=sb_, n=n, qs=qs, qt=qt, kl=kl: e.matmul(bank[sb_][:, 0:n], qS[qs][:, qt * P:qt * P + P], kl[:, 0:n], start=False, stop=True))
                if qt == 3:
                    qfree[qs] = ts
                m = DM[:, qt - 1, 0:n] if (B_["mask"] == "sel" and qt > 0) else Mc[:, 384 - qt * P:512]
                E = Ebuf[i % 4]
                c = i % 8
                tm_ = V.do(lambda e, E=E, n=n, sb_=sb_, m=m, c=c: e.tensor_tensor_reduce(E[:, 0:n], bank[sb_][:, 0:n], m, 1.0, 3e38, ALU.add, ALU.min, sm[:, 0, c:c + 1]),
                           ts, ef[i % 4])
                pf[sb_] = tm_
                te = A.do(lambda e, E=E, n=n, c=c: e.activation(E[:, 0:n], E[:, 0:n], ACT.Exp, bias=sm[:, 0, c:c + 1], scale=-1.0, accum_out=sm[:, 1, c:c + 1]), tm_)
                tr2 = V.do(lambda e, c=c: e.reciprocal(sm[:, 2, c:c + 1], sm[:, 1, c:c + 1]), te)
                gate = B_["gate"]
                g2 = None if gate is None else GNS[:, qt, gate:gate + 1]
                tp_ = G.do(lambda e, E=E, n=n, c=c, g2=g2: e.tensor_scalar(E[:, 0:n], E[:, 0:n], sm[:, 2, c:c + 1], g2, ALU.mult, *([ALU.mult] if g2 is not None else [])), tr2)
                stv[i] = tp_
            j = i - LT
            if 0 <= j < len(todo):
                bi, qt = todo[j]
                B_ = branches[bi]
                E = Ebuf[j % 4]
                tb_ = TBK[j % 2]
                T.wait(pf[tb_], stv[j])
                for kt in range(qt + 1):
                    tt = T.do(lambda e, tb_=tb_, kt=kt, E=E: e.transpose(bank[tb_][:, kt * P:kt * P + P], E[:, kt * P:kt * P + P], ident))
                ef[j % 4] = tt
                ph, pl = PTb[bi % 2]
                dh, dl = ph[:, 0:qt + 1, qt * P:qt * P + P], pl[:, 0:qt + 1, qt * P:qt * P + P]
                pv_ = bank[tb_][:, 0:(qt + 1) * P].rearrange("p (k n) -> p k n", n=P)
                th = A.do(lambda e, dh=dh, pv_=pv_: e.activation(dh, pv_, ACT.Copy), tt, ptf[bi % 2])
                tl = V.do(lambda e, dh=dh, dl=dl, pv_=pv_: e.tensor_tensor(dl, pv_, fr(dh), ALU.subtract), th)
                pf[tb_] = tl
                stv[("pt", j)] = tl
                if qt == 1 and bi + 2 < len(branches):
                    nx = branches[bi + 2]
                    if nx["kv"] not in kvtok and nx["kv"] < 3:
                        prep_kv(nx["kv"])
                    if nx["q"] not in qtok and nq[0] < 16:
                        prep_q(nx["q"])
            j = i - LP
            if 0 <= j < len(todo) and todo[j][1] == 3:
                bi, _ = todo[j]
                B_ = branches[bi]
                ob = OBK[B_["pr"] % 2]
                ph, pl = PTb[bi % 2]
                vh, vl = VE[kvset[B_["kv"]]]
                sl = slice(64, 192) if B_["par"] == 0 else slice(0, 128)
                T.wait(stv[("pt", j)])
                if B_["first"] or B_["cmp"]:
                    T.wait(pf[ob])
                started = False
                if B_["cmp"]:
                    kvh, pp = B_["cmp"]
                    T.go(lambda e, kvh=kvh, pp=pp, ob=ob: e.matmul(bank[ob][:, :], BD[:, kvh, pp, :], PTC[kvh], start=True, stop=False, skip_group_check=True), tptc)
                    started = True
                for kt in range(NT):
                    cs_ = slice(kt * P, 512)
                    for a_, b_ in ((vh, ph), (vl, ph), (vh, pl)):
                        st_ = B_["first"] and not started
                        started = True
                        fin = B_["last"] and kt == 3 and b_ is pl
                        tpv = T.do(lambda e, ob=ob, cs_=cs_, a_=a_, b_=b_, kt=kt, sl=sl, st_=st_, fin=fin: e.matmul(
                            bank[ob][:, cs_], a_[:, kt, sl], b_[:, kt, cs_], start=st_, stop=fin, skip_group_check=True))
                ptf[bi % 2] = tpv
                if bi + 1 == len(branches) or branches[bi + 1]["kv"] != B_["kv"]:
                    kvfree[kvset[B_["kv"]]] = tpv
                if B_["last"]:
                    oh, ol = B_["o"]
                    pr = B_["pr"]
                    th = A.do(lambda e, oh=oh, pr=pr, ob=ob: e.activation(oh[:, pr, :], bank[ob][:, :], ACT.Copy), tpv)
                    tl = V.do(lambda e, oh=oh, ol=ol, pr=pr, ob=ob: e.tensor_tensor(ol[:, pr, :], bank[ob][:, :], fr(oh[:, pr, :]), ALU.subtract), th)
                    pf[ob] = tl
        phase("merge")

        M.pos = FX
        X1 = M.f(4, 1024)
        X1E = M.pos
        MThi, MTlo = M.r(8, 512), M.r(8, 512)
        GL = [M.f(4, 512) for _ in range(2)]
        MM = [M.f(2, 512) for _ in range(2)]
        assert M.pos <= OAB
        W.limit = 36 + 8 + 8
        glf = [None, None]
        glt = {}

        def load_gates(i):
            g = GL[i % 2]
            s_ = slot(f"gl{i % 2}")
            dma(A, s_, g[:, 0:2, :], GT[2 * i:2 * i + 2].rearrange("f p n -> p f n"), glf[i % 2])
            glt[i] = dma(A, s_, g[:, 2:4, :], GT[8 + 2 * i:10 + 2 * i].rearrange("f p n -> p f n"))

        load_gates(0)
        load_gates(1)
        for i in range(4):
            fa, fb = [None, None], [None, None]
            o = 4 * (i % 2)
            gemm_feat(OA[0], OA[1], 4, (o, o + 1), fa, None)
            gemm_feat(OB[0], OB[1], 4, (o + 2, o + 3), fb, None)
            for f in range(2):
                ta = V.do(lambda e, f=f, o=o, i=i: e.tensor_tensor(MM[f][:, 0, :], bank[o + f][:, :], GL[i % 2][:, f, :], ALU.mult), fa[f], glt[i])
                pf[o + f] = ta
                tb = V.do(lambda e, f=f, o=o, i=i: e.tensor_tensor(MM[f][:, 1, :], bank[o + 2 + f][:, :], GL[i % 2][:, 2 + f, :], ALU.mult), fb[f])
                pf[o + 2 + f] = tb
                tc = V.do(lambda e, f=f: e.tensor_tensor(MM[f][:, 0, :], MM[f][:, 0, :], MM[f][:, 1, :], ALU.add), tb)
                k = 2 * i + f
                th = V.do(lambda e, f=f, k=k: e.tensor_copy(MThi[:, k, :], MM[f][:, 0, :]), tc)
                tl = V.do(lambda e, f=f, k=k: e.tensor_tensor(MTlo[:, k, :], MM[f][:, 0, :], fr(MThi[:, k, :]), ALU.subtract), th)
            glf[i % 2] = tb
            if i < 2:
                load_gates(i + 2)
        tx = [dma(A, slot("x"), X1, io["x"].rearrange("(t p) n -> p t n", p=P))]

        def ev_out(j, t, b, tk):
            return V.do(lambda e: e.tensor_tensor(X1[:, t, 512 * j:512 * j + 512], b[:, :], X1[:, t, 512 * j:512 * j + 512], ALU.add), tk, tx)

        gemm_tok(MThi, MTlo, 8, 2, 512, 2, [(0, 1, 2, 3), (4, 5, 6, 7)], ev_out, tl)
        phase("route")

        M.pos = X1E
        HThi, HTlo = M.r(8, 512), M.r(8, 512)
        XN = [M.f(1024) for _ in range(2)]
        gB = M.f(1024)
        st = M.f(16)
        scr = M.f(1024)
        wr = M.f(8, 36)
        wrh, wrl = M.r(8, 36), M.r(8, 36)
        br = M.f(36)
        tg = dma(A, slot("g"), gB, io["norm_ffn"].partition_broadcast(P))
        twr = [dma(A, slot("wr"), wr[:, :, 0:4], io["w_group"].rearrange("(k p) n -> p k n", p=P)),
               dma(A, slot("wr"), wr[:, :, 4:36], io["w_expert"].rearrange("(k p) n -> p k n", p=P))]
        tbr = [dma(A, slot("br"), br[:, 0:4], io["b_group"].partition_broadcast(P)),
               dma(A, slot("br"), br[:, 4:36], io["b_expert"].partition_broadcast(P))]
        tr_ = rms_rows(X1, st, scr, [])
        xf = [None, None]
        for t in range(NT):
            tn = V.do(lambda e, t=t: e.scalar_tensor_tensor(out=XN[t % 2], in0=X1[:, t, :], scalar=st[:, t:t + 1], in1=gB,
                                                            op0=ALU.mult, op1=ALU.mult), tr_, tg, xf[t % 2])
            t1, tht = turn(XN[t % 2], t, HThi, HTlo, (2 * (t % 2), 2 * (t % 2) + 1), tn)
            t2 = dma(G, slot(f"h2{t % 2}"), H2[t * P:t * P + P, :], XN[t % 2], tn)
            xf[t % 2] = [t1, t2]
        t_h2 = [xf[0][1], xf[1][1]]
        t1 = V.do(lambda e: e.tensor_copy(wrh, wr), twr[1])
        t1 = V.do(lambda e: e.tensor_tensor(wrl, wr, fr(wrh), ALU.subtract), t1)
        LG = M.f(4, 36)
        for t in range(NT):
            b = 4 + t % 2
            sl = slice(t * P, t * P + P)
            for k in range(8):
                tk = mm3(bank[b][:, 0:36], ((HThi[:, k, sl], HTlo[:, k, sl]), (wrh[:, k, :], wrl[:, k, :])), k == 0, k == 7, tht, t1, pf[b] if k == 0 else None)
            pf[b] = V.do(lambda e, t=t, b=b: e.tensor_tensor(LG[:, t, :], bank[b][:, 0:36], br, ALU.add), tk, tbr[1])
        tlg = pf[b]

        RS = M.f(16, 128)
        s4 = M.f(24, 4)
        IO32 = M.f(32)
        UT = M.f(128)
        ON = M.f(128)
        gi = G.do(lambda e: e.iota(ti[:, 16:48], pattern=[[1, 32]], base=0, channel_multiplier=0))
        gi = G.do(lambda e: e.tensor_copy(IO32, ti[:, 16:48]), gi)
        gt = G.do(lambda e: e.iota(ti[:, 4:8], pattern=[[P, 4]], base=0, channel_multiplier=1))
        go_ = G.do(lambda e: e.memset(ON, 1.0))
        gu = G.do(lambda e: e.affine_select(out=UT, in_=ON, compare_op=ALU.is_gt, fill=0.0, base=0, pattern=[[1, P]], channel_multiplier=-1), go_)

        def r3(i, n=32):
            return RS[:, i, 0:4 * n].rearrange("p (t n) -> p t n", t=4)

        def bc(x, n):
            return x.unsqueeze(2).broadcast_to([P, 4, n])

        def i3(n):
            return IO32[:, 0:n].unsqueeze(1).broadcast_to([P, 4, n])

        def chain(*fns, first=None):
            v = first
            for f in fns:
                v = V.do(f, v)
            return v

        def first_of(src, n, mx, idx, oh, tmp):
            return [
                lambda e: e.tensor_reduce(mx, src, AX, ALU.max),
                lambda e: e.tensor_tensor(tmp, src, bc(mx, n), ALU.is_equal),
                lambda e: e.tensor_scalar(tmp, tmp, -1000.0, 1000.0, ALU.mult, ALU.add),
                lambda e: e.tensor_tensor(tmp, tmp, i3(n), ALU.add),
                lambda e: e.tensor_reduce(idx, tmp, AX, ALU.min),
                lambda e: e.tensor_tensor(oh, i3(n), bc(idx, n), ALU.is_equal),
            ]

        gl, el = LG[:, :, 0:4], LG[:, :, 4:36]
        goh, oh1, oh2, tmp, em, e2, AS, RK, PR, CN, TMPa = (r3(0, 4), r3(1), r3(2), r3(3), r3(4), r3(5), r3(6), r3(7), r3(8), r3(9), r3(10))
        gx, gidx, gsum, gp, m1, i1, m2, i2, ex, w1_, w2_, rk1, rk2, d1, d2, big_, o1, o2 = [s4[:, i, :] for i in range(18)]
        v = chain(*first_of(gl, 4, gx, gidx, goh, r3(3, 4)), first=[tlg, gi])
        v = chain(lambda e: e.tensor_tensor(r3(3, 4), gl, bc(gx, 4), ALU.subtract), first=v)
        a = A.do(lambda e: e.activation(r3(11, 4), r3(3, 4), ACT.Exp), v)
        v = chain(lambda e: e.tensor_reduce(gsum, r3(11, 4), AX, ALU.add),
                  lambda e: e.reciprocal(gp, gsum), first=a)
        g8 = goh.unsqueeze(3).broadcast_to([P, 4, 4, 8])
        e4 = lambda x: x.rearrange("p t (g i) -> p t g i", g=4)
        v = chain(lambda e: e.tensor_tensor(e4(em), e4(el), g8, ALU.mult),
                  lambda e: e.tensor_scalar(e4(tmp), g8, BIG, -BIG, ALU.mult, ALU.add),
                  lambda e: e.tensor_tensor(em, em, tmp, ALU.add),
                  *first_of(em, 32, m1, i1, oh1, tmp),
                  lambda e: e.tensor_scalar(tmp, oh1, -3e30, None, ALU.mult),
                  lambda e: e.tensor_tensor(e2, em, tmp, ALU.add),
                  *first_of(e2, 32, m2, i2, oh2, tmp),
                  lambda e: e.tensor_tensor(w1_, m2, m1, ALU.subtract), first=v)
        a = A.do(lambda e: e.activation(ex, w1_, ACT.Exp), v)
        v = chain(lambda e: e.tensor_scalar(w2_, ex, 1.0, None, ALU.add),
                  lambda e: e.reciprocal(w1_, w2_),
                  lambda e: e.tensor_tensor(w1_, w1_, gp, ALU.mult),
                  lambda e: e.tensor_tensor(w2_, w1_, ex, ALU.mult),
                  lambda e: e.tensor_tensor(AS, oh1, oh2, ALU.add), first=a)
        T.wait(pf[6], pf[7], v, gu, go_)
        for t in range(NT):
            for u in range(t + 1):
                tk = T.do(lambda e, t=t, u=u: e.matmul(bank[6][:, 32 * t:32 * t + 32], UT if u == t else ON, AS[:, u, :], start=u == 0, stop=u == t, skip_group_check=True))
        for u in range(NT):
            tk2 = T.do(lambda e, u=u: e.matmul(bank[7][:, 0:32], ON, AS[:, u, :], start=u == 0, stop=u == 3))
        OV = M.f(8, 32)
        cnt, ovn, s_a, s_b, cex = [OV[:, i, :] for i in range(5)]
        v = chain(lambda e: e.tensor_copy(RK, bank[6][:, 0:128].rearrange("p (t n) -> p t n", t=4)),
                  lambda e: e.tensor_copy(cnt, bank[7][:, 0:32]),
                  lambda e: e.tensor_scalar(ovn, cnt, 128.5, None, ALU.is_gt),
                  lambda e: e.tensor_scalar(s_a, cnt, 256.5, None, ALU.is_gt),
                  lambda e: e.tensor_tensor(ovn, ovn, s_a, ALU.add),
                  lambda e: e.tensor_scalar(s_a, cnt, 384.5, None, ALU.is_gt),
                  lambda e: e.tensor_tensor(ovn, ovn, s_a, ALU.add),
                  lambda e: e.tensor_copy(s_a, ovn), first=[tk2])
        cur, oth = s_a, s_b
        for sh in (1, 2, 4, 8, 16):
            v = chain(lambda e, c=cur, o=oth, sh=sh: e.tensor_copy(o[:, 0:sh], c[:, 0:sh]),
                      lambda e, c=cur, o=oth, sh=sh: e.tensor_tensor(o[:, sh:32], c[:, sh:32], c[:, 0:32 - sh], ALU.add), first=v)
            cur, oth = oth, cur
        incl = cur
        v = chain(lambda e: e.tensor_tensor(cex, incl, ovn, ALU.subtract), first=v)
        p40 = M.f(4, 32)
        full = r3(12)
        j_ = r3(13)
        fl = r3(14)
        v = chain(lambda e: e.tensor_scalar(fl, RK, 127.5, None, ALU.is_gt),
                  lambda e: e.tensor_scalar(j_, RK, 255.5, None, ALU.is_gt),
                  lambda e: e.tensor_tensor(fl, fl, j_, ALU.add),
                  lambda e: e.tensor_scalar(j_, RK, 383.5, None, ALU.is_gt),
                  lambda e: e.tensor_tensor(fl, fl, j_, ALU.add),
                  lambda e: e.tensor_scalar(j_, fl, -128.0, None, ALU.mult),
                  lambda e: e.tensor_tensor(full, RK, j_, ALU.add),
                  lambda e: e.tensor_scalar(full, full, float(TCOLS), None, ALU.mult),
                  lambda e: e.tensor_tensor(j_, fl, cex.unsqueeze(1).broadcast_to([P, 4, 32]), ALU.add),
                  lambda e: e.tensor_scalar(j_, j_, 31.0, None, ALU.add),
                  lambda e: e.tensor_scalar(tmp, fl, 0.5, None, ALU.is_gt),
                  lambda e: e.tensor_tensor(j_, j_, i3(32), ALU.subtract),
                  lambda e: e.tensor_tensor(j_, j_, tmp, ALU.mult),
                  lambda e: e.tensor_tensor(j_, j_, i3(32), ALU.add),
                  lambda e: e.tensor_tensor(full, full, j_, ALU.add),
                  lambda e: e.tensor_tensor(tmp, full, oh1, ALU.mult),
                  lambda e: e.tensor_reduce(d1, tmp, AX, ALU.add),
                  lambda e: e.tensor_tensor(tmp, full, oh2, ALU.mult),
                  lambda e: e.tensor_reduce(d2, tmp, AX, ALU.add),
                  lambda e: e.tensor_copy(ti[:, 8:12], d1),
                  lambda e: e.tensor_copy(ti[:, 12:16], d2), first=v)
        PL = ti[:, 64:96].rearrange("p (k t w) -> p k t w", k=2, t=4)
        tokf = s4[:, 18, :]
        v = V.do(lambda e: e.tensor_copy(tokf, ti[:, 4:8]), v, gt)
        v = chain(lambda e: e.tensor_copy(PL[:, 0, :, 0], tokf), lambda e: e.tensor_copy(PL[:, 1, :, 0], tokf),
                  lambda e: e.tensor_copy(PL[:, 0, :, 1], tokf),
                  lambda e: e.tensor_scalar(PL[:, 1, :, 1], tokf, float(S), None, ALU.add),
                  lambda e: e.tensor_copy(PL[:, 0, :, 2].bitcast(F32), w1_),
                  lambda e: e.tensor_copy(PL[:, 1, :, 2].bitcast(F32), w2_),
                  lambda e: e.memset(PL[:, :, :, 3], 0), first=v)
        TBS = M.f(TCOLS * 4)
        TBi = TBS.bitcast(I32)
        g0 = G.do(lambda e: e.memset(TBi, FAR))
        t_fill = dma(G, slot("tbf"), TB.rearrange("(p c) w -> p (c w)", p=P), TBi, g0)
        G.wait(t_fill, v)
        sc_sl = slot("tbs")
        for k in range(2):
            for t in range(NT):
                sc_sl.n += 16
                idx = ti[:, 8 + 4 * k + t:9 + 4 * k + t].bitcast(U32)
                G.eng.indirect_dma_start(
                    TB, bass.IndirectOffsetOnAxis(idx, 0), PL[:, k, t, :], None).then_inc(sc_sl.key, 16)
        TAB = M.f(TCOLS, 4)
        t_tab = dma(G, slot("tab"), TAB.bitcast(I32), TB.rearrange("(p c) w -> p c w", p=P), (sc_sl.key, sc_sl.n))
        OE = M.f(8)
        OI = M.f(8, 10)
        v = V.last()
        for j in range(NOVER):
            v = V.do(lambda e, j=j: e.tensor_scalar(s_b if incl is s_a else s_a, incl, j + 0.5, None, ALU.is_lt), v)
            v = V.do(lambda e, j=j: e.tensor_reduce(OE[:, j:j + 1], s_b if incl is s_a else s_a, AX, ALU.add), v)
        v = V.do(lambda e: e.tensor_scalar(OE[:, 0:NOVER], OE[:, 0:NOVER], 31.0, None, ALU.min), v)
        gi2 = G.do(lambda e: e.iota(ti[:, 48:58], pattern=[[P, 10]], base=0, channel_multiplier=1))
        IOF = M.f(10)
        v = V.do(lambda e: e.tensor_copy(IOF, ti[:, 48:58]), v, gi2)
        v = V.do(lambda e: e.tensor_scalar(IOF[:, 8:10], IOF[:, 8:10], -1024.0, None, ALU.add), v)
        toi = []
        for j in range(NOVER):
            v = V.do(lambda e, j=j: e.scalar_tensor_tensor(out=OI[:, j, 0:8], in0=OE[:, j:j + 1].to_broadcast([P, 8]), scalar=1024.0, in1=IOF[:, 0:8], op0=ALU.mult, op1=ALU.add), v)
            v = V.do(lambda e, j=j: e.scalar_tensor_tensor(out=OI[:, j, 8:10], in0=OE[:, j:j + 1].to_broadcast([P, 2]), scalar=256.0, in1=IOF[:, 8:10], op0=ALU.mult, op1=ALU.add), v)
        OIi = M.f(8, 10).bitcast(I32)
        t_oi = V.do(lambda e: e.tensor_copy(OIi[:, 0:NOVER, :], OI[:, 0:NOVER, :]), v)

        XG = [M.f(1024) for _ in range(2)]
        XT = [(M.r(8, 128), M.r(8, 128)) for _ in range(2)]
        SG = [M.f(256) for _ in range(2)]
        AT = [(M.r(2, 128), M.r(2, 128)) for _ in range(2)]
        YS = [M.f(1024) for _ in range(2)]
        xz = [G.do(lambda e, x=x: e.memset(x, 0.0)) for x in XG]
        xgf, ysf = list(xz), [None, None]
        xtf, atf, sgf = [None, None], [None, None], [None, None]
        W.limit = W.used + 6 * NEXP
        gtok = {}

        def gather(c):
            i = c % 2
            s_ = slot(f"xg{i}")
            G.wait(xgf[i], t_tab, t_h2)
            s_.n += 16
            G.eng.indirect_dma_start(XG[i], None, H2, bass.IndirectOffsetOnAxis(TAB[:, c, 0:1].bitcast(U32), 0),
                                                                 bounds_check=S - 1, oob_is_err=False).then_inc(s_.key, 16)
            gtok[c] = (s_.key, s_.n)

        tyall = []

        def tokens_in(c):
            i = c % 2
            hi, lo = XT[i]
            for g in range(2):
                b = 4 + g
                T.wait(pf[b], gtok[c])
                for k in range(4):
                    tt = T.do(lambda e, k=k, g=g, b=b: e.transpose(bank[b][:, k * P:k * P + P], XG[i][:, (4 * g + k) * P:(4 * g + k + 1) * P], ident))
                pv = bank[b][:, :].rearrange("p (k n) -> p k n", k=4)
                h, l = hi[:, 4 * g:4 * g + 4, :], lo[:, 4 * g:4 * g + 4, :]
                th = A.do(lambda e, h=h, pv=pv: e.activation(h, pv, ACT.Copy), tt, xtf[i])
                tl = V.do(lambda e, h=h, l=l, pv=pv: e.tensor_tensor(l, pv, fr(h), ALU.subtract), th)
                pf[b] = tl
            xgf[i] = tt
            return tl

        def expert(c, getw, xready):
            i = c % 2
            hi, lo = XT[i]
            b = i
            for s_ in range(4):
                wh, wl_, ready, done = getw()
                for kk in range(2):
                    k = 2 * s_ + kk
                    tk = mm3(bank[b][:, :], ((hi[:, k, :], lo[:, k, :]), (wh[:, kk, :], wl_[:, kk, :])), k == 0, k == 7, ready, xready, pf[b] if k == 0 else None)
                done(tk)
            xtf[i] = tk
            ta = A.do(lambda e: e.activation(SG[i], bank[b][:, 0:256], ACT.Silu), tk, sgf[i])
            tv = V.do(lambda e: e.tensor_tensor(SG[i], SG[i], bank[b][:, 256:512], ALU.mult), ta)
            pf[b] = tv
            yield
            b = 6
            T.wait(pf[b], tv)
            for f in range(2):
                tt = T.do(lambda e, f=f, b=b: e.transpose(bank[b][:, f * P:f * P + P], SG[i][:, f * P:f * P + P], ident))
            sgf[i] = tt
            pv = bank[b][:, 0:256].rearrange("p (k n) -> p k n", k=2)
            ah, al = AT[i]
            th = A.do(lambda e: e.activation(ah, pv, ACT.Copy), tt, atf[i])
            tl = V.do(lambda e: e.tensor_tensor(al, pv, fr(ah), ALU.subtract), th)
            pf[b] = tl
            yield
            for f in range(2):
                wh, wl_, ready, done = getw()
                for n in range(2):
                    tk = mm3(bank[2 + n][:, :], ((ah[:, f, :], al[:, f, :]), (wh[:, 0, 512 * n:512 * n + 512], wl_[:, 0, 512 * n:512 * n + 512])),
                             f == 0, f == 1, ready, tl, pf[2 + n] if f == 0 else None)
                done(tk)
            atf[i] = tk
            wt = TAB[:, c, 2:3]
            ty0 = A.do(lambda e: e.activation(YS[i][:, 0:512], bank[2][:, :], ACT.Copy, scale=wt), tk, ysf[i])
            pf[2] = ty0
            ty1 = A.do(lambda e: e.activation(YS[i][:, 512:1024], bank[3][:, :], ACT.Copy, scale=wt))
            pf[3] = ty1
            s_ = slot(f"ys{i}")
            G.wait(ty1)
            s_.n += 16
            G.eng.indirect_dma_start(Y2, bass.IndirectOffsetOnAxis(TAB[:, c, 1:2].bitcast(U32), 0), YS[i], None,
                                                                 bounds_check=2 * S - 1, oob_is_err=False).then_inc(s_.key, 16)
            ysf[i] = (s_.key, s_.n)
            yield

        def ring():
            hi, lo, ready = W.use()
            return hi, lo, ready, W.used_by

        gather(0)
        gather(1)
        xr = tokens_in(0)
        for c in range(NEXP):
            ex_ = expert(c, ring, xr)
            next(ex_)
            if c + 2 < NEXP:
                pass
            xr2 = None
            if c + 1 < NEXP:
                xr2 = tokens_in(c + 1)
            if c + 2 < NEXP + NOVER:
                gather(c + 2)
            next(ex_)
            next(ex_)
            xr = xr2

        wg_rows = io["w_gate_up"].rearrange("e k n -> (e k) n")
        wd_rows = io["w_down"].rearrange("e k n -> (e k) n")
        OW = [M.f(2, 512) for _ in range(2)]
        OWR = [(M.r(2, 512), M.r(2, 512)) for _ in range(2)]
        owf = [[None, None], [None, None]]
        now = [0]

        def over_w(j):
            s = [0]

            def get():
                i = now[0] % 2
                now[0] += 1
                sl_ = slot(f"ow{i}")
                G.wait(owf[i][0], t_oi)
                if s[0] < 4:
                    for kk in range(2):
                        k = 2 * s[0] + kk
                        sl_.n += 16
                        G.eng.indirect_dma_start(
                            OW[i][:, kk, :], None, wg_rows, bass.IndirectOffsetOnAxis(OIi[:, j, k:k + 1].bitcast(U32), 0)).then_inc(sl_.key, 16)
                    a_, b_ = 2, 512
                else:
                    f = s[0] - 4
                    sl_.n += 16
                    G.eng.indirect_dma_start(
                        OW[i].rearrange("p a b -> p (a b)"), None, wd_rows, bass.IndirectOffsetOnAxis(OIi[:, j, 8 + f:9 + f].bitcast(U32), 0)).then_inc(sl_.key, 16)
                    a_, b_ = 1, 1024
                s[0] += 1
                hi, lo = OWR[i]
                th = A.do(lambda e: e.activation(hi, OW[i], ACT.Copy), (sl_.key, sl_.n), owf[i][1])
                tl = V.do(lambda e: e.tensor_tensor(lo, OW[i], fr(hi), ALU.subtract), th)
                owf[i][0] = tl
                vw = lambda x: x.rearrange("p a b -> p (a b)").rearrange("p (a b) -> p a b", a=a_)

                def done(tk):
                    owf[i][1] = tk
                return vw(hi), vw(lo), [th, tl], done
            return get

        for j in range(NOVER):
            c = NEXP + j
            xr = tokens_in(c)
            if j + 2 < NOVER and c + 2 not in gtok:
                gather(c + 2)
            for _ in expert(c, over_w(j), xr):
                pass
        phase("final")
        M.pos = X1E
        st = M.f(16)

        YA = [M.f(1024) for _ in range(2)]
        for q in (V, A, G):
            q.wait(*ysf)
        yf = [None, None]
        A.wait(*ysf)
        n = 0
        v = None
        for k in range(2):
            for t in range(NT):
                i = n % 2
                ty = dma(A, slot(f"ya{i}"), YA[i], Y2[k * S + t * P:k * S + t * P + P, :], yf[i])
                yf[i] = V.do(lambda e, i=i, t=t: e.tensor_tensor(X1[:, t, :], X1[:, t, :], YA[i], ALU.add), ty, v if k else None)
                n += 1
        tsum = V.last()
        gB = M.f(1024)
        bB = M.f(1024)
        scr = M.f(1024)
        tg = dma(A, slot("g"), gB, io["norm_final"].partition_broadcast(P))
        tr_ = rms_rows(X1, st, scr, [tsum])
        for t in range(NT):
            tn = V.do(lambda e, t=t: e.scalar_tensor_tensor(out=X1[:, t, :], in0=X1[:, t, :], scalar=st[:, t:t + 1], in1=gB, op0=ALU.mult, op1=ALU.mult), tr_, tg)
        tg2 = dma(A, slot("lg"), gB, io["ln_in_g_2"].partition_broadcast(P), tn)
        tb2 = dma(A, slot("lb"), bB, io["ln_in_b_2"].partition_broadcast(P))

        def layernorm(x, gb, bb, ln, toks, gtoks):
            bn = ln[:, 0:48].rearrange("p (t s w) -> p t s w", t=4, s=2)
            mv = ln[:, 48:56].rearrange("p (t w) -> p t w", t=4)
            rs = ln[:, 56:60]
            outs = []
            for t in range(NT):
                for s_ in range(2):
                    v = V.do(lambda e, t=t, s_=s_: e.bn_stats(bn[:, t, s_, :], x[:, t, 512 * s_:512 * s_ + 512]), toks[t])
            for t in range(NT):
                v2 = V.do(lambda e, t=t: e.bn_aggr(mv[:, t, :], bn[:, t, :, :].rearrange("p s w -> p (s w)")), v)
            v = V.do(lambda e: e.tensor_scalar(ln[:, 60:64], mv[:, :, 1], 1e-5, None, ALU.add), v2)
            g = G.do(lambda e: e.tensor_tensor(rs, ln[:, 60:64], eps[:, 0:1].to_broadcast([P, 4]), ALU.pow), v)
            for t in range(NT):
                v = V.do(lambda e, t=t: e.tensor_scalar(x[:, t, :], x[:, t, :], mv[:, t, 0:1], rs[:, t:t + 1], ALU.subtract, ALU.mult), g)
                v = V.do(lambda e, t=t: e.tensor_tensor(x[:, t, :], x[:, t, :], gb, ALU.mult), v, gtoks)
                v = V.do(lambda e, t=t: e.tensor_tensor(x[:, t, :], x[:, t, :], bb, ALU.add), v)
                outs.append(v)
            return outs

        lnb = M.f(64)
        touts = layernorm(X1, gB, bB, lnb, [tn] * 4, [tg2, tb2])
        phase("lay")

        M.pos = X1E
        Hs = X1
        lnb = M.f(64)
        small = M.f(64)
        bdo = M.f(4, 8)
        sel8 = M.f(4, 128)
        TOE = M.f(896)
        lamb = M.f(8)
        LPm = M.f(4, 32)
        subg = M.f(4)
        bfc = M.f(8)
        LAY = M.pos
        g0 = G.do(lambda e: e.memset(bdo, 0.0))
        g0b = G.do(lambda e: e.memset(sel8, 0.0))
        for pr in range(4):
            for hh in range(2):
                tbo = G.do(lambda e, pr=pr, hh=hh: e.memset(bdo[64 * hh:64 * hh + 64, pr, 2 * pr + hh:2 * pr + hh + 1], 1.0 / 64), G.last())
        tse = G.do(lambda e: e.memset(sel8[0:8, :, :], 1.0), tbo)
        sv = sel8[0:8, :, :].rearrange("p r (h d) -> p r h d", h=2)
        tse = G.do(lambda e: e.affine_select(out=sv, in_=sv, compare_op=ALU.is_equal, fill=0.0, base=0,
                                             pattern=[[-2, 4], [-1, 2], [0, 64]], channel_multiplier=1), tse)
        tio = G.do(lambda e: e.iota(TOE.bitcast(I32), pattern=[[-1, 896]], base=384, channel_multiplier=1))
        v = V.do(lambda e: e.tensor_copy(TOE, TOE.bitcast(I32)), tio)
        ttoe = V.do(lambda e: e.scalar_tensor_tensor(out=TOE, in0=TOE, scalar=-1.0, in1=TOE, op0=ALU.mult, op1=ALU.max), v)
        SC32 = 32.0 ** -0.5

        for l in range(2):
            lam_init = 0.8 - 0.6 * math.exp(-0.3 * l)
            M.pos = LAY
            HThi, HTlo = M.r(8, 512), M.r(8, 512)
            CT0 = M.pos
            CThi, CTlo = M.r(8, 512), M.r(8, 512)
            CT1 = M.pos
            tlp = dma(A, slot("lp"), LPm, io["lam_params_2"][l].partition_broadcast(P))
            tsg_ = dma(A, slot("sg"), subg[:, 0:1], io["subln_g_2"][l])
            tbf = dma(A, slot("bf"), bfc[:, 0:4], io["b_f_2"][l])
            v = V.do(lambda e: e.tensor_tensor(LPm[:, 0:4:2, :], LPm[:, 0:4:2, :], LPm[:, 1:4:2, :], ALU.mult), tlp)
            v = V.do(lambda e: e.tensor_reduce(lamb[:, 0:2], LPm[:, 0:4:2, :], AX, ALU.add), v)
            a = A.do(lambda e: e.activation(lamb[:, 2:4], lamb[:, 0:2], ACT.Exp), v)
            v = V.do(lambda e: e.tensor_tensor(lamb[:, 4:5], lamb[:, 3:4], lamb[:, 2:3], ALU.subtract), a)
            tlam = V.do(lambda e, li=lam_init: e.tensor_scalar(lamb[:, 5:6], lamb[:, 4:5], -li, None, ALU.add), v)
            tsub = V.do(lambda e, li=lam_init: e.tensor_scalar(subg[:, 1:2], subg[:, 0:1], 1.0 - li, None, ALU.mult), tsg_)
            for t in range(NT):
                _, tht = turn(Hs[:, t, :], t, HThi, HTlo, (2 * (t % 2), 2 * (t % 2) + 1))

            uT = (M.r(4, 512), M.r(4, 512))
            AB = (M.r(4, 4, 256), M.r(4, 4, 256))
            C1s = (M.r(256), M.r(256))
            wfR = (M.r(4, 128), M.r(4, 128))
            c1 = M.f(256)
            wf = M.f(4, 128)
            tc1 = dma(A, slot("c1"), c1, io["c_c128"])
            twf = dma(A, slot("wf"), wf, io["w_f_2"][l].rearrange("g c d -> c g d"))
            v = V.do(lambda e: e.tensor_copy(C1s[0], c1), tc1)
            tc1 = V.do(lambda e: e.tensor_tensor(C1s[1], c1, fr(C1s[0]), ALU.subtract), v)
            v = V.do(lambda e: e.tensor_copy(wfR[0], wf), twf)
            twf = V.do(lambda e: e.tensor_tensor(wfR[1], wf, fr(wfR[0]), ALU.subtract), v)
            W.limit = W.used + 4 + 4 + 12
            tu = {}

            def halves(b, hi, lo, tk, *toks):
                th = A.do(lambda e: e.activation(hi, b, ACT.Copy), tk, *toks)
                return V.do(lambda e: e.tensor_tensor(lo, b, fr(hi), ALU.subtract), th)

            for fp in range(2):
                fd = [None, None]
                bs = (4, 5) if fp == 0 else (6, 7)
                gemm_feat(HThi, HTlo, 8, bs, fd, tht)
                for f in range(2):
                    g = 2 * fp + f
                    pf[bs[f]] = tu[g] = halves(bank[bs[f]][:, :], uT[0][:, g, :], uT[1][:, g, :], fd[f])
            n = 0
            for g in range(4):
                for t2 in range(2):
                    b = n % 4
                    n += 1
                    for tt_ in range(2):
                        t = 2 * t2 + tt_
                        sl = slice(t * P, t * P + P)
                        tk = mm3(bank[b][:, 256 * tt_:256 * tt_ + 256], ((uT[0][:, g, sl], uT[1][:, g, sl]), C1s), True, True, tu[g], tc1, pf[b] if tt_ == 0 else None)
                    bv = bank[b][:, :].rearrange("p (t c) -> p t c", t=2)
                    pf[b] = tab = halves(bv, AB[0][:, 2 * t2:2 * t2 + 2, g, :], AB[1][:, 2 * t2:2 * t2 + 2, g, :], tk)
            for cs_ in range(2):
                for s_ in range(2):
                    hi, lo, ready = W.use()
                    for kk in range(2):
                        t = 2 * s_ + kk
                        for g in range(4):
                            c = slice(128 * cs_, 128 * cs_ + 128)
                            tk = mm3(bank[4 + g][:, :], ((AB[0][:, t, g, c], AB[1][:, t, g, c]), (hi[:, kk, :], lo[:, kk, :])),
                                     cs_ == 0 and t == 0, cs_ == 1 and t == 3, ready, tab, pf[4 + g] if (cs_ == 0 and t == 0) else None)
                    W.used_by(tk)
            for g in range(4):
                pf[4 + g] = tu[g] = halves(bank[4 + g][:, :], uT[0][:, g, :], uT[1][:, g, :], tk)
            for g in range(4):
                tk = mm3(bank[g][:, :], ((wfR[0][:, g, :], wfR[1][:, g, :]), (uT[0][:, g, :], uT[1][:, g, :])), True, True, tu[g], twf, pf[g])
                bias = bfc[:, g:g + 1]
                th = V.do(lambda e, g=g, bias=bias: e.tensor_scalar(CThi[:, 4 + g, :], bank[g][:, :], bias, None, ALU.add), tk, tbf)
                pf[g] = V.do(lambda e, g=g, bias=bias: e.scalar_tensor_tensor(out=CTlo[:, 4 + g, :], in0=bank[g][:, :], scalar=bias, in1=fr(CThi[:, 4 + g, :]),
                                                                             op0=ALU.add, op1=ALU.subtract), th)
            phase(f"qkv{l}")
            M.pos = CT1
            QK = M.f(4, 1024)
            VV = (M.r(4, 4, 192), M.r(4, 4, 192))
            for x in VV:
                for t in range(NT):
                    tz = V.do(lambda e, x=x, t=t: e.tensor_copy(x[:, t, :, 64:128], zeros.rearrange("p (a b) -> p a b", a=4)), t_zero)

            def ev_qkv(j, t, b, tk):
                if j < 2:
                    sc_ = -SC32 if j == 0 else 1.0
                    return A.do(lambda e: e.activation(QK[:, t, 512 * j:512 * j + 512], b[:, :], ACT.Copy, scale=sc_), tk)
                bv = b[:, :].rearrange("p (r h d) -> p r h d", r=4, h=2)
                vv = [x[:, t, :, :].rearrange("p r (c d) -> p r c d", c=3)[:, :, 0:3:2, :] for x in VV]
                return halves(bv, vv[0], vv[1], tk)

            gemm_tok(HThi, HTlo, 8, 2, 512, 3, [(0, 1, 2, 3), (4, 5, 6, 7)], ev_qkv, None)
            phase(f"at{l}")

            PT2 = [(HThi[:, 0:4, :], HTlo[:, 0:4, :]), (HThi[:, 4:8, :], HTlo[:, 4:8, :])]
            SH = [M.r(512) for _ in range(2)]
            QI2 = [CThi[:, i, :] for i in range(4)]
            KI2 = [CTlo[:, i, :] for i in range(4)]
            Eb = [M.f(2, 512) for _ in range(3)]
            AB2 = [M.f(896) for _ in range(2)]
            OO = M.f(4, 512)
            sm2 = M.f(4, 16)
            sq, rsd = Eb[2][:, 0, :], Eb[2][:, 1, :]
            gB, bB = Eb[0].rearrange("p a b -> p (a b)"), Eb[1].rearrange("p a b -> p (a b)")
            shf, qif, kif = [None] * 2, [None] * 4, [None] * 4
            abf = [None, None]
            nsh = [0]
            prept = {}

            def prep(h):
                for c in range(2):
                    i = (2 * h + c) % 4
                    col = 64 * h + 32 * c
                    for off, dst, fl, mc in ((0, QI2, qif, 1), (512, KI2, kif, 2)):
                        k = nsh[0] % 2
                        nsh[0] += 1
                        _, tq = stack(QK[:, :, off + col:off + col + 32], 32, 96, 7, SH[k], shf[k], dst[i], fl[i], mc)
                        shf[k] = tq
                slope = 2.0 ** (-8.0 * (h + 1) / 8)
                tb_ = G.do(lambda e: e.tensor_scalar(AB2[h % 2], TOE, slope, None, ALU.mult), ttoe, abf[h % 2])
                prept[h] = [tq, tb_]

            todo = [(h, qt) for h in range(8) for qt in range(NT)]
            LT, LP = 2, 3
            ef = [None] * 3
            stv, ptf = {}, [None, None]
            SBK, TBK, OBK = [0, 1, 2, 3], [4, 5], 6
            prep(0)
            for i in range(len(todo) + LP):
                if i < len(todo):
                    h, qt = todo[i]
                    if qt == 1 and h + 1 < 8:
                        prep(h + 1)
                    E = Eb[i % 3]
                    tes = []
                    for c in range(2):
                        sb_ = SBK[(2 * i + c) % 4]
                        qi_ = (2 * h + c) % 4
                        ts = T.do(lambda e, sb_=sb_, qi_=qi_, qt=qt: e.matmul(bank[sb_][:, :], QI2[qi_][0:96, qt * P:qt * P + P], KI2[qi_][0:96, :], start=True, stop=True),
                                  pf[sb_], prept[h])
                        if qt == 3:
                            qif[qi_] = kif[qi_] = ts
                        m = AB2[h % 2][:, 384 - qt * P:896 - qt * P]
                        k = (2 * i + c) % 16
                        tm_ = V.do(lambda e, E=E, c=c, sb_=sb_, m=m, k=k: e.tensor_tensor_reduce(E[:, c, :], bank[sb_][:, :], m, 1.0, 3e38, ALU.add, ALU.min, sm2[:, 0, k:k + 1]),
                                   ts, ef[i % 3])
                        pf[sb_] = tm_
                        te = A.do(lambda e, E=E, c=c, k=k: e.activation(E[:, c, :], E[:, c, :], ACT.Exp, bias=sm2[:, 0, k:k + 1], scale=-1.0, accum_out=sm2[:, 1, k:k + 1]), tm_)
                    if qt == 3:
                        abf[h % 2] = tm_
                    k = (2 * i) % 16
                    tr2 = V.do(lambda e, k=k: e.reciprocal(sm2[:, 2, k:k + 2], sm2[:, 1, k:k + 2]), te)
                    tg_ = G.do(lambda e, E=E, k=k: e.tensor_scalar(E[:, 1, :], E[:, 1, :], sm2[:, 2, k + 1:k + 2], lamb[:, 5:6], ALU.mult, ALU.mult), tr2, tlam)
                    stv[i] = V.do(lambda e, E=E, k=k: e.scalar_tensor_tensor(out=E[:, 0, :], in0=E[:, 0, :], scalar=sm2[:, 2, k:k + 1], in1=E[:, 1, :], op0=ALU.mult, op1=ALU.add), tg_)
                j = i - LT
                if 0 <= j < len(todo):
                    h, qt = todo[j]
                    E = Eb[j % 3]
                    tb_ = TBK[j % 2]
                    T.wait(pf[tb_], stv[j])
                    for kt in range(4):
                        tt = T.do(lambda e, tb_=tb_, kt=kt, E=E: e.transpose(bank[tb_][:, kt * P:kt * P + P], E[:, 0, kt * P:kt * P + P], ident))
                    ef[j % 3] = tt
                    ph, pl = PT2[h % 2]
                    dh, dl = ph[:, :, qt * P:qt * P + P], pl[:, :, qt * P:qt * P + P]
                    pv_ = bank[tb_][:, :].rearrange("p (k n) -> p k n", n=P)
                    th = A.do(lambda e, dh=dh, pv_=pv_: e.activation(dh, pv_, ACT.Copy), tt, ptf[h % 2])
                    pf[tb_] = stv[("pt", j)] = V.do(lambda e, dh=dh, dl=dl, pv_=pv_: e.tensor_tensor(dl, pv_, fr(dh), ALU.subtract), th)
                j = i - LP
                if 0 <= j < len(todo) and todo[j][1] == 3:
                    h = todo[j][0]
                    pr, hh = h // 2, h % 2
                    ph, pl = PT2[h % 2]
                    sl = slice(64 * hh, 64 * hh + 128)
                    T.wait(stv[("pt", j)])
                    if hh == 0:
                        T.wait(pf[OBK])
                    for kt in range(NT):
                        for x_, (a_, b_) in enumerate(((VV[0], ph), (VV[1], ph), (VV[0], pl))):
                            tpv = T.do(lambda e, kt=kt, a_=a_, b_=b_, pr=pr, sl=sl, hh=hh, x_=x_: e.matmul(
                                bank[OBK][:, :], a_[:, kt, pr, sl], b_[:, kt, :], start=(hh == 0 and kt == 0 and x_ == 0), stop=(hh == 1 and kt == 3 and x_ == 2),
                                skip_group_check=True))
                    ptf[h % 2] = tpv
                    if hh == 1:
                        pf[OBK] = too = A.do(lambda e, pr=pr: e.activation(OO[:, pr, :], bank[OBK][:, :], ACT.Copy), tpv)
            for pr in range(4):
                sqf = tk if pr else None
                ta = A.do(lambda e, pr=pr: e.activation(sq, OO[:, pr, :], ACT.Square), too, sqf)
                tk = T.do(lambda e, pr=pr: e.matmul(bank[0][0:8, :], bdo[:, pr, :], sq, start=pr == 0, stop=pr == 3, skip_group_check=True), ta, pf[0], tbo)
            v = V.do(lambda e: e.tensor_scalar(sq[0:8, :], bank[0][0:8, :], 1e-5, None, ALU.add), tk)
            pf[0] = v
            g = G.do(lambda e: e.tensor_tensor(rsd[0:8, :], sq[0:8, :], eps[0:8, 0:1].to_broadcast([8, 512]), ALU.pow), v)
            for pr in range(4):
                b = 1 + pr % 2
                tk = T.do(lambda e, pr=pr, b=b: e.matmul(bank[b][:, :], sel8[0:8, pr, :], rsd[0:8, :], start=True, stop=True), g, pf[b], tse)
                v = V.do(lambda e, pr=pr, b=b: e.scalar_tensor_tensor(out=OO[:, pr, :], in0=OO[:, pr, :], scalar=subg[:, 1:2], in1=bank[b][:, :], op0=ALU.mult, op1=ALU.mult), tk, tsub)
                pf[b] = v
                v = V.do(lambda e, pr=pr: e.tensor_copy(CThi[:, pr, :], OO[:, pr, :]), v)
                tct = V.do(lambda e, pr=pr: e.tensor_tensor(CTlo[:, pr, :], OO[:, pr, :], fr(CThi[:, pr, :]), ALU.subtract), v)
            A.wait(too, tk)
            tg1 = [dma(A, slot("lg"), gB, io["ln1_g_2"][l:l + 1, :].rearrange("a n -> (a n)").partition_broadcast(P)),
                   dma(A, slot("lb"), bB, io["ln1_b_2"][l:l + 1, :].rearrange("a n -> (a n)").partition_broadcast(P))]
            W.limit = W.used + 8
            hadd = {}

            def ev_res(j, t, b, tk):
                d = Hs[:, t, 512 * j:512 * j + 512]
                hadd[t] = V.do(lambda e: e.scalar_tensor_tensor(out=d, in0=d, scalar=ALPHA, in1=b[:, :], op0=ALU.mult, op1=ALU.add), tk)
                return hadd[t]

            gemm_tok(CThi, CTlo, 8, 2, 512, 2, [(0, 1, 2, 3), (4, 5, 6, 7)], ev_res, tct)
            tl1 = layernorm(Hs, gB, bB, lnb, [hadd[t] for t in range(4)], tg1)
            phase(f"ffn{l}")
            M.pos = LAY
            HThi, HTlo = M.r(8, 512), M.r(8, 512)
            FAh, FAl = M.r(22, 512), M.r(22, 512)
            gB, bB = M.f(1024), M.f(1024)
            SL = [M.f(512) for _ in range(2)]
            UP = [M.f(512) for _ in range(2)]
            tg1 = [dma(A, slot("lg"), gB, io["ln2_g_2"][l:l + 1, :].rearrange("a n -> (a n)").partition_broadcast(P)),
                   dma(A, slot("lb"), bB, io["ln2_b_2"][l:l + 1, :].rearrange("a n -> (a n)").partition_broadcast(P))]
            for t in range(NT):
                _, tht = turn(Hs[:, t, :], t, HThi, HTlo, (2 * (t % 2), 2 * (t % 2) + 1))
            W.limit = W.used + 44 + 22
            slf, upf = [None] * 2, [None] * 2
            for i in range(11):
                o = 4 * (i % 2)
                fa, fb = [None, None], [None, None]
                gemm_feat(HThi, HTlo, 8, (o, o + 1), fa, tht)
                s2 = []
                for f in range(2):
                    k = f
                    ta = A.do(lambda e, k=k, b=o + f: e.activation(SL[k], bank[b][:, :], ACT.Silu), fa[f], slf[k])
                    pf[o + f] = ta
                    s2.append((k, ta))
                gemm_feat(HThi, HTlo, 8, (o + 2, o + 3), fb, tht)
                for f in range(2):
                    k, ta = s2[f]
                    u = UP[f]
                    tv = V.do(lambda e, k=k, b=o + 2 + f, u=u: e.tensor_tensor(u, bank[b][:, :], SL[k], ALU.mult), fb[f], ta, upf[f])
                    pf[o + 2 + f] = tv
                    slf[k] = tv
                    th = A.do(lambda e, u=u, i=i, f=f: e.activation(FAh[:, 2 * i + f, :], u, ACT.Copy), tv)
                    tl = G.do(lambda e, u=u, i=i, f=f: e.tensor_tensor(FAl[:, 2 * i + f, :], u, fr(FAh[:, 2 * i + f, :]), ALU.subtract), th)
                    upf[f] = tl
            gemm_tok(FAh, FAl, 22, 2, 512, 2, [(0, 1, 2, 3), (4, 5, 6, 7)], ev_res, tl)
            tl2 = layernorm(Hs, gB, bB, lnb, [hadd[t] for t in range(4)], tg1)
            phase(f"end{l}")
        ov = io["out"].rearrange("(t p) n -> p t n", p=P)
        tout = dma(Y, slot("out"), ov, Hs, tl2)
        Y.wait(tout)

        assert W.used == len(chunks), (W.used, len(chunks))


_INS = ["x", "c_pos", "c_invf", "norm_mix", "w_in", "pe_k", "w1_k", "w2_k", "pe_v", "w1_v", "w2_v", "w_br_a", "w_br_b", "w_out",
        "norm_ffn", "w_group", "b_group", "w_expert", "b_expert", "w_gate_up", "w_down", "norm_final", "ln_in_g_2", "ln_in_b_2",
        "w_in_2", "lam_params_2", "subln_g_2", "w_f_2", "b_f_2", "w_o_2", "ln1_g_2", "ln1_b_2", "w_gu_2", "w_down_2", "ln2_g_2",
        "ln2_b_2", "c_cos", "c_sin", "c_c128"]


def constants():
    inv = (10000.0 ** (-np.arange(32, dtype=np.float64) / 32)).astype(np.float32)
    s = np.arange(S)
    w = 2 * np.pi * ((s[:, None] * s[None, :]) % S) / S
    c = np.arange(P)
    v = 2 * np.pi * ((c[:, None] * c[None, :]) % P) / P
    return {
        "c_invf": np.ascontiguousarray(np.broadcast_to(inv, (P, 32))),
        "c_cos": (np.cos(w) / np.sqrt(S)).astype(np.float32),
        "c_sin": (np.sin(w) / np.sqrt(S)).astype(np.float32),
        "c_c128": np.concatenate([np.cos(v), -np.sin(v)], axis=1).astype(np.float32) * np.float32(1.0) / np.float32(np.sqrt(P)),
    }


def lay_out(inputs):
    a = {k: np.asarray(v) for k, v in inputs.items()}
    for n in ("norm_mix", "w_in", "w1_k", "w2_k", "w1_v", "w2_v", "w_br_a", "w_br_b", "w_out", "norm_ffn", "w_group",
              "b_group", "w_expert", "b_expert", "w_gate_up", "w_down"):
        a[n] = a[n][0]
    a["x"] = a["x"][0]
    a["c_pos"] = a.pop("positions").reshape(NT, P).T
    for n in ("pe_k", "pe_v"):
        a[n] = a[n][0].reshape(16, P).T
    a["subln_g_2"] = np.tile(a["subln_g_2"], (1, 2)).reshape(2, P, 1)
    a["b_f_2"] = a["b_f_2"].reshape(2, 4, P).transpose(0, 2, 1)
    a.update(constants())
    return {n: np.ascontiguousarray(a[n]) for n in _INS}


def kernel(**inputs):
    import concourse.bacc as bacc
    from concourse.bass_utils import run_bass_kernel_spmd

    nc = bacc.Bacc("TRN2", target_bir_lowering=False, num_devices=1)
    arrays = lay_out(inputs)
    io = {n: nc.dram_tensor("in_" + n, a.shape, mybir.dt.from_np(a.dtype), kind="ExternalInput").ap() for n, a in arrays.items()}
    io["out"] = nc.dram_tensor("out_y", (S, D), F32, kind="ExternalOutput").ap()
    build_program(nc, io)
    r = run_bass_kernel_spmd(nc, [{"in_" + n: a for n, a in arrays.items()}], core_ids=[0])
    return r.results[0]["out_y"].reshape(1, S, D)
```

```python
from contextlib import ExitStack

import math

import numpy as np

import concourse.bass as bass
from concourse import mybir

F32 = mybir.dt.float32
F32R = mybir.dt.float32r
I32 = mybir.dt.int32
U32 = mybir.dt.uint32
ALU = mybir.AluOpType
ACT = mybir.ActivationFunctionType
AX = mybir.AxisListType.X

P = 128
S = 512
D = 1024
NT = S // P
KD = D // P
HD = 64
TOPK = 128
NEXP = 32
CAP = 128
NOVER = 7
TCOLS = 40
NFF = 22
BIG = 1e30
FAR = 1 << 20
ALPHA = (2.0 * 2) ** 0.25

RAW = 4
HL = 3


class Queue:

    def __init__(self, eng, name):
        self.eng, self.name, self.seen, self.sem, self.n, self.loose = eng, name, {}, None, 0, False

    def wait(self, *toks):
        for t in toks:
            if t is None:
                continue
            if isinstance(t, list):
                self.wait(*t)
            elif self.seen.get(t[0], 0) < t[1]:
                self.seen[t[0]] = t[1]
                self.eng.wait_ge(t[0], t[1])

    def do(self, fn, *toks):
        self.wait(*toks)
        self.n += 1
        self.loose = False
        fn(self.eng).then_inc(self.sem, 1)
        return (self.sem, self.n)

    def go(self, fn, *toks):
        self.wait(*toks)
        self.loose = True
        fn(self.eng)

    def last(self):
        assert not self.loose
        return (self.sem, self.n) if self.n else None


class Slot:

    def __init__(self, key):
        self.key, self.n = key, 0


def dma(q, slot, out, in_, *toks):
    q.wait(*toks)
    slot.n += 16
    q.eng.dma_start(out, in_).then_inc(slot.key, 16)
    return (slot.key, slot.n)


class Memory:

    def __init__(self, nc):
        self.nc, self.n = nc, 0
        self.base = (nc.sbuf_base + 63) // 64 * 64
        self.size = (nc.sbuf_usable_end - self.base) // 32 * 8
        self.pos, self.top = 0, 0

    def place(self, dt, *dims):
        n = int(np.prod(dims))
        t = self.nc.alloc_sbuf_tensor_at(f"m{self.n}", [P, n], dt, offset=self.base + 4 * self.pos)
        self.n += 1
        self.pos += (n + 7) // 8 * 8
        self.top = max(self.top, self.pos)
        assert self.pos <= self.size, (self.pos, self.size)
        ap = t[:, :]
        if len(dims) == 2:
            ap = ap.rearrange("p (a b) -> p a b", a=dims[0])
        elif len(dims) == 3:
            ap = ap.rearrange("p (a b c) -> p a b c", a=dims[0], b=dims[1])
        return ap

    def f(self, *dims):
        return self.place(F32, *dims)

    def r(self, *dims):
        return self.place(F32R, *dims)


def build_program(nc, io):
    ctx = ExitStack()
    with ctx:
        semnames = []

        def newsem(name):
            semnames.append(name)
            return ctx.enter_context(nc.semaphore("s_" + name))

        V, A, T = Queue(nc.vector, "V"), Queue(nc.scalar, "A"), Queue(nc.tensor, "T")
        G, Y = Queue(nc.gpsimd, "G"), Queue(nc.sync, "Y")
        slots = {}

        def slot(name):
            if name not in slots:
                slots[name] = Slot(newsem("d_" + name))
            return slots[name]

        M = Memory(nc)
        ti = M.place(I32, 96)
        bank = [ctx.enter_context(nc.psum_tensor(f"b{i}", [P, 512], F32)) for i in range(8)]
        pf = [None] * 8

        H2 = nc.dram_tensor("s_h2", [S, D], F32).ap()
        GT = nc.dram_tensor("s_gt", [16, P, S], F32).ap()
        TB = nc.dram_tensor("s_tb", [P * TCOLS, 4], I32).ap()
        Y2 = nc.dram_tensor("s_y2", [2 * S, D], F32).ap()

        def phase(name):
            ends = [q.last() for q in (V, A, T, G)]
            for q in (V, A, T, G):
                q.wait(*[t for t in ends if t and t[0] != q.sem], q.last())
                q.sem, q.n = newsem(f"{q.name}_{name}"), 0
            return ends

        def fr(ap):
            return ap.bitcast(F32)

        phase("init")

        ident = M.f(P)
        zeros = M.f(256)
        mneg = M.f(4)
        eps = M.f(4)
        raw = [M.f(1024) for _ in range(RAW)]
        DUP = [M.f(512) for _ in range(2)]
        dupf, ndup = [None, None], [0]

        def doubled(src, n, rep, *toks):
            i = ndup[0] % 2
            ndup[0] += 1
            d = DUP[i][:, 0:4 * rep * n].rearrange("p (t r n) -> p t r n", t=4, r=rep)
            tk = G.do(lambda e: e.tensor_scalar(d, src.unsqueeze(2).broadcast_to([P, 4, rep, n]), 1.0, 1.0, ALU.mult, ALU.mult), dupf[i], *toks)
            return i, DUP[i][:, 0:4 * rep * n].rearrange("p (t m) -> p t m", t=4), tk

        ring0 = M.pos
        whi = [M.r(1024) for _ in range(HL)]
        wlo = [M.r(1024) for _ in range(HL)]

        z0 = G.do(lambda e: e.memset(ident, 0.0))
        t_ident = G.do(lambda e: e.affine_select(out=ident, in_=ident, compare_op=ALU.not_equal, fill=1.0, base=0,
                                                 pattern=[[-1, P]], channel_multiplier=1), z0)
        t_zero = G.do(lambda e: e.memset(zeros, 0.0))
        m0 = G.do(lambda e: e.memset(mneg, 0.0))
        m0 = G.do(lambda e: e.memset(mneg[64:128, 0:1], -1.0), m0)
        m0 = G.do(lambda e: e.memset(mneg[32:64, 1:2], -1.0), m0)
        t_mneg = G.do(lambda e: e.memset(mneg[64:96, 2:3], -1.0), m0)
        t_eps = G.do(lambda e: e.memset(eps[:, 0:1], -0.5), t_mneg)

        chunks = []

        class Stream:
            def __init__(self):
                self.dmas = 0
                self.splits = 0
                self.used = 0
                self.rawfree = [None] * RAW
                self.hlfree = [None] * HL
                self.landed = {}
                self.ready = {}
                self.limit = 0
                self.plain = {}
                self.poolhi = False

            def load(self):
                i = self.dmas
                src, a, b = chunks[i]
                dst = raw[i % RAW][:, 0:a * b].rearrange("p (a b) -> p a b", a=a)
                self.landed[i] = dma(Y, slot(f"raw{i % RAW}"), dst, src, self.rawfree[i % RAW])
                self.dmas += 1

            def split(self):
                i = self.splits
                while self.dmas <= i:
                    self.load()
                n = chunks[i][1] * chunks[i][2]
                r, h, l = raw[i % RAW][:, 0:n], whi[i % HL][:, 0:n], wlo[i % HL][:, 0:n]
                if self.poolhi and i % 3 == 2:
                    th = G.do(lambda e: e.tensor_copy(h, r), self.landed[i], self.hlfree[i % HL])
                else:
                    th = A.do(lambda e: e.activation(h, r, ACT.Copy), self.landed[i], self.hlfree[i % HL])
                tl = V.do(lambda e: e.tensor_tensor(l, r, fr(h), ALU.subtract), th)
                self.ready[i] = [th, tl]
                self.rawfree[i % RAW] = [th, tl]
                self.splits += 1
                while self.dmas < min(i + 1 + RAW, len(chunks)):
                    self.load()

            def use(self):
                i = self.used
                while self.splits < min(i + HL, self.limit):
                    self.split()
                a, b = chunks[i][1:]
                view = lambda x: x[:, 0:a * b].rearrange("p (a b) -> p a b", a=a)
                return view(whi[i % HL]), view(wlo[i % HL]), self.ready[i]

            def used_by(self, tok):
                self.hlfree[self.used % HL] = tok
                self.used += 1

        W = Stream()

        def wchunks(w, kt, ks, cols, cw):
            v = w.rearrange("(k p) n -> p k n", p=P)
            for c in cols:
                for k in range(0, kt, ks):
                    chunks.append((v[:, k:k + ks, c:c + cw], ks, cw))

        wchunks(io["w_in"], 8, 2, range(0, 2240, 448), 448)
        wchunks(io["w_in"], 8, 4, range(2240, 4288, 256), 256)
        for c in range(0, 1024, 256):
            wchunks(io["w_br_a"], 4, 4, [c], 256)
            wchunks(io["w_br_b"], 4, 4, [c], 256)
        wchunks(io["w_out"], 8, 2, (0, 512), 512)
        for e in range(NEXP):
            wchunks(io["w_gate_up"][e], 8, 2, [0], 512)
            wchunks(io["w_down"][e], 2, 1, [0], 1024)
        for l in range(2):
            wchunks(io["w_in_2"][l], 8, 4, (1536, 1792), 256)
            wchunks(io["c_cos"], 4, 2, [0], 512)
            wchunks(io["c_sin"], 4, 2, [0], 512)
            wchunks(io["w_in_2"][l], 8, 2, (0, 512, 1024), 512)
            wo = io["w_o_2"][l].rearrange("(k p) n -> p k n", p=P)
            for c in (0, 512):
                for k in (4, 6, 0, 2):
                    chunks.append((wo[:, k:k + 2, c:c + 512], 2, 512))
            for f in range(0, 2816, 256):
                wchunks(io["w_gu_2"][l], 8, 4, [f], 256)
                wchunks(io["w_gu_2"][l], 8, 4, [2816 + f], 256)
            wchunks(io["w_down_2"][l], 22, 2, (0, 512), 512)

        def mm3(b, pairs, start, stop, *toks):
            (xh, xl), (yh, yl) = pairs
            T.wait(*toks)
            T.go(lambda e: e.matmul(b, xh, yh, start=start, stop=False, skip_group_check=True))
            T.go(lambda e: e.matmul(b, xh, yl, start=False, stop=False, skip_group_check=True))
            return T.do(lambda e: e.matmul(b, xl, yh, start=False, stop=stop, skip_group_check=True))

        def gemm_tok(xhi, xlo, kt, ks, width, nblocks, banks, evac, xready, hook=None):
            for j in range(nblocks):
                bs = banks[j % len(banks)]
                for s in range(kt // ks):
                    hi, lo, ready = W.use()
                    for kk in range(ks):
                        k = s * ks + kk
                        for t in range(NT):
                            sl = slice(t * P, t * P + P)
                            tk = mm3(bank[bs[t]][:, 0:width], ((xhi[:, k, sl], xlo[:, k, sl]), (hi[:, kk, :], lo[:, kk, :])),
                                     k == 0, k == kt - 1, ready, xready, pf[bs[t]] if k == 0 else None)
                            if k == kt - 1:
                                pf[bs[t]] = evac(j, t, bank[bs[t]], tk)
                    W.used_by(tk)
                    if hook:
                        hook()

        def gemm_feat(xhi, xlo, kt, banks, fdone, xready, hook=None):
            for s in range(kt // 4):
                hi, lo, ready = W.use()
                for kk in range(4):
                    k = s * 4 + kk
                    for f in range(2):
                        sl = slice(f * P, f * P + P)
                        tk = mm3(bank[banks[f]][:, :], ((hi[:, kk, sl], lo[:, kk, sl]), (xhi[:, k, :], xlo[:, k, :])),
                                 k == 0, k == kt - 1, ready, xready, pf[banks[f]] if k == 0 else None)
                        fdone[f] = tk
                W.used_by(tk)
                if hook:
                    hook()

        def turn(src, t, hi, lo, bs, *toks):
            for g in range(2):
                b = bs[g]
                T.wait(pf[b], t_ident, *toks)
                for k in range(4):
                    tt = T.do(lambda e, k=k, g=g, b=b: e.transpose(bank[b][:, k * P:k * P + P], src[:, (4 * g + k) * P:(4 * g + k + 1) * P], ident))
                pv = bank[b][:, :].rearrange("p (k n) -> p k n", k=4)
                h, l = hi[:, 4 * g:4 * g + 4, t * P:t * P + P], lo[:, 4 * g:4 * g + 4, t * P:t * P + P]
                th = A.do(lambda e, h=h, pv=pv: e.activation(h, pv, ACT.Copy), tt)
                tl = V.do(lambda e, h=h, l=l, pv=pv: e.tensor_tensor(l, pv, fr(h), ALU.subtract), th)
                pf[b] = tl
            return tt, tl

        def rms_rows(x, st, scr, toks):
            for t in range(NT):
                ta = A.do(lambda e, t=t: e.activation(scr, x[:, t, :], ACT.Square, accum_out=st[:, 8 + t:9 + t]), toks, A.last())
            tv = V.do(lambda e: e.tensor_scalar(st[:, 4:8], st[:, 8:12], 1.0 / D, 1e-6, ALU.mult, ALU.add), ta)
            return G.do(lambda e: e.tensor_tensor(st[:, 0:4], st[:, 4:8], eps[:, 0:1].to_broadcast([P, 4]), ALU.pow), tv, t_eps)

        FX = M.pos
        PJ = M.f(4, 2240)
        RT = M.f(12, 128)
        invf = M.f(32)
        posf = M.f(4)
        M8 = M.f(3, 8)
        Mc = M.f(512)
        DM = M.f(3, 512)
        GNS = M.f(4, 24)
        PTC = [M.f(512) for _ in range(2)]
        BD = M.f(2, 2, 128)
        AT0 = M.pos
        TM = M.f(4, 1024)
        TM1 = M.pos
        HThi, HTlo = M.r(8, 512), M.r(8, 512)
        HT1 = M.pos
        X = M.f(4, 1024)
        XN = [PJ[:, 0, 0:1024], PJ[:, 1, 0:1024]]
        gB = PJ[:, 2, 0:1024]
        st = M.f(16)
        scr = PJ[:, 3, 0:1024]
        tx = dma(A, slot("x"), X, io["x"].rearrange("(t p) n -> p t n", p=P))
        tg = dma(A, slot("g"), gB, io["norm_mix"].partition_broadcast(P))
        W.limit = 20
        for _ in range(RAW):
            W.load()
        tr_ = rms_rows(X, st, scr, [tx])
        xf = [None, None]
        for t in range(NT):
            tn = V.do(lambda e, t=t: e.scalar_tensor_tensor(out=XN[t % 2], in0=X[:, t, :], scalar=st[:, t:t + 1], in1=gB,
                                                            op0=ALU.mult, op1=ALU.mult), tr_, tg, xf[t % 2])
            xf[t % 2], tht = turn(XN[t % 2], t, HThi, HTlo, (2 * (t % 2), 2 * (t % 2) + 1), tn)
        phase("proj")
        M.pos = HT1

        def ev_proj(j, t, b, tk):
            dst = PJ[:, t, 448 * j:448 * j + 448]
            if t % 2:
                return V.do(lambda e: e.tensor_copy(dst, b[:, 0:448]), tk)
            return A.do(lambda e: e.activation(dst, b[:, 0:448], ACT.Copy), tk)

        QA, KA, VA, QI, KI, WI, QB, KVB, GB = 0, 512, 576, 640, 896, 928, 936, 1448, 2216

        RTr = [RT[:, i, :].rearrange("p (t d) -> p t d", t=4) for i in range(12)]
        WK = [M.f(3, 512)]
        tp = dma(A, slot("pos"), ti[:, 0:4], io["c_pos"])
        ti_ = dma(A, slot("invf"), invf, io["c_invf"])
        v = V.do(lambda e: e.tensor_copy(posf, ti[:, 0:4]), tp)
        for t in range(NT):
            v = V.do(lambda e, t=t: e.tensor_scalar(RTr[0][:, t, :], invf, posf[:, t:t + 1], None, ALU.mult), v, ti_)
        MAGIC = 12582912.0
        C1 = 6.28125
        C2 = float(np.float32(2 * math.pi - C1))
        C2 = float(np.frombuffer(np.uint32(np.frombuffer(np.float32(C2).tobytes(), np.uint32)[0] & 0xFFFFF000).tobytes(), np.float32)[0])
        C3 = float(np.float32(2 * math.pi - C1 - C2))
        for which, dst, off, add in (("sin", 2, 0.0, 0.0), ("cos", 3, 0.25, math.pi / 2)):
            v = V.do(lambda e, off=off: e.tensor_scalar(RT[:, 1, :], RT[:, 0, :], 1.0 / (2 * math.pi), off, ALU.mult, ALU.add), v)
            v = V.do(lambda e: e.tensor_scalar(RT[:, 1, :], RT[:, 1, :], MAGIC, None, ALU.add), v)
            v = V.do(lambda e: e.tensor_scalar(RT[:, 1, :], RT[:, 1, :], -MAGIC, None, ALU.add), v)
            v = V.do(lambda e, dst=dst: e.scalar_tensor_tensor(out=RT[:, dst, :], in0=RT[:, 1, :], scalar=-C1, in1=RT[:, 0, :], op0=ALU.mult, op1=ALU.add), v)
            v = V.do(lambda e, dst=dst: e.scalar_tensor_tensor(out=RT[:, dst, :], in0=RT[:, 1, :], scalar=-C2, in1=RT[:, dst, :], op0=ALU.mult, op1=ALU.add), v)
            v = V.do(lambda e, dst=dst: e.scalar_tensor_tensor(out=RT[:, dst, :], in0=RT[:, 1, :], scalar=-C3, in1=RT[:, dst, :], op0=ALU.mult, op1=ALU.add), v)
            v = V.do(lambda e, dst=dst, add=add: e.tensor_scalar(RT[:, dst, :], RT[:, dst, :], add, 3.1415925, ALU.add, ALU.min), v)
            v = V.do(lambda e, dst=dst: e.tensor_scalar(RT[:, dst, :], RT[:, dst, :], -3.1415925, None, ALU.max), v)
        SN, CS, NSN, NCS = RTr[4], RTr[5], RTr[6], RTr[7]
        a = A.do(lambda e: e.activation(RT[:, 4, :], RT[:, 2, :], ACT.Sin), v)
        a = A.do(lambda e: e.activation(RT[:, 5, :], RT[:, 3, :], ACT.Sin), v)
        trt = V.do(lambda e: e.tensor_scalar(RT[:, 6:8, :], RT[:, 4:6, :], -0.125, None, ALU.mult), a)
        c0 = G.do(lambda e: e.memset(Mc, 0.0))
        t_mc = G.do(lambda e: e.affine_select(out=Mc[:, 384:512], in_=Mc[:, 384:512], compare_op=ALU.is_ge, fill=BIG, base=0,
                                              pattern=[[-1, P]], channel_multiplier=1), c0)

        gemm_tok(HThi, HTlo, 8, 2, 448, 5, [(0, 1, 2, 3), (4, 5, 6, 7)], ev_proj, None)
        tproj = [V.last(), A.last()]

        def rope(E, src, dst, nh, half, cs, sn, tm, *toks):
            n = 4 * nh * half
            tmp = [tm[:, i, 0:n].rearrange("p (t h d) -> p t h d", t=4, h=nh) for i in range(4)]
            sv = src.rearrange("p t (h two d) -> p t h two d", h=nh, two=2)
            dv = dst.rearrange("p t (h two d) -> p t h two d", h=nh, two=2)
            c = cs.unsqueeze(2).broadcast_to([P, 4, nh, half])
            s = sn.unsqueeze(2).broadcast_to([P, 4, nh, half])
            x1, x2 = sv[:, :, :, 0, :], sv[:, :, :, 1, :]
            for i, (x, y) in enumerate(((x1, c), (x2, s), (x1, s), (x2, c))):
                tk = E.do(lambda e, i=i, x=x, y=y: e.tensor_tensor(tmp[i], x, y, ALU.mult), *toks)
            E.do(lambda e: e.tensor_tensor(dv[:, :, :, 0, :], tmp[0], tmp[1], ALU.subtract), tk)
            return E.do(lambda e: e.tensor_tensor(dv[:, :, :, 1, :], tmp[2], tmp[3], ALU.add), tk)

        cs16, sn16 = CS[:, :, 0:32:2], SN[:, :, 0:32:2]
        t_ki = rope(V, PJ[:, :, KI:KI + 32], PJ[:, :, KI:KI + 32], 1, 16, cs16, sn16, TM, tproj, trt)
        t_qi = rope(V, PJ[:, :, QI:QI + 256], PJ[:, :, QI:QI + 256], 8, 16, cs16, sn16, TM, t_ki)

        kI = M.r(512)
        qI = [M.r(512) for _ in range(2)]
        hI = [M.r(512) for _ in range(2)]
        RL = [TM[:, 2, 0:512], TM[:, 3, 0:512], TM[:, 2, 512:1024], TM[:, 3, 512:1024]]
        rlf = [t_qi] * 4
        AC = WK[0]

        def stack_steps(res, src, n, nrow, b, tmp, tmpfree, out, outfree, mcol, *toks):
            di, d, td = doubled(src, n, nrow // n, *toks)
            yield
            T.wait(pf[b], t_ident, td)
            for t in range(NT):
                tt = T.do(lambda e, t=t: e.transpose(bank[b][0:nrow, t * P:t * P + P], d[:, t, :], ident))
            dupf[di] = tt
            yield
            th = A.do(lambda e: e.activation(tmp[0:nrow, :], bank[b][0:nrow, :], ACT.Copy), tt, tmpfree() if callable(tmpfree) else tmpfree)
            yield
            tl = V.do(lambda e: e.scalar_tensor_tensor(out=out[0:nrow, :], in0=fr(tmp[0:nrow, :]), scalar=mneg[0:nrow, mcol:mcol + 1],
                                                       in1=bank[b][0:nrow, :], op0=ALU.mult, op1=ALU.add), th, outfree() if callable(outfree) else outfree, t_mneg)
            pf[b] = tl
            res.append(tl)

        def stack(*a):
            res = []
            for _ in stack_steps(res, *a):
                pass
            return None, res[0]

        _, tk_ki = stack(PJ[:, :, KI:KI + 32], 32, 96, 0, hI[0], None, kI, None, 2, t_ki, tproj)
        hf, qf = [tk_ki, None], [None, None]
        n_rl = 0
        acc = {}
        for h in range(8):
            _, tq = stack(PJ[:, :, QI + 32 * h:QI + 32 * h + 32], 32, 96, 1 + h % 2, hI[(h + 1) % 2], hf[(h + 1) % 2], qI[h % 2], qf[h % 2], 1, t_qi)
            hf[(h + 1) % 2] = tq
            for qt in (1, 2, 3):
                n = (qt + 1) * P
                b = 3 + n_rl % 4
                ts = T.do(lambda e, b=b, n=n, qt=qt, h=h: e.matmul(bank[b][:, 0:n], qI[h % 2][0:96, qt * P:qt * P + P], kI[0:96, 0:n], start=True, stop=True),
                          tq, tk_ki, pf[b])
                r = n_rl % 4
                ta = A.do(lambda e, b=b, n=n, r=r: e.activation(RL[r][:, 0:n], bank[b][:, 0:n], ACT.Relu), ts, rlf[r])
                pf[b] = ta
                wcol = PJ[:, qt, WI + h:WI + h + 1]
                if h == 0:
                    tv = V.do(lambda e, n=n, r=r, qt=qt, wcol=wcol: e.tensor_scalar(AC[:, qt - 1, 0:n], RL[r][:, 0:n], wcol, None, ALU.mult), ta)
                else:
                    tv = V.do(lambda e, n=n, r=r, qt=qt, wcol=wcol: e.scalar_tensor_tensor(out=AC[:, qt - 1, 0:n], in0=RL[r][:, 0:n], scalar=wcol,
                                                                                         in1=AC[:, qt - 1, 0:n], op0=ALU.mult, op1=ALU.add), ta, acc[qt])
                acc[qt] = tv
                rlf[r] = tv
                n_rl += 1
            qf[h % 2] = ts
        for qt in (1, 2, 3):
            d = slice(qt * P, qt * P + P)
            acc[qt] = V.do(lambda e, qt=qt, d=d: e.tensor_tensor(AC[:, qt - 1, d], AC[:, qt - 1, d], Mc[:, 384:512], ALU.subtract), acc[qt], t_mc)

        WA = {qt: AC[:, qt - 1, 0:(qt + 1) * P] for qt in (1, 2, 3)}
        WB = {qt: TM[:, qt - 1, 0:(qt + 1) * P] for qt in (1, 2, 3)}

        def topk_steps():
            tk = dict(acc)
            for r in range(TOPK // 8):
                for qt in (1, 2, 3):
                    src, dst = (WA, WB) if r % 2 == 0 else (WB, WA)
                    tk[qt] = V.do(lambda e, qt=qt, src=src: e.max(M8[:, qt - 1, :], src[qt]), tk[qt])
                for qt in (1, 2, 3):
                    src, dst = (WA, WB) if r % 2 == 0 else (WB, WA)
                    tk[qt] = V.do(lambda e, qt=qt, src=src, dst=dst: e.match_replace(dst[qt], M8[:, qt - 1, :], src[qt], -3e38), tk[qt],
                                  [tk[q] for q in tk])
                yield
            for qt in (1, 2, 3):
                tk[qt] = V.do(lambda e, qt=qt: e.tensor_scalar(DM[:, qt - 1, 0:(qt + 1) * P], WA[qt], -2e38, BIG, ALU.is_gt, ALU.mult), tk[qt])
            yield

        steps = topk_steps()

        GS = [M.f(512) for _ in range(4)]
        gsf = [None] * 4
        W.limit = 20 + 16
        n = 0
        for fp in range(8):
            bs = [(0, 1), (2, 3), (4, 5), (6, 7)][fp % 4]
            fd = [None, None]
            gemm_feat(HThi, HTlo, 8, bs, fd, None, hook=lambda: next(steps, None))
            for f in range(2):
                i = n % 4
                ta = A.do(lambda e, i=i, b=bs[f]: e.activation(GS[i], bank[b][:, :], ACT.Sigmoid), fd[f], gsf[i])
                pf[bs[f]] = ta
                gsf[i] = dma(G, slot(f"gs{i}"), GT[2 * fp + f], GS[i], ta)
                n += 1
        for _ in steps:
            pass
        phase("cmp")
        for q in (A, V, G):
            q.wait(*gsf)

        M.pos = TM1
        VE = [(M.r(4, 192), M.r(4, 192)) for _ in range(3)]
        VE1 = M.pos
        w1v = {"k": TM[:, 0:2, :], "v": TM[:, 2:4, :]}
        KV2 = [M.f(512), M.f(512)]
        Zt = M.f(16, 64)
        hid = M.f(2, 64)
        kcT = M.f(2, 64)
        w2 = M.f(3, 64)
        peT = M.f(2, 16)
        wl = [dma(A, slot("w1k"), w1v["k"].rearrange("p a (b c) -> p (a b) c", c=P), io["w1_k"].rearrange("(j p) c -> p j c", p=P)),
              dma(A, slot("w1v"), w1v["v"].rearrange("p a (b c) -> p (a b) c", c=P), io["w1_v"].rearrange("(j p) c -> p j c", p=P)),
              dma(A, slot("w2"), w2[:, 0, :], io["w2_k"]), dma(A, slot("w2"), w2[:, 1, :], io["w2_k"]), dma(A, slot("w2"), w2[:, 2, :], io["w2_v"]),
              dma(A, slot("pe"), peT[:, 0, :], io["pe_k"]), dma(A, slot("pe"), peT[:, 1, :], io["pe_v"])]
        wl = [wl[0], wl[1], wl[4], wl[6]]
        tsg = A.do(lambda e: e.activation(GNS, PJ[:, :, GB:GB + 24], ACT.Sigmoid))
        for hi_, lo_ in VE:
            for x in (hi_, lo_):
                for c in (0, 128):
                    tz = V.do(lambda e, x=x, c=c: e.tensor_copy(x[:, :, c:c + 64], zeros.rearrange("p (a b) -> p a b", a=4)), t_zero)
        kvf = [None, None]
        zf = None
        tbd = None
        for s_, (nm, col) in enumerate((("k", KVB), ("v", KVB + 128))):
            for kvh in range(2):
                b = kvh
                di, d, td = doubled(PJ[:, :, col + 64 * kvh:col + 64 * kvh + 64], 64, 2)
                T.wait(pf[b], td)
                for t in range(NT):
                    tt = T.do(lambda e, t=t, d=d, b=b: e.transpose(bank[b][:, t * P:t * P + P], d[:, t, :], ident))
                dupf[di] = tt
                x = KV2[kvh]
                V.do(lambda e, x=x, b=b: e.tensor_copy(x[0:64, :], bank[b][0:64, :]), tt, kvf[kvh])
                tv = V.do(lambda e, x=x, b=b: e.tensor_copy(x[64:128, 0:511], bank[b][64:128, 1:512]), tt)
                pf[b] = tv
                z = Zt[:, :, 32 * kvh:32 * kvh + 31]
                pe_b = lambda k: peT[:, s_, k:k + 8].unsqueeze(2).broadcast_to([P, 8, 31])
                s0 = x[:, 0:496].rearrange("p (n j two) -> p j two n", j=8, two=2)[:, :, 0, :]
                s1 = x[:, 16:512].rearrange("p (n j two) -> p j two n", j=8, two=2)[:, :, 0, :]
                V.do(lambda e, z=z, s0=s0, pb=pe_b(0): e.tensor_tensor(z[:, 0:8, :], s0, pb, ALU.add), tv, wl, zf)
                tzv = V.do(lambda e, z=z, s1=s1, pb=pe_b(8): e.tensor_tensor(z[:, 8:16, :], s1, pb, ALU.add), tv)
                kvf[kvh] = tzv
            b = 2
            T.wait(pf[b], tzv, wl)
            for j in range(16):
                wj = w1v[nm].rearrange("p a (b c) -> p (a b) c", c=P)[:, j, :]
                for kvh in range(2):
                    th = T.do(lambda e, j=j, wj=wj, kvh=kvh: e.matmul(bank[3 + kvh][:, 0:31], wj, Zt[:, j, 32 * kvh:32 * kvh + 31], start=j == 0, stop=j == 15,
                                                                      skip_group_check=True), pf[3 + kvh] if j == 0 else None)
            zf = th
            for kvh in range(2):
                ta = A.do(lambda e, s_=s_, kvh=kvh: e.activation(hid[:, s_, 32 * kvh:32 * kvh + 31], bank[3 + kvh][:, 0:31], ACT.Silu), th)
                pf[3 + kvh] = ta
            if nm == "k":
                T.wait(pf[5])
                for kvh in range(2):
                    w2d = w2[:, 0:2, :].rearrange("p a b -> p (a b)")
                    tt = T.do(lambda e, kvh=kvh, w2d=w2d: e.matmul(bank[5][:, 32 * kvh:32 * kvh + 31], w2d, hid[:, 0, 32 * kvh:32 * kvh + 31], start=True, stop=True,
                                                                   skip_group_check=True), ta)
                tk0 = V.do(lambda e: e.memset(kcT, 0.0))
                for kvh in range(2):
                    for r in (0, 64):
                        tkc = V.do(lambda e, kvh=kvh: e.tensor_copy(kcT[r:r + 64, kvh, r // 2:r // 2 + 31], bank[5][r:r + 64, 32 * kvh:32 * kvh + 31]), tt, tk0)
                pf[5] = tkc
            else:
                T.wait(pf[6], ta)
                for kvh in range(2):
                    tt = T.do(lambda e, kvh=kvh: e.matmul(bank[6][0:31, 64 * kvh:64 * kvh + 64], hid[:, 1, 32 * kvh:32 * kvh + 31], w2[:, 2, :], start=True, stop=True,
                                                          skip_group_check=True))
                tb0 = V.do(lambda e: e.memset(BD, 0.0))
                for kvh in range(2):
                    for h in range(4):
                        tbd = V.do(lambda e, kvh=kvh, h=h: e.tensor_copy(BD[32 * h:32 * h + 31, kvh, h // 2, 64 * (h % 2):64 * (h % 2) + 64],
                                                                         bank[6][0:31, 64 * kvh:64 * kvh + 64]), tt, tb0)
                pf[6] = tbd
        CM = TM[:, 0, 0:128]
        c0 = G.do(lambda e: e.memset(CM, 0.0), zf)
        CMv = CM.rearrange("p (t n) -> p t n", t=4)
        t_cm = G.do(lambda e: e.affine_select(out=CMv, in_=CMv, compare_op=ALU.is_ge, fill=BIG, base=-31,
                                              pattern=[[P, 4], [-16, 32]], channel_multiplier=1), c0)
        RV = TM[:, 0, 128:132]
        c0 = G.do(lambda e: e.memset(RV, 1.0), zf)
        t_rv = G.do(lambda e: e.affine_select(out=RV, in_=RV, compare_op=ALU.is_ge, fill=0.0, base=-31,
                                              pattern=[[P, 4]], channel_multiplier=1), c0)
        QN = [TM[:, 1, 0:512], TM[:, 1, 512:1024]]
        SC = TM[:, 2, :].rearrange("p (t h n) -> p t h n", t=4, h=8)
        cst = TM[:, 3, 0:256].rearrange("p (a t h) -> p a t h", a=8, t=4)
        tsc0 = V.do(lambda e: e.memset(SC, 0.0), zf)
        tsc = None
        qnf = [None, None]
        for pr in range(4):
            b = pr % 2
            T.wait(pf[b])
            for t in range(NT):
                tt = T.do(lambda e, t=t, pr=pr, b=b: e.transpose(bank[b][:, t * P:t * P + P], PJ[:, t, QB + P * pr:QB + P * pr + P], ident))
            tq = V.do(lambda e, pr=pr, b=b: e.tensor_scalar(QN[pr % 2], bank[b][:, :], -0.125, None, ALU.mult), tt, qnf[pr % 2], zf)
            pf[b] = tq
            for t in range(NT):
                ts = T.do(lambda e: e.matmul(bank[2 + t][:, 64 * pr:64 * pr + 64], QN[pr % 2][:, t * P:t * P + P], kcT[:, pr // 2, :],
                                             start=True, stop=True, skip_group_check=True), tq, tkc, pf[2 + t] if pr == 0 else None)
            qnf[pr % 2] = ts
        for t in range(NT):
            bv = bank[2 + t][:, 0:256].rearrange("p (h n) -> p h n", h=8)[:, :, 0:31]
            cm = CMv[:, t, 0:31].unsqueeze(1).broadcast_to([P, 8, 31])
            tsc = V.do(lambda e, t=t, bv=bv, cm=cm: e.tensor_tensor(SC[:, t, :, 0:31], bv, cm, ALU.add), ts, tsc0, t_cm)
            pf[2 + t] = tsc
        SCf = SC.rearrange("p t h n -> p (t h) n")[:, :, 0:31]
        cf = lambda i: cst[:, i, :, :].rearrange("p t h -> p (t h)")
        v = V.do(lambda e: e.tensor_reduce(cf(0), SCf, AX, ALU.min), tsc)
        v = V.do(lambda e: e.tensor_tensor(SCf, SCf, cf(0).unsqueeze(2).broadcast_to([P, 32, 31]), ALU.subtract), v)
        a = A.do(lambda e: e.activation(SCf, SCf, ACT.Exp, scale=-1.0), v)
        v = V.do(lambda e: e.tensor_reduce(cf(1), SCf, AX, ALU.add), a)
        v = V.do(lambda e: e.reciprocal(cf(2), cf(1)), v)
        v = V.do(lambda e: e.tensor_tensor(cst[:, 3], cst[:, 2], GNS[:, :, 0:8], ALU.mult), v, tsg)
        v = V.do(lambda e: e.tensor_tensor(cst[:, 4], cst[:, 3], RV.unsqueeze(2).broadcast_to([P, 4, 8]), ALU.mult), v, t_rv)
        v = V.do(lambda e: e.tensor_tensor(SCf, SCf, cf(4).unsqueeze(2).broadcast_to([P, 32, 31]), ALU.mult), v)
        for kvh in range(2):
            b = kvh
            T.wait(pf[b], v)
            for t in range(NT):
                tt = T.do(lambda e, t=t, kvh=kvh, b=b: e.transpose(bank[b][:, t * P:t * P + P], SC[:, t, 4 * kvh:4 * kvh + 4, :].rearrange("p h n -> p (h n)"), ident))
            tptc = V.do(lambda e, kvh=kvh, b=b: e.tensor_copy(PTC[kvh], bank[b][:, :]), tt)
            pf[b] = tptc
        tmdone = [v, tt, qnf[0], qnf[1]]
        t_qa = rope(V, PJ[:, :, QA:QA + 512], PJ[:, :, QA:QA + 512], 8, 32, NCS, NSN, TM, tmdone)
        t_ka = rope(V, PJ[:, :, KA:KA + 64], PJ[:, :, KA:KA + 64], 1, 32, CS, SN, TM, t_qa)
        t_qb = rope(V, PJ[:, :, QB:QB + 512], PJ[:, :, QB:QB + 512], 8, 32, NCS, NSN, TM, t_ka)
        t_k2 = rope(V, PJ[:, :, KVB + 256:KVB + 384], PJ[:, :, KVB + 256:KVB + 384], 2, 32, CS, SN, TM, t_qb)
        t_k4 = rope(V, PJ[:, :, KVB + 512:KVB + 640], PJ[:, :, KVB + 512:KVB + 640], 2, 32, CS, SN, TM, t_k2)
        phase("att")

        M.pos = AT0
        PTb = [(M.r(4, 512), M.r(4, 512))]
        assert M.pos <= TM1
        M.pos = VE1
        KS = [(M.r(512), M.r(512)) for _ in range(3)]
        qH = [M.r(512) for _ in range(2)]
        qS = [M.r(512) for _ in range(3)]
        Ebuf = [M.f(512) for _ in range(4)]
        sm = M.f(3, 8)
        OAB = M.size - 8192
        assert M.pos <= OAB
        M.pos = OAB
        OA = (M.r(4, 512), M.r(4, 512))
        OB = (M.r(4, 512), M.r(4, 512))
        M.pos = ring0
        PTb.append((M.r(4, 512), M.r(4, 512)))
        branches = []
        for h in range(8):
            branches.append(dict(q=("a", h), kv=0, mask="sel", gate=None, par=h % 2, o=OA, pr=h // 2,
                                 first=h % 2 == 0, last=h % 2 == 1, cmp=None))
        for h in range(8):
            for br in range(2):
                branches.append(dict(q=("b", h), kv=1 + 2 * (h // 4) + br, mask="causal", gate=(1 + br) * 8 + h, par=h % 2, o=OB, pr=h // 2,
                                     first=False, last=(h % 2 == 1 and br == 1), cmp=(h // 4, (h % 4) // 2) if (h % 2 == 0 and br == 0) else None))
        kvsrc = [(KA, VA), (KVB + 256, KVB + 384), (KVB + 512, KVB + 640), (KVB + 320, KVB + 448), (KVB + 576, KVB + 704)]
        kvset = [0, 1, 2, 0, 1]
        kvtok, kvfree, kvasked = {}, [None] * 3, set()
        qtok, qfree, qhf = {}, [None] * 3, [None, None]
        qasked = {}
        jobs = []

        def prep_kv(i):
            s = kvset[i]
            kc, vc = kvsrc[i]
            b = 7
            di, d, td = doubled(PJ[:, :, kc:kc + 64], 64, 2)
            yield
            T.wait(pf[b], td)
            for t in range(NT):
                tt = T.do(lambda e, t=t: e.transpose(bank[b][:, t * P:t * P + P], d[:, t, :], ident))
            dupf[di] = tt
            yield
            kh, kl = KS[s]
            vh, vl = VE[s]
            src = PJ[:, :, vc:vc + 64]
            th = A.do(lambda e: e.activation(kh, bank[b][:, :], ACT.Copy), tt, kvfree[s])
            th2 = A.do(lambda e: e.activation(vh[:, :, 64:128], src, ACT.Copy))
            yield
            pf[b] = V.do(lambda e: e.tensor_tensor(kl, bank[b][:, :], fr(kh), ALU.subtract), th, kvfree[s])
            kvtok[i] = V.do(lambda e: e.tensor_tensor(vl[:, :, 64:128], src, fr(vh[:, :, 64:128]), ALU.subtract), th2)

        def prep_q(key):
            i = qasked[key]
            c = (QA if key[0] == "a" else QB) + 64 * key[1]
            res = []
            yield from stack_steps(res, PJ[:, :, c:c + 64], 64, 128, 7, qH[i % 2], qhf[i % 2], qS[i % 3], qfree[i % 3], 0)
            qhf[i % 2] = res[0]
            qtok[key] = (i % 3, res[0])

        def ask(B_):
            if B_["kv"] not in kvasked:
                kvasked.add(B_["kv"])
                jobs.append(prep_kv(B_["kv"]))
            if B_["q"] not in qasked:
                qasked[B_["q"]] = len(qasked)
                jobs.append(prep_q(B_["q"]))

        def work(n):
            for _ in range(n):
                if jobs and next(jobs[0], 0) == 0:
                    jobs.pop(0)

        SBK, TBK, OBK = [0, 1], [2, 3, 4], [5, 6]
        nbr = len(branches)
        todo = [(i, qt) for i in range(nbr) for qt in range(NT)]
        NS = len(todo)
        ef = [None] * 4
        tS, tM, tX, tP, tT, tH = {}, {}, {}, {}, {}, {}
        ptf = [None, None]

        def pv_part(bi, kt):
            B_ = branches[bi]
            ob = OBK[B_["pr"] % 2]
            ph, pl = PTb[bi % 2]
            vh, vl = VE[kvset[B_["kv"]]]
            sl = slice(64, 192) if B_["par"] == 0 else slice(0, 128)
            T.wait(tH[4 * bi + 3])
            started = kt > 0
            if kt == 0 and (B_["first"] or B_["cmp"]):
                T.wait(pf[ob])
            if kt == 0 and B_["cmp"]:
                kvh, pp = B_["cmp"]
                T.go(lambda e: e.matmul(bank[ob][:, :], BD[:, kvh, pp, :], PTC[kvh], start=True, stop=False, skip_group_check=True), tptc)
                started = True
            cs_ = slice(kt * P, 512)
            for a_, b_ in ((vh, ph), (vl, ph), (vh, pl)):
                st_ = B_["first"] and not started
                started = True
                fin = B_["last"] and kt == 3 and b_ is pl
                tpv = T.do(lambda e: e.matmul(bank[ob][:, cs_], a_[:, kt, sl], b_[:, kt, cs_], start=st_, stop=fin, skip_group_check=True))
            if kt < 3:
                return
            ptf[bi % 2] = tpv
            kvfree[kvset[B_["kv"]]] = tpv
            if B_["last"]:
                oh, ol = B_["o"]
                pr = B_["pr"]
                th = A.do(lambda e: e.activation(oh[:, pr, :], bank[ob][:, :], ACT.Copy), tpv)
                pf[ob] = V.do(lambda e: e.tensor_tensor(ol[:, pr, :], bank[ob][:, :], fr(oh[:, pr, :]), ALU.subtract), th)

        for B_ in branches[0:2]:
            ask(B_)
        work(99)
        for i in range(NS + 10):
            k = i - 1
            if 0 <= k < NS:
                bi, qt = todo[k]
                B_ = branches[bi]
                n = (qt + 1) * P
                sb_ = SBK[k % 2]
                m = DM[:, qt - 1, 0:n] if (B_["mask"] == "sel" and qt > 0) else Mc[:, 384 - qt * P:512]
                E = Ebuf[k % 4]
                c = k % 8
                tM[k] = V.do(lambda e: e.tensor_tensor_reduce(E[:, 0:n], bank[sb_][:, 0:n], m, 1.0, 3e38, ALU.add, ALU.min, sm[:, 0, c:c + 1]),
                             tS[k], ef[k % 4])
                pf[sb_] = tM[k]
            k = i - 5
            if 0 <= k < NS:
                bi, qt = todo[k]
                ph, pl = PTb[bi % 2]
                dh, pv_ = ph[:, 0:qt + 1, qt * P:qt * P + P], bank[TBK[k % 3]][:, 0:(qt + 1) * P].rearrange("p (k n) -> p k n", n=P)
                th5 = A.do(lambda e: e.activation(dh, pv_, ACT.Copy), tT[k], ptf[bi % 2])
            k = i - 1
            if 0 <= k < NS:
                n = (todo[k][1] + 1) * P
                E = Ebuf[k % 4]
                c = k % 8
                tX[k] = A.do(lambda e: e.activation(E[:, 0:n], E[:, 0:n], ACT.Exp, bias=sm[:, 0, c:c + 1], scale=-1.0, accum_out=sm[:, 1, c:c + 1]), tM[k])
            k = i - 2
            if 0 <= k < NS:
                bi, qt = todo[k]
                n = (qt + 1) * P
                E = Ebuf[k % 4]
                c = k % 8
                gate = branches[bi]["gate"]
                tr2 = V.do(lambda e: e.reciprocal(sm[:, 2, c:c + 1], sm[:, 1, c:c + 1]), tX[k])
                g2 = 1.0 if gate is None else GNS[:, qt, gate:gate + 1]
                tP[k] = G.do(lambda e: e.tensor_scalar(E[:, 0:n], E[:, 0:n], sm[:, 2, c:c + 1], g2, ALU.mult, ALU.mult), tr2)
            k = i - 5
            if 0 <= k < NS:
                bi, qt = todo[k]
                ph, pl = PTb[bi % 2]
                dh, dl = ph[:, 0:qt + 1, qt * P:qt * P + P], pl[:, 0:qt + 1, qt * P:qt * P + P]
                pv_ = bank[TBK[k % 3]][:, 0:(qt + 1) * P].rearrange("p (k n) -> p k n", n=P)
                pf[TBK[k % 3]] = tH[k] = V.do(lambda e: e.tensor_tensor(dl, pv_, fr(dh), ALU.subtract), th5)
            pv_here = 9 <= i < 4 * nbr + 9
            if pv_here and i < NS and todo[i][1] == 0 and branches[todo[i][0]]["kv"] not in kvasked:
                pv_part((i - 9) // 4, (i - 9) % 4)
                pv_here = False
            work(1)
            if i < NS:
                bi, qt = todo[i]
                B_ = branches[bi]
                if qt == 0:
                    ask(B_)
                    while B_["q"] not in qtok or B_["kv"] not in kvtok:
                        work(1)
                    if bi + 2 < nbr and branches[bi + 2]["kv"] < 4:
                        ask(branches[bi + 2])
                n = (qt + 1) * P
                sb_ = SBK[i % 2]
                kh, kl = KS[kvset[B_["kv"]]]
                qs, tq = qtok[B_["q"]]
                T.wait(pf[sb_], tq, kvtok[B_["kv"]])
                T.go(lambda e: e.matmul(bank[sb_][:, 0:n], qS[qs][:, qt * P:qt * P + P], kh[:, 0:n], start=True, stop=False))
                tS[i] = T.do(lambda e: e.matmul(bank[sb_][:, 0:n], qS[qs][:, qt * P:qt * P + P], kl[:, 0:n], start=False, stop=True))
                if qt == 3:
                    qfree[qs] = tS[i]
            k = i - 4
            if 0 <= k < NS:
                qt = todo[k][1]
                E = Ebuf[k % 4]
                tb_ = TBK[k % 3]
                T.wait(pf[tb_], tP[k])
                for kt in range(qt + 1):
                    ef[k % 4] = tT[k] = T.do(lambda e, kt=kt: e.transpose(bank[tb_][:, kt * P:kt * P + P], E[:, kt * P:kt * P + P], ident))
            if pv_here:
                pv_part((i - 9) // 4, (i - 9) % 4)
        phase("merge")

        M.pos = FX
        X1 = M.f(4, 1024)
        X1E = M.pos
        MThi, MTlo = M.r(8, 512), M.r(8, 512)
        GL = [M.f(4, 512) for _ in range(2)]
        MM = [M.f(2, 512) for _ in range(2)]
        assert M.pos <= OAB
        W.limit = 36 + 8 + 8
        glf = [None, None]
        glt = {}

        def load_gates(i):
            g = GL[i % 2]
            s_ = slot(f"gl{i % 2}")
            dma(A, s_, g[:, 0:2, :], GT[2 * i:2 * i + 2].rearrange("f p n -> p f n"), glf[i % 2])
            glt[i] = dma(A, s_, g[:, 2:4, :], GT[8 + 2 * i:10 + 2 * i].rearrange("f p n -> p f n"))

        load_gates(0)
        load_gates(1)
        for i in range(4):
            fa, fb = [None, None], [None, None]
            o = 4 * (i % 2)
            gemm_feat(OA[0], OA[1], 4, (o, o + 1), fa, None)
            gemm_feat(OB[0], OB[1], 4, (o + 2, o + 3), fb, None)
            for f in range(2):
                ta = V.do(lambda e, f=f, o=o, i=i: e.tensor_tensor(MM[f][:, 0, :], bank[o + f][:, :], GL[i % 2][:, f, :], ALU.mult), fa[f], glt[i])
                pf[o + f] = ta
                tb = V.do(lambda e, f=f, o=o, i=i: e.tensor_tensor(MM[f][:, 1, :], bank[o + 2 + f][:, :], GL[i % 2][:, 2 + f, :], ALU.mult), fb[f])
                pf[o + 2 + f] = tb
                tc = V.do(lambda e, f=f: e.tensor_tensor(MM[f][:, 0, :], MM[f][:, 0, :], MM[f][:, 1, :], ALU.add), tb)
                k = 2 * i + f
                th = V.do(lambda e, f=f, k=k: e.tensor_copy(MThi[:, k, :], MM[f][:, 0, :]), tc)
                tl = V.do(lambda e, f=f, k=k: e.tensor_tensor(MTlo[:, k, :], MM[f][:, 0, :], fr(MThi[:, k, :]), ALU.subtract), th)
            glf[i % 2] = tb
            if i < 2:
                load_gates(i + 2)
        tx = [dma(A, slot("x"), X1, io["x"].rearrange("(t p) n -> p t n", p=P))]

        def ev_out(j, t, b, tk):
            return V.do(lambda e: e.tensor_tensor(X1[:, t, 512 * j:512 * j + 512], b[:, :], X1[:, t, 512 * j:512 * j + 512], ALU.add), tk, tx)

        gemm_tok(MThi, MTlo, 8, 2, 512, 2, [(0, 1, 2, 3), (4, 5, 6, 7)], ev_out, tl)
        phase("route")

        M.pos = X1E
        HThi, HTlo = M.r(8, 512), M.r(8, 512)
        XN = [M.f(1024) for _ in range(2)]
        gB = M.f(1024)
        st = M.f(16)
        scr = M.f(1024)
        wr = M.f(8, 36)
        wrh, wrl = M.r(8, 36), M.r(8, 36)
        br = M.f(36)
        tg = dma(A, slot("g"), gB, io["norm_ffn"].partition_broadcast(P))
        twr = [dma(A, slot("wr"), wr[:, :, 0:4], io["w_group"].rearrange("(k p) n -> p k n", p=P)),
               dma(A, slot("wr"), wr[:, :, 4:36], io["w_expert"].rearrange("(k p) n -> p k n", p=P))]
        tbr = [dma(A, slot("br"), br[:, 0:4], io["b_group"].partition_broadcast(P)),
               dma(A, slot("br"), br[:, 4:36], io["b_expert"].partition_broadcast(P))]
        tr_ = rms_rows(X1, st, scr, [])
        xf = [None, None]
        for t in range(NT):
            tn = V.do(lambda e, t=t: e.scalar_tensor_tensor(out=XN[t % 2], in0=X1[:, t, :], scalar=st[:, t:t + 1], in1=gB,
                                                            op0=ALU.mult, op1=ALU.mult), tr_, tg, xf[t % 2])
            t1, tht = turn(XN[t % 2], t, HThi, HTlo, (2 * (t % 2), 2 * (t % 2) + 1), tn)
            t2 = dma(G, slot(f"h2{t % 2}"), H2[t * P:t * P + P, :], XN[t % 2], tn)
            xf[t % 2] = [t1, t2]
        t_h2 = [xf[0][1], xf[1][1]]
        t1 = V.do(lambda e: e.tensor_copy(wrh, wr), twr[1])
        t1 = V.do(lambda e: e.tensor_tensor(wrl, wr, fr(wrh), ALU.subtract), t1)
        LG = M.f(4, 36)
        for t in range(NT):
            b = 4 + t % 2
            sl = slice(t * P, t * P + P)
            for k in range(8):
                tk = mm3(bank[b][:, 0:36], ((HThi[:, k, sl], HTlo[:, k, sl]), (wrh[:, k, :], wrl[:, k, :])), k == 0, k == 7, tht, t1, pf[b] if k == 0 else None)
            pf[b] = V.do(lambda e, t=t, b=b: e.tensor_tensor(LG[:, t, :], bank[b][:, 0:36], br, ALU.add), tk, tbr[1])
        tlg = pf[b]

        RS = M.f(16, 128)
        s4 = M.f(24, 4)
        IO32 = M.f(32)
        UT = M.f(128)
        ON = M.f(128)
        gi = G.do(lambda e: e.iota(ti[:, 16:48], pattern=[[1, 32]], base=0, channel_multiplier=0))
        gi = G.do(lambda e: e.tensor_copy(IO32, ti[:, 16:48]), gi)
        gt = G.do(lambda e: e.iota(ti[:, 4:8], pattern=[[P, 4]], base=0, channel_multiplier=1))
        go_ = G.do(lambda e: e.memset(ON, 1.0))
        gu = G.do(lambda e: e.affine_select(out=UT, in_=ON, compare_op=ALU.is_gt, fill=0.0, base=0, pattern=[[1, P]], channel_multiplier=-1), go_)

        def r3(i, n=32):
            return RS[:, i, 0:4 * n].rearrange("p (t n) -> p t n", t=4)

        def bc(x, n):
            return x.unsqueeze(2).broadcast_to([P, 4, n])

        def i3(n):
            return IO32[:, 0:n].unsqueeze(1).broadcast_to([P, 4, n])

        def chain(*fns, first=None):
            v = first
            for f in fns:
                v = V.do(f, v)
            return v

        def first_of(src, n, mx, idx, oh, tmp):
            return [
                lambda e: e.tensor_reduce(mx, src, AX, ALU.max),
                lambda e: e.tensor_tensor(tmp, src, bc(mx, n), ALU.is_equal),
                lambda e: e.tensor_scalar(tmp, tmp, -1000.0, 1000.0, ALU.mult, ALU.add),
                lambda e: e.tensor_tensor(tmp, tmp, i3(n), ALU.add),
                lambda e: e.tensor_reduce(idx, tmp, AX, ALU.min),
                lambda e: e.tensor_tensor(oh, i3(n), bc(idx, n), ALU.is_equal),
            ]

        gl, el = LG[:, :, 0:4], LG[:, :, 4:36]
        goh, oh1, oh2, tmp, em, e2, AS, RK, PR, CN, TMPa = (r3(0, 4), r3(1), r3(2), r3(3), r3(4), r3(5), r3(6), r3(7), r3(8), r3(9), r3(10))
        gx, gidx, gsum, gp, m1, i1, m2, i2, ex, w1_, w2_, rk1, rk2, d1, d2, big_, o1, o2 = [s4[:, i, :] for i in range(18)]
        v = chain(*first_of(gl, 4, gx, gidx, goh, r3(3, 4)), first=[tlg, gi])
        v = chain(lambda e: e.tensor_tensor(r3(3, 4), gl, bc(gx, 4), ALU.subtract), first=v)
        a = A.do(lambda e: e.activation(r3(11, 4), r3(3, 4), ACT.Exp), v)
        v = chain(lambda e: e.tensor_reduce(gsum, r3(11, 4), AX, ALU.add),
                  lambda e: e.reciprocal(gp, gsum), first=a)
        g8 = goh.unsqueeze(3).broadcast_to([P, 4, 4, 8])
        e4 = lambda x: x.rearrange("p t (g i) -> p t g i", g=4)
        v = chain(lambda e: e.tensor_tensor(e4(em), e4(el), g8, ALU.mult),
                  lambda e: e.tensor_scalar(e4(tmp), g8, BIG, -BIG, ALU.mult, ALU.add),
                  lambda e: e.tensor_tensor(em, em, tmp, ALU.add),
                  *first_of(em, 32, m1, i1, oh1, tmp),
                  lambda e: e.tensor_scalar(tmp, oh1, -3e30, None, ALU.mult),
                  lambda e: e.tensor_tensor(e2, em, tmp, ALU.add),
                  *first_of(e2, 32, m2, i2, oh2, tmp),
                  lambda e: e.tensor_tensor(w1_, m2, m1, ALU.subtract), first=v)
        a = A.do(lambda e: e.activation(ex, w1_, ACT.Exp), v)
        v = chain(lambda e: e.tensor_scalar(w2_, ex, 1.0, None, ALU.add),
                  lambda e: e.reciprocal(w1_, w2_),
                  lambda e: e.tensor_tensor(w1_, w1_, gp, ALU.mult),
                  lambda e: e.tensor_tensor(w2_, w1_, ex, ALU.mult),
                  lambda e: e.tensor_tensor(AS, oh1, oh2, ALU.add), first=a)
        T.wait(pf[6], pf[7], v, gu, go_)
        for t in range(NT):
            for u in range(t + 1):
                tk = T.do(lambda e, t=t, u=u: e.matmul(bank[6][:, 32 * t:32 * t + 32], UT if u == t else ON, AS[:, u, :], start=u == 0, stop=u == t, skip_group_check=True))
        for u in range(NT):
            tk2 = T.do(lambda e, u=u: e.matmul(bank[7][:, 0:32], ON, AS[:, u, :], start=u == 0, stop=u == 3))
        OV = M.f(8, 32)
        cnt, ovn, s_a, s_b, cex = [OV[:, i, :] for i in range(5)]
        v = chain(lambda e: e.tensor_copy(RK, bank[6][:, 0:128].rearrange("p (t n) -> p t n", t=4)),
                  lambda e: e.tensor_copy(cnt, bank[7][:, 0:32]),
                  lambda e: e.tensor_scalar(ovn, cnt, 128.5, None, ALU.is_gt),
                  lambda e: e.tensor_scalar(s_a, cnt, 256.5, None, ALU.is_gt),
                  lambda e: e.tensor_tensor(ovn, ovn, s_a, ALU.add),
                  lambda e: e.tensor_scalar(s_a, cnt, 384.5, None, ALU.is_gt),
                  lambda e: e.tensor_tensor(ovn, ovn, s_a, ALU.add),
                  lambda e: e.tensor_copy(s_a, ovn), first=[tk2])
        cur, oth = s_a, s_b
        for sh in (1, 2, 4, 8, 16):
            v = chain(lambda e, c=cur, o=oth, sh=sh: e.tensor_copy(o[:, 0:sh], c[:, 0:sh]),
                      lambda e, c=cur, o=oth, sh=sh: e.tensor_tensor(o[:, sh:32], c[:, sh:32], c[:, 0:32 - sh], ALU.add), first=v)
            cur, oth = oth, cur
        incl = cur
        v = chain(lambda e: e.tensor_tensor(cex, incl, ovn, ALU.subtract), first=v)
        p40 = M.f(4, 32)
        full = r3(12)
        j_ = r3(13)
        fl = r3(14)
        v = chain(lambda e: e.tensor_scalar(fl, RK, 127.5, None, ALU.is_gt),
                  lambda e: e.tensor_scalar(j_, RK, 255.5, None, ALU.is_gt),
                  lambda e: e.tensor_tensor(fl, fl, j_, ALU.add),
                  lambda e: e.tensor_scalar(j_, RK, 383.5, None, ALU.is_gt),
                  lambda e: e.tensor_tensor(fl, fl, j_, ALU.add),
                  lambda e: e.tensor_scalar(j_, fl, -128.0, None, ALU.mult),
                  lambda e: e.tensor_tensor(full, RK, j_, ALU.add),
                  lambda e: e.tensor_scalar(full, full, float(TCOLS), None, ALU.mult),
                  lambda e: e.tensor_tensor(j_, fl, cex.unsqueeze(1).broadcast_to([P, 4, 32]), ALU.add),
                  lambda e: e.tensor_scalar(j_, j_, 31.0, None, ALU.add),
                  lambda e: e.tensor_scalar(tmp, fl, 0.5, None, ALU.is_gt),
                  lambda e: e.tensor_tensor(j_, j_, i3(32), ALU.subtract),
                  lambda e: e.tensor_tensor(j_, j_, tmp, ALU.mult),
                  lambda e: e.tensor_tensor(j_, j_, i3(32), ALU.add),
                  lambda e: e.tensor_tensor(full, full, j_, ALU.add),
                  lambda e: e.tensor_tensor(tmp, full, oh1, ALU.mult),
                  lambda e: e.tensor_reduce(d1, tmp, AX, ALU.add),
                  lambda e: e.tensor_tensor(tmp, full, oh2, ALU.mult),
                  lambda e: e.tensor_reduce(d2, tmp, AX, ALU.add),
                  lambda e: e.tensor_copy(ti[:, 8:12], d1),
                  lambda e: e.tensor_copy(ti[:, 12:16], d2), first=v)
        PL = ti[:, 64:96].rearrange("p (k t w) -> p k t w", k=2, t=4)
        tokf = s4[:, 18, :]
        v = V.do(lambda e: e.tensor_copy(tokf, ti[:, 4:8]), v, gt)
        v = chain(lambda e: e.tensor_copy(PL[:, 0, :, 0], tokf), lambda e: e.tensor_copy(PL[:, 1, :, 0], tokf),
                  lambda e: e.tensor_copy(PL[:, 0, :, 1], tokf),
                  lambda e: e.tensor_scalar(PL[:, 1, :, 1], tokf, float(S), None, ALU.add),
                  lambda e: e.tensor_copy(PL[:, 0, :, 2].bitcast(F32), w1_),
                  lambda e: e.tensor_copy(PL[:, 1, :, 2].bitcast(F32), w2_),
                  lambda e: e.memset(PL[:, :, :, 3], 0), first=v)
        TBS = M.f(TCOLS * 4)
        TBi = TBS.bitcast(I32)
        g0 = G.do(lambda e: e.memset(TBi, FAR))
        t_fill = dma(G, slot("tbf"), TB.rearrange("(p c) w -> p (c w)", p=P), TBi, g0)
        G.wait(t_fill, v)
        sc_sl = slot("tbs")
        for k in range(2):
            for t in range(NT):
                sc_sl.n += 16
                idx = ti[:, 8 + 4 * k + t:9 + 4 * k + t].bitcast(U32)
                G.eng.indirect_dma_start(
                    TB, bass.IndirectOffsetOnAxis(idx, 0), PL[:, k, t, :], None).then_inc(sc_sl.key, 16)
        TAB = M.f(TCOLS, 4)
        t_tab = dma(G, slot("tab"), TAB.bitcast(I32), TB.rearrange("(p c) w -> p c w", p=P), (sc_sl.key, sc_sl.n))
        OE = M.f(8)
        OI = M.f(8, 10)
        v = V.last()
        for j in range(NOVER):
            v = V.do(lambda e, j=j: e.tensor_scalar(s_b if incl is s_a else s_a, incl, j + 0.5, None, ALU.is_lt), v)
            v = V.do(lambda e, j=j: e.tensor_reduce(OE[:, j:j + 1], s_b if incl is s_a else s_a, AX, ALU.add), v)
        v = V.do(lambda e: e.tensor_scalar(OE[:, 0:NOVER], OE[:, 0:NOVER], 31.0, None, ALU.min), v)
        gi2 = G.do(lambda e: e.iota(ti[:, 48:58], pattern=[[P, 10]], base=0, channel_multiplier=1))
        IOF = M.f(10)
        v = V.do(lambda e: e.tensor_copy(IOF, ti[:, 48:58]), v, gi2)
        v = V.do(lambda e: e.tensor_scalar(IOF[:, 8:10], IOF[:, 8:10], -1024.0, None, ALU.add), v)
        toi = []
        for j in range(NOVER):
            v = V.do(lambda e, j=j: e.scalar_tensor_tensor(out=OI[:, j, 0:8], in0=OE[:, j:j + 1].to_broadcast([P, 8]), scalar=1024.0, in1=IOF[:, 0:8], op0=ALU.mult, op1=ALU.add), v)
            v = V.do(lambda e, j=j: e.scalar_tensor_tensor(out=OI[:, j, 8:10], in0=OE[:, j:j + 1].to_broadcast([P, 2]), scalar=256.0, in1=IOF[:, 8:10], op0=ALU.mult, op1=ALU.add), v)
        OIi = M.f(8, 10).bitcast(I32)
        t_oi = V.do(lambda e: e.tensor_copy(OIi[:, 0:NOVER, :], OI[:, 0:NOVER, :]), v)

        XG = [M.f(1024) for _ in range(2)]
        XT = [(M.r(8, 128), M.r(8, 128)) for _ in range(2)]
        SG = [M.f(256) for _ in range(2)]
        AT = [(M.r(2, 128), M.r(2, 128)) for _ in range(2)]
        YS = [M.f(1024) for _ in range(2)]
        xz = [G.do(lambda e, x=x: e.memset(x, 0.0)) for x in XG]
        xgf, ysf = list(xz), [None, None]
        xtf, atf, sgf = [None, None], [None, None], [None, None]
        W.limit = W.used + 6 * NEXP
        gtok = {}

        def gather(c):
            i = c % 2
            s_ = slot(f"xg{i}")
            G.wait(xgf[i], t_tab, t_h2)
            s_.n += 16
            G.eng.indirect_dma_start(XG[i], None, H2, bass.IndirectOffsetOnAxis(TAB[:, c, 0:1].bitcast(U32), 0),
                                                                 bounds_check=S - 1, oob_is_err=False).then_inc(s_.key, 16)
            gtok[c] = (s_.key, s_.n)

        tyall = []

        def tokens_in(c):
            i = c % 2
            hi, lo = XT[i]
            for g in range(2):
                b = 4 + g
                T.wait(pf[b], gtok[c])
                for k in range(4):
                    tt = T.do(lambda e, k=k, g=g, b=b: e.transpose(bank[b][:, k * P:k * P + P], XG[i][:, (4 * g + k) * P:(4 * g + k + 1) * P], ident))
                pv = bank[b][:, :].rearrange("p (k n) -> p k n", k=4)
                h, l = hi[:, 4 * g:4 * g + 4, :], lo[:, 4 * g:4 * g + 4, :]
                th = A.do(lambda e, h=h, pv=pv: e.activation(h, pv, ACT.Copy), tt, xtf[i])
                tl = V.do(lambda e, h=h, l=l, pv=pv: e.tensor_tensor(l, pv, fr(h), ALU.subtract), th)
                pf[b] = tl
            xgf[i] = tt
            return tl

        def expert(c, getw, xready):
            i = c % 2
            hi, lo = XT[i]
            b = i
            for s_ in range(4):
                wh, wl_, ready, done = getw()
                for kk in range(2):
                    k = 2 * s_ + kk
                    tk = mm3(bank[b][:, :], ((hi[:, k, :], lo[:, k, :]), (wh[:, kk, :], wl_[:, kk, :])), k == 0, k == 7, ready, xready, pf[b] if k == 0 else None)
                done(tk)
            xtf[i] = tk
            ta = A.do(lambda e: e.activation(SG[i], bank[b][:, 0:256], ACT.Silu), tk, sgf[i])
            tv = V.do(lambda e: e.tensor_tensor(SG[i], SG[i], bank[b][:, 256:512], ALU.mult), ta)
            pf[b] = tv
            yield
            b = 6
            T.wait(pf[b], tv)
            for f in range(2):
                tt = T.do(lambda e, f=f, b=b: e.transpose(bank[b][:, f * P:f * P + P], SG[i][:, f * P:f * P + P], ident))
            sgf[i] = tt
            pv = bank[b][:, 0:256].rearrange("p (k n) -> p k n", k=2)
            ah, al = AT[i]
            th = A.do(lambda e: e.activation(ah, pv, ACT.Copy), tt, atf[i])
            tl = V.do(lambda e: e.tensor_tensor(al, pv, fr(ah), ALU.subtract), th)
            pf[b] = tl
            yield
            for f in range(2):
                wh, wl_, ready, done = getw()
                for n in range(2):
                    tk = mm3(bank[2 + n][:, :], ((ah[:, f, :], al[:, f, :]), (wh[:, 0, 512 * n:512 * n + 512], wl_[:, 0, 512 * n:512 * n + 512])),
                             f == 0, f == 1, ready, tl, pf[2 + n] if f == 0 else None)
                done(tk)
            atf[i] = tk
            wt = TAB[:, c, 2:3]
            ty0 = A.do(lambda e: e.activation(YS[i][:, 0:512], bank[2][:, :], ACT.Copy, scale=wt), tk, ysf[i])
            pf[2] = ty0
            ty1 = A.do(lambda e: e.activation(YS[i][:, 512:1024], bank[3][:, :], ACT.Copy, scale=wt))
            pf[3] = ty1
            s_ = slot(f"ys{i}")
            G.wait(ty1)
            s_.n += 16
            G.eng.indirect_dma_start(Y2, bass.IndirectOffsetOnAxis(TAB[:, c, 1:2].bitcast(U32), 0), YS[i], None,
                                                                 bounds_check=2 * S - 1, oob_is_err=False).then_inc(s_.key, 16)
            ysf[i] = (s_.key, s_.n)
            yield

        def ring():
            hi, lo, ready = W.use()
            return hi, lo, ready, W.used_by

        gather(0)
        gather(1)
        xr = tokens_in(0)
        for c in range(NEXP):
            ex_ = expert(c, ring, xr)
            next(ex_)
            if c + 2 < NEXP:
                pass
            xr2 = None
            if c + 1 < NEXP:
                xr2 = tokens_in(c + 1)
            if c + 2 < NEXP + NOVER:
                gather(c + 2)
            next(ex_)
            next(ex_)
            xr = xr2

        wg_rows = io["w_gate_up"].rearrange("e k n -> (e k) n")
        wd_rows = io["w_down"].rearrange("e k n -> (e k) n")
        OW = [M.f(2, 512) for _ in range(2)]
        OWR = [(M.r(2, 512), M.r(2, 512)) for _ in range(2)]
        owf = [[None, None], [None, None]]
        now = [0]

        def over_w(j):
            s = [0]

            def get():
                i = now[0] % 2
                now[0] += 1
                sl_ = slot(f"ow{i}")
                G.wait(owf[i][0], t_oi)
                if s[0] < 4:
                    for kk in range(2):
                        k = 2 * s[0] + kk
                        sl_.n += 16
                        G.eng.indirect_dma_start(
                            OW[i][:, kk, :], None, wg_rows, bass.IndirectOffsetOnAxis(OIi[:, j, k:k + 1].bitcast(U32), 0)).then_inc(sl_.key, 16)
                    a_, b_ = 2, 512
                else:
                    f = s[0] - 4
                    sl_.n += 16
                    G.eng.indirect_dma_start(
                        OW[i].rearrange("p a b -> p (a b)"), None, wd_rows, bass.IndirectOffsetOnAxis(OIi[:, j, 8 + f:9 + f].bitcast(U32), 0)).then_inc(sl_.key, 16)
                    a_, b_ = 1, 1024
                s[0] += 1
                hi, lo = OWR[i]
                th = A.do(lambda e: e.activation(hi, OW[i], ACT.Copy), (sl_.key, sl_.n), owf[i][1])
                tl = V.do(lambda e: e.tensor_tensor(lo, OW[i], fr(hi), ALU.subtract), th)
                owf[i][0] = tl
                vw = lambda x: x.rearrange("p a b -> p (a b)").rearrange("p (a b) -> p a b", a=a_)

                def done(tk):
                    owf[i][1] = tk
                return vw(hi), vw(lo), [th, tl], done
            return get

        for j in range(NOVER):
            c = NEXP + j
            xr = tokens_in(c)
            if j + 2 < NOVER and c + 2 not in gtok:
                gather(c + 2)
            for _ in expert(c, over_w(j), xr):
                pass
        phase("final")
        M.pos = X1E
        st = M.f(16)

        YA = [M.f(1024) for _ in range(2)]
        for q in (V, A, G):
            q.wait(*ysf)
        yf = [None, None]
        A.wait(*ysf)
        n = 0
        v = None
        for k in range(2):
            for t in range(NT):
                i = n % 2
                ty = dma(A, slot(f"ya{i}"), YA[i], Y2[k * S + t * P:k * S + t * P + P, :], yf[i])
                yf[i] = V.do(lambda e, i=i, t=t: e.tensor_tensor(X1[:, t, :], X1[:, t, :], YA[i], ALU.add), ty, v if k else None)
                n += 1
        tsum = V.last()
        gB = M.f(1024)
        bB = M.f(1024)
        scr = M.f(1024)
        tg = dma(A, slot("g"), gB, io["norm_final"].partition_broadcast(P))
        tr_ = rms_rows(X1, st, scr, [tsum])
        for t in range(NT):
            tn = V.do(lambda e, t=t: e.scalar_tensor_tensor(out=X1[:, t, :], in0=X1[:, t, :], scalar=st[:, t:t + 1], in1=gB, op0=ALU.mult, op1=ALU.mult), tr_, tg)
        tg2 = dma(A, slot("lg"), gB, io["ln_in_g_2"].partition_broadcast(P), tn)
        tb2 = dma(A, slot("lb"), bB, io["ln_in_b_2"].partition_broadcast(P))

        def layernorm(x, gb, bb, ln, toks, gtoks):
            bn = ln[:, 0:48].rearrange("p (t s w) -> p t s w", t=4, s=2)
            mv = ln[:, 48:56].rearrange("p (t w) -> p t w", t=4)
            rs = ln[:, 56:60]
            outs = []
            for t in range(NT):
                for s_ in range(2):
                    v = V.do(lambda e, t=t, s_=s_: e.bn_stats(bn[:, t, s_, :], x[:, t, 512 * s_:512 * s_ + 512]), toks[t])
            for t in range(NT):
                v2 = V.do(lambda e, t=t: e.bn_aggr(mv[:, t, :], bn[:, t, :, :].rearrange("p s w -> p (s w)")), v)
            v = V.do(lambda e: e.tensor_scalar(ln[:, 60:64], mv[:, :, 1], 1e-5, None, ALU.add), v2)
            g = G.do(lambda e: e.tensor_tensor(rs, ln[:, 60:64], eps[:, 0:1].to_broadcast([P, 4]), ALU.pow), v)
            for t in range(NT):
                v = V.do(lambda e, t=t: e.tensor_scalar(x[:, t, :], x[:, t, :], mv[:, t, 0:1], rs[:, t:t + 1], ALU.subtract, ALU.mult), g)
                v = V.do(lambda e, t=t: e.tensor_tensor(x[:, t, :], x[:, t, :], gb, ALU.mult), v, gtoks)
                v = V.do(lambda e, t=t: e.tensor_tensor(x[:, t, :], x[:, t, :], bb, ALU.add), v)
                outs.append(v)
            return outs

        lnb = M.f(64)
        touts = layernorm(X1, gB, bB, lnb, [tn] * 4, [tg2, tb2])
        phase("lay")

        M.pos = X1E
        Hs = X1
        lnb = M.f(64)
        small = M.f(64)
        bdo = M.f(4, 8)
        sel8 = M.f(4, 128)
        TOE = M.f(896)
        lamb = M.f(8)
        LPm = M.f(4, 32)
        subg = M.f(4)
        bfc = M.f(8)
        LAY = M.pos
        g0 = G.do(lambda e: e.memset(bdo, 0.0))
        g0b = G.do(lambda e: e.memset(sel8, 0.0))
        for pr in range(4):
            for hh in range(2):
                tbo = G.do(lambda e, pr=pr, hh=hh: e.memset(bdo[64 * hh:64 * hh + 64, pr, 2 * pr + hh:2 * pr + hh + 1], 1.0 / 64), G.last())
        tse = G.do(lambda e: e.memset(sel8[0:8, :, :], 1.0), tbo)
        sv = sel8[0:8, :, :].rearrange("p r (h d) -> p r h d", h=2)
        tse = G.do(lambda e: e.affine_select(out=sv, in_=sv, compare_op=ALU.is_equal, fill=0.0, base=0,
                                             pattern=[[-2, 4], [-1, 2], [0, 64]], channel_multiplier=1), tse)
        tio = G.do(lambda e: e.iota(TOE.bitcast(I32), pattern=[[-1, 896]], base=384, channel_multiplier=1))
        v = V.do(lambda e: e.tensor_copy(TOE, TOE.bitcast(I32)), tio)
        ttoe = V.do(lambda e: e.scalar_tensor_tensor(out=TOE, in0=TOE, scalar=-1.0, in1=TOE, op0=ALU.mult, op1=ALU.max), v)
        SC32 = 32.0 ** -0.5

        for l in range(2):
            lam_init = 0.8 - 0.6 * math.exp(-0.3 * l)
            M.pos = LAY
            HThi, HTlo = M.r(8, 512), M.r(8, 512)
            CT0 = M.pos
            CThi, CTlo = M.r(8, 512), M.r(8, 512)
            CT1 = M.pos
            tlp = dma(A, slot("lp"), LPm, io["lam_params_2"][l].partition_broadcast(P))
            tsg_ = dma(A, slot("sg"), subg[:, 0:1], io["subln_g_2"][l])
            tbf = dma(A, slot("bf"), bfc[:, 0:4], io["b_f_2"][l])
            v = V.do(lambda e: e.tensor_tensor(LPm[:, 0:4:2, :], LPm[:, 0:4:2, :], LPm[:, 1:4:2, :], ALU.mult), tlp)
            v = V.do(lambda e: e.tensor_reduce(lamb[:, 0:2], LPm[:, 0:4:2, :], AX, ALU.add), v)
            a = A.do(lambda e: e.activation(lamb[:, 2:4], lamb[:, 0:2], ACT.Exp), v)
            v = V.do(lambda e: e.tensor_tensor(lamb[:, 4:5], lamb[:, 3:4], lamb[:, 2:3], ALU.subtract), a)
            tlam = V.do(lambda e, li=lam_init: e.tensor_scalar(lamb[:, 5:6], lamb[:, 4:5], -li, None, ALU.add), v)
            tsub = V.do(lambda e, li=lam_init: e.tensor_scalar(subg[:, 1:2], subg[:, 0:1], 1.0 - li, None, ALU.mult), tsg_)
            for t in range(NT):
                _, tht = turn(Hs[:, t, :], t, HThi, HTlo, (2 * (t % 2), 2 * (t % 2) + 1))

            uT = (M.r(4, 512), M.r(4, 512))
            AB = (M.r(4, 4, 256), M.r(4, 4, 256))
            C1s = (M.r(256), M.r(256))
            wfR = (M.r(4, 128), M.r(4, 128))
            c1 = M.f(256)
            wf = M.f(4, 128)
            tc1 = dma(A, slot("c1"), c1, io["c_c128"])
            twf = dma(A, slot("wf"), wf, io["w_f_2"][l].rearrange("g c d -> c g d"))
            v = V.do(lambda e: e.tensor_copy(C1s[0], c1), tc1)
            tc1 = V.do(lambda e: e.tensor_tensor(C1s[1], c1, fr(C1s[0]), ALU.subtract), v)
            v = V.do(lambda e: e.tensor_copy(wfR[0], wf), twf)
            twf = V.do(lambda e: e.tensor_tensor(wfR[1], wf, fr(wfR[0]), ALU.subtract), v)
            W.limit = W.used + 4 + 4 + 12
            tu = {}

            def halves(b, hi, lo, tk, *toks):
                th = A.do(lambda e: e.activation(hi, b, ACT.Copy), tk, *toks)
                return V.do(lambda e: e.tensor_tensor(lo, b, fr(hi), ALU.subtract), th)

            for fp in range(2):
                fd = [None, None]
                bs = (4, 5) if fp == 0 else (6, 7)
                gemm_feat(HThi, HTlo, 8, bs, fd, tht)
                for f in range(2):
                    g = 2 * fp + f
                    pf[bs[f]] = tu[g] = halves(bank[bs[f]][:, :], uT[0][:, g, :], uT[1][:, g, :], fd[f])
            n = 0
            for g in range(4):
                for t2 in range(2):
                    b = n % 4
                    n += 1
                    for tt_ in range(2):
                        t = 2 * t2 + tt_
                        sl = slice(t * P, t * P + P)
                        tk = mm3(bank[b][:, 256 * tt_:256 * tt_ + 256], ((uT[0][:, g, sl], uT[1][:, g, sl]), C1s), True, True, tu[g], tc1, pf[b] if tt_ == 0 else None)
                    bv = bank[b][:, :].rearrange("p (t c) -> p t c", t=2)
                    pf[b] = tab = halves(bv, AB[0][:, 2 * t2:2 * t2 + 2, g, :], AB[1][:, 2 * t2:2 * t2 + 2, g, :], tk)
            for cs_ in range(2):
                for s_ in range(2):
                    hi, lo, ready = W.use()
                    for kk in range(2):
                        t = 2 * s_ + kk
                        for g in range(4):
                            c = slice(128 * cs_, 128 * cs_ + 128)
                            tk = mm3(bank[4 + g][:, :], ((AB[0][:, t, g, c], AB[1][:, t, g, c]), (hi[:, kk, :], lo[:, kk, :])),
                                     cs_ == 0 and t == 0, cs_ == 1 and t == 3, ready, tab, pf[4 + g] if (cs_ == 0 and t == 0) else None)
                    W.used_by(tk)
            for g in range(4):
                pf[4 + g] = tu[g] = halves(bank[4 + g][:, :], uT[0][:, g, :], uT[1][:, g, :], tk)
            for g in range(4):
                tk = mm3(bank[g][:, :], ((wfR[0][:, g, :], wfR[1][:, g, :]), (uT[0][:, g, :], uT[1][:, g, :])), True, True, tu[g], twf, pf[g])
                bias = bfc[:, g:g + 1]
                th = V.do(lambda e, g=g, bias=bias: e.tensor_scalar(CThi[:, 4 + g, :], bank[g][:, :], bias, None, ALU.add), tk, tbf)
                pf[g] = V.do(lambda e, g=g, bias=bias: e.scalar_tensor_tensor(out=CTlo[:, 4 + g, :], in0=bank[g][:, :], scalar=bias, in1=fr(CThi[:, 4 + g, :]),
                                                                             op0=ALU.add, op1=ALU.subtract), th)
            phase(f"qkv{l}")
            M.pos = CT1
            QK = M.f(4, 1024)
            VV = (M.r(4, 4, 192), M.r(4, 4, 192))
            for x in VV:
                for t in range(NT):
                    tz = V.do(lambda e, x=x, t=t: e.tensor_copy(x[:, t, :, 64:128], zeros.rearrange("p (a b) -> p a b", a=4)), t_zero)

            def ev_qkv(j, t, b, tk):
                if j < 2:
                    sc_ = -SC32 if j == 0 else 1.0
                    return A.do(lambda e: e.activation(QK[:, t, 512 * j:512 * j + 512], b[:, :], ACT.Copy, scale=sc_), tk)
                bv = b[:, :].rearrange("p (r h d) -> p r h d", r=4, h=2)
                vv = [x[:, t, :, :].rearrange("p r (c d) -> p r c d", c=3)[:, :, 0:3:2, :] for x in VV]
                return halves(bv, vv[0], vv[1], tk)

            gemm_tok(HThi, HTlo, 8, 2, 512, 3, [(0, 1, 2, 3), (4, 5, 6, 7)], ev_qkv, None)
            phase(f"at{l}")

            PT2 = [(HThi[:, 0:4, :], HTlo[:, 0:4, :]), (HThi[:, 4:8, :], HTlo[:, 4:8, :])]
            SH = M.r(512)
            QI2 = [CThi[:, i, :] for i in range(4)]
            KI2 = [CTlo[:, i, :] for i in range(4)]
            Eb = [M.f(2, 512) for _ in range(4)]
            AB2 = [M.f(896) for _ in range(2)]
            OO = M.f(4, 512)
            sm2 = M.f(4, 16)
            SQ = [QK[:, t, 0:512] for t in range(NT)]
            gB, bB = Eb[0].rearrange("p a b -> p (a b)"), Eb[1].rearrange("p a b -> p (a b)")
            shf, qif, kif = [None], [None] * 4, [None] * 4
            abf = [None, None]
            gens, prept, tbias = {}, {}, {}

            def part(n):
                if not 0 <= n < 32:
                    return
                if n not in gens:
                    h, c, kind = n // 4, (n // 2) % 2, n % 2
                    dst, fl, mc = ((QI2, qif, 1), (KI2, kif, 2))[kind]
                    i = (2 * h + c) % 4
                    col = 512 * kind + 64 * h + 32 * c

                    def run():
                        res = []
                        yield from stack_steps(res, QK[:, :, col:col + 32], 32, 96, 7, SH, lambda: shf[0], dst[i], lambda: fl[i], mc)
                        shf[0] = prept[n] = res[0]
                    gens[n] = run()
                next(gens[n], None)

            todo = [(h, qt) for h in range(8) for qt in range(NT)]
            NS = len(todo)
            ef = [None] * 4
            ptf = [None, None]
            tS, tM, tX, tL, tR, tE, tT, tH = {}, {}, {}, {}, {}, {}, {}, {}
            SBK, TBK, OBK = [0, 1, 2, 3], [4, 5], 6

            def pv_part(h, kt):
                pr, hh = h // 2, h % 2
                ph, pl = PT2[h % 2]
                sl = slice(64 * hh, 64 * hh + 128)
                T.wait(tH[4 * h + 3])
                if hh == 0 and kt == 0:
                    T.wait(pf[OBK])
                for x_, (a_, b_) in enumerate(((VV[0], ph), (VV[1], ph), (VV[0], pl))):
                    tpv = T.do(lambda e: e.matmul(bank[OBK][:, :], a_[:, kt, pr, sl], b_[:, kt, :], start=(hh == 0 and kt == 0 and x_ == 0),
                                                  stop=(hh == 1 and kt == 3 and x_ == 2), skip_group_check=True))
                if kt < 3:
                    return
                ptf[h % 2] = tpv
                if hh == 1:
                    pf[OBK] = A.do(lambda e: e.activation(OO[:, pr, :], bank[OBK][:, :], ACT.Copy), tpv)

            for i in range(-6, NS + 9):
                k = i - 1
                if 0 <= k < NS:
                    h, qt = todo[k]
                    m = AB2[h % 2][:, 384 - qt * P:896 - qt * P]
                    for c in range(2):
                        w = (2 * k + c) % 16
                        sb_ = SBK[(2 * k + c) % 4]
                        tM[k, c] = V.do(lambda e: e.tensor_tensor_reduce(Eb[k % 4][:, c, :], bank[sb_][:, :], m, 1.0, 3e38, ALU.add, ALU.min, sm2[:, 0, w:w + 1]),
                                        tS[k, c], ef[k % 4], tbias[h])
                        pf[sb_] = tM[k, c]
                    if qt == 3:
                        abf[h % 2] = tM[k, 1]
                k = i - 5
                if 0 <= k < NS:
                    h, qt = todo[k]
                    ph, pl = PT2[h % 2]
                    dh, dl = ph[:, :, qt * P:qt * P + P], pl[:, :, qt * P:qt * P + P]
                    pv_ = bank[TBK[k % 2]][:, :].rearrange("p (k n) -> p k n", n=P)
                    tH0 = A.do(lambda e: e.activation(dh, pv_, ACT.Copy), tT[k], ptf[h % 2])
                k = i - 1
                if 0 <= k < NS:
                    for c in range(2):
                        w = (2 * k + c) % 16
                        tX[k] = A.do(lambda e: e.activation(Eb[k % 4][:, c, :], Eb[k % 4][:, c, :], ACT.Exp, bias=sm2[:, 0, w:w + 1], scale=-1.0,
                                                            accum_out=sm2[:, 1, w:w + 1]), tM[k, c])
                k = i - 2
                if 0 <= k < NS:
                    w = (2 * k) % 16
                    E = Eb[k % 4]
                    tR[k] = V.do(lambda e: e.reciprocal(sm2[:, 2, w:w + 2], sm2[:, 1, w:w + 2]), tX[k])
                    tL[k] = G.do(lambda e: e.tensor_scalar(E[:, 1, :], E[:, 1, :], sm2[:, 2, w + 1:w + 2], lamb[:, 5:6], ALU.mult, ALU.mult), tR[k], tlam)
                k = i - 3
                if 0 <= k < NS:
                    w2_ = (2 * k) % 16
                    E2 = Eb[k % 4]
                    tE[k] = V.do(lambda e: e.scalar_tensor_tensor(out=E2[:, 0, :], in0=E2[:, 0, :], scalar=sm2[:, 2, w2_:w2_ + 1], in1=E2[:, 1, :], op0=ALU.mult, op1=ALU.add), tL[k])
                k = i - 5
                if 0 <= k < NS:
                    pf[TBK[k % 2]] = tH[k] = V.do(lambda e: e.tensor_tensor(dl, pv_, fr(dh), ALU.subtract), tH0)
                part(i + 4)
                part(i + 6)
                if 0 <= i < NS:
                    h, qt = todo[i]
                    for c in range(2):
                        sb_ = SBK[(2 * i + c) % 4]
                        qi_ = (2 * h + c) % 4
                        tS[i, c] = T.do(lambda e: e.matmul(bank[sb_][:, :], QI2[qi_][0:96, qt * P:qt * P + P], KI2[qi_][0:96, :], start=True, stop=True),
                                        pf[sb_], prept[4 * h + 3])
                        if qt == 3:
                            qif[qi_] = kif[qi_] = tS[i, c]
                k = i - 4
                if 0 <= k < NS:
                    T.wait(pf[TBK[k % 2]], tE[k])
                    for kt in range(4):
                        ef[k % 4] = tT[k] = T.do(lambda e: e.transpose(bank[TBK[k % 2]][:, kt * P:kt * P + P], Eb[k % 4][:, 0, kt * P:kt * P + P], ident))
                part(i + 5)
                part(i + 5)
                if (i + 3) % 4 == 0 and (i + 3) // 4 < 8:
                    h = (i + 3) // 4
                    tbias[h] = A.do(lambda e: e.activation(AB2[h % 2], TOE, ACT.Copy, scale=2.0 ** (-8.0 * (h + 1) / 8)), ttoe, abf[h % 2])
                if 9 <= i:
                    pv_part((i - 9) // 4, (i - 9) % 4)
            W.limit = W.used + 8
            hadd = {}

            def ev_res(j, t, b, tk):
                d = Hs[:, t, 512 * j:512 * j + 512]
                hadd[t] = V.do(lambda e: e.scalar_tensor_tensor(out=d, in0=d, scalar=ALPHA, in1=b[:, :], op0=ALU.mult, op1=ALU.add), tk)
                return hadd[t]

            def wo_chunk(j, k0, first, last, ready_rows):
                hi, lo, ready = W.use()
                for kk in range(2):
                    k = k0 + kk
                    for t in range(NT):
                        sl = slice(t * P, t * P + P)
                        b = 4 + t - 4 * j
                        tk = mm3(bank[b][:, :], ((CThi[:, k, sl], CTlo[:, k, sl]), (hi[:, kk, :], lo[:, kk, :])), first and kk == 0, last and kk == 1,
                                 ready, ready_rows.get(k), pf[b] if first and kk == 0 else None)
                        if last and kk == 1:
                            pf[b] = ev_res(j, t, bank[b], tk)
                W.used_by(tk)

            too = pf[OBK]
            wo_chunk(0, 4, True, False, {})
            for pr in range(4):
                ta = A.do(lambda e: e.activation(SQ[pr], OO[:, pr, :], ACT.Square), too)
                tk = T.do(lambda e: e.matmul(bank[0][0:8, :], bdo[:, pr, :], SQ[pr], start=pr == 0, stop=pr == 3, skip_group_check=True), ta, pf[0], tbo)
            ms, y_, z_ = [Eb[2][0:8, i, :] for i in range(2)] + [Eb[3][0:8, 0, :]]
            v = V.do(lambda e: e.tensor_scalar(ms, bank[0][0:8, :], 1e-5, None, ALU.add), tk)
            pf[0] = v
            a = A.do(lambda e: e.activation(z_, ms, ACT.Sqrt), v)
            v = V.do(lambda e: e.reciprocal(y_, z_), a)
            v = V.do(lambda e: e.tensor_tensor(z_, y_, y_, ALU.mult), v)
            v = V.do(lambda e: e.tensor_tensor(z_, z_, ms, ALU.mult), v)
            v = V.do(lambda e: e.tensor_scalar(z_, z_, -0.5, 1.5, ALU.mult, ALU.add), v)
            g = V.do(lambda e: e.tensor_tensor(y_, y_, z_, ALU.mult), v)
            wo_chunk(0, 6, False, False, {})
            rows = {}
            for pr in range(4):
                b = 1 + pr % 2
                tk = T.do(lambda e: e.matmul(bank[b][:, :], sel8[0:8, pr, :], y_, start=True, stop=True), g, pf[b], tse)
                pf[b] = v = V.do(lambda e: e.scalar_tensor_tensor(out=OO[:, pr, :], in0=OO[:, pr, :], scalar=subg[:, 1:2], in1=bank[b][:, :], op0=ALU.mult, op1=ALU.mult), tk, tsub)
                a = A.do(lambda e: e.activation(CThi[:, pr, :], OO[:, pr, :], ACT.Copy), v)
                rows[pr] = V.do(lambda e: e.tensor_tensor(CTlo[:, pr, :], OO[:, pr, :], fr(CThi[:, pr, :]), ALU.subtract), a)
            wo_chunk(0, 0, False, False, rows)
            wo_chunk(0, 2, False, True, rows)
            tg1 = [dma(A, slot("lg"), gB, io["ln1_g_2"][l:l + 1, :].rearrange("a n -> (a n)").partition_broadcast(P)),
                   dma(A, slot("lb"), bB, io["ln1_b_2"][l:l + 1, :].rearrange("a n -> (a n)").partition_broadcast(P))]
            for n_, k in enumerate((4, 6, 0, 2)):
                wo_chunk(1, k, n_ == 0, n_ == 3, rows)
            tl1 = layernorm(Hs, gB, bB, lnb, [hadd[t] for t in range(4)], tg1)
            phase(f"ffn{l}")
            M.pos = LAY
            HThi, HTlo = M.r(8, 512), M.r(8, 512)
            FAh, FAl = M.r(22, 512), M.r(22, 512)
            gB, bB = M.f(1024), M.f(1024)
            SL = [M.f(512) for _ in range(2)]
            UP = [M.f(512) for _ in range(2)]
            tg1 = [dma(A, slot("lg"), gB, io["ln2_g_2"][l:l + 1, :].rearrange("a n -> (a n)").partition_broadcast(P)),
                   dma(A, slot("lb"), bB, io["ln2_b_2"][l:l + 1, :].rearrange("a n -> (a n)").partition_broadcast(P))]
            for t in range(NT):
                _, tht = turn(Hs[:, t, :], t, HThi, HTlo, (2 * (t % 2), 2 * (t % 2) + 1))
            W.limit = W.used + 44 + 22
            slf, upf = [None] * 2, [None] * 2
            for i in range(11):
                o = 4 * (i % 2)
                fa, fb = [None, None], [None, None]
                gemm_feat(HThi, HTlo, 8, (o, o + 1), fa, tht)
                s2 = []
                for f in range(2):
                    k = f
                    ta = A.do(lambda e, k=k, b=o + f: e.activation(SL[k], bank[b][:, :], ACT.Silu), fa[f], slf[k])
                    pf[o + f] = ta
                    s2.append((k, ta))
                gemm_feat(HThi, HTlo, 8, (o + 2, o + 3), fb, tht)
                for f in range(2):
                    k, ta = s2[f]
                    u = UP[f]
                    tv = V.do(lambda e, k=k, b=o + 2 + f, u=u: e.tensor_tensor(u, bank[b][:, :], SL[k], ALU.mult), fb[f], ta, upf[f])
                    pf[o + 2 + f] = tv
                    slf[k] = tv
                    th = A.do(lambda e, u=u, i=i, f=f: e.activation(FAh[:, 2 * i + f, :], u, ACT.Copy), tv)
                    tl = G.do(lambda e, u=u, i=i, f=f: e.tensor_tensor(FAl[:, 2 * i + f, :], u, fr(FAh[:, 2 * i + f, :]), ALU.subtract), th)
                    upf[f] = tl
            gemm_tok(FAh, FAl, 22, 2, 512, 2, [(0, 1, 2, 3), (4, 5, 6, 7)], ev_res, tl)
            tl2 = layernorm(Hs, gB, bB, lnb, [hadd[t] for t in range(4)], tg1)
            phase(f"end{l}")
        ov = io["out"].rearrange("(t p) n -> p t n", p=P)
        tout = dma(Y, slot("out"), ov, Hs, tl2)
        Y.wait(tout)

        assert W.used == len(chunks), (W.used, len(chunks))


_INS = ["x", "c_pos", "c_invf", "norm_mix", "w_in", "pe_k", "w1_k", "w2_k", "pe_v", "w1_v", "w2_v", "w_br_a", "w_br_b", "w_out",
        "norm_ffn", "w_group", "b_group", "w_expert", "b_expert", "w_gate_up", "w_down", "norm_final", "ln_in_g_2", "ln_in_b_2",
        "w_in_2", "lam_params_2", "subln_g_2", "w_f_2", "b_f_2", "w_o_2", "ln1_g_2", "ln1_b_2", "w_gu_2", "w_down_2", "ln2_g_2",
        "ln2_b_2", "c_cos", "c_sin", "c_c128"]


def constants():
    inv = (10000.0 ** (-np.arange(32, dtype=np.float64) / 32)).astype(np.float32)
    s = np.arange(S)
    w = 2 * np.pi * ((s[:, None] * s[None, :]) % S) / S
    c = np.arange(P)
    v = 2 * np.pi * ((c[:, None] * c[None, :]) % P) / P
    return {
        "c_invf": np.ascontiguousarray(np.broadcast_to(inv, (P, 32))),
        "c_cos": (np.cos(w) / np.sqrt(S)).astype(np.float32),
        "c_sin": (np.sin(w) / np.sqrt(S)).astype(np.float32),
        "c_c128": np.concatenate([np.cos(v), -np.sin(v)], axis=1).astype(np.float32) * np.float32(1.0) / np.float32(np.sqrt(P)),
    }


def lay_out(inputs):
    a = {k: np.asarray(v) for k, v in inputs.items()}
    for n in ("norm_mix", "w_in", "w1_k", "w2_k", "w1_v", "w2_v", "w_br_a", "w_br_b", "w_out", "norm_ffn", "w_group",
              "b_group", "w_expert", "b_expert", "w_gate_up", "w_down"):
        a[n] = a[n][0]
    a["x"] = a["x"][0]
    a["c_pos"] = a.pop("positions").reshape(NT, P).T
    for n in ("pe_k", "pe_v"):
        a[n] = a[n][0].reshape(16, P).T
    a["subln_g_2"] = np.tile(a["subln_g_2"], (1, 2)).reshape(2, P, 1)
    a["b_f_2"] = a["b_f_2"].reshape(2, 4, P).transpose(0, 2, 1)
    a.update(constants())
    return {n: np.ascontiguousarray(a[n]) for n in _INS}


def kernel(**inputs):
    import concourse.bacc as bacc
    from concourse.bass_utils import run_bass_kernel_spmd

    nc = bacc.Bacc("TRN2", target_bir_lowering=False, num_devices=1)
    arrays = lay_out(inputs)
    io = {n: nc.dram_tensor("in_" + n, a.shape, mybir.dt.from_np(a.dtype), kind="ExternalInput").ap() for n, a in arrays.items()}
    io["out"] = nc.dram_tensor("out_y", (S, D), F32, kind="ExternalOutput").ap()
    build_program(nc, io)
    r = run_bass_kernel_spmd(nc, [{"in_" + n: a for n, a in arrays.items()}], core_ids=[0])
    return r.results[0]["out_y"].reshape(1, S, D)
```

```python
from contextlib import ExitStack

import math

import numpy as np

import concourse.bass as bass
from concourse import mybir

F32 = mybir.dt.float32
F32R = mybir.dt.float32r
I32 = mybir.dt.int32
U32 = mybir.dt.uint32
ALU = mybir.AluOpType
ACT = mybir.ActivationFunctionType
AX = mybir.AxisListType.X

P = 128
S = 512
D = 1024
NT = S // P
KD = D // P
HD = 64
TOPK = 128
NEXP = 32
CAP = 64
NOVER = 15
TCOLS = 48
NFF = 22
BIG = 1e30
FAR = 1 << 20
ALPHA = (2.0 * 2) ** 0.25

RAW = 4
HL = 3


class Queue:

    def __init__(self, eng, name):
        self.eng, self.name, self.seen, self.sem, self.n, self.loose = eng, name, {}, None, 0, False
        self.kept = None

    def put(self, fn):
        if self.kept is None:
            fn(self.eng)
        else:
            self.kept.append(fn)

    def wait(self, *toks):
        for t in toks:
            if t is None:
                continue
            if isinstance(t, list):
                self.wait(*t)
            elif self.seen.get(t[0], 0) < t[1]:
                self.seen[t[0]] = t[1]
                self.put(lambda e, t=t: e.wait_ge(t[0], t[1]))

    def do(self, fn, *toks):
        self.wait(*toks)
        self.n += 1
        self.loose = False
        sem = self.sem
        self.put(lambda e: fn(e).then_inc(sem, 1))
        return (sem, self.n)

    def go(self, fn, *toks):
        self.wait(*toks)
        self.loose = True
        self.put(fn)

    def last(self):
        assert not self.loose
        return (self.sem, self.n) if self.n else None


class Slot:

    def __init__(self, key):
        self.key, self.n = key, 0


def dma(q, slot, out, in_, *toks):
    q.wait(*toks)
    slot.n += 16
    q.eng.dma_start(out, in_).then_inc(slot.key, 16)
    return (slot.key, slot.n)


class Memory:

    def __init__(self, nc):
        self.nc, self.n = nc, 0
        self.base = (nc.sbuf_base + 63) // 64 * 64
        self.size = (nc.sbuf_usable_end - self.base) // 32 * 8
        self.pos, self.top = 0, 0

    def place(self, dt, *dims):
        n = int(np.prod(dims))
        t = self.nc.alloc_sbuf_tensor_at(f"m{self.n}", [P, n], dt, offset=self.base + 4 * self.pos)
        self.n += 1
        self.pos += (n + 7) // 8 * 8
        self.top = max(self.top, self.pos)
        assert self.pos <= self.size, (self.pos, self.size)
        ap = t[:, :]
        if len(dims) == 2:
            ap = ap.rearrange("p (a b) -> p a b", a=dims[0])
        elif len(dims) == 3:
            ap = ap.rearrange("p (a b c) -> p a b c", a=dims[0], b=dims[1])
        return ap

    def f(self, *dims):
        return self.place(F32, *dims)

    def r(self, *dims):
        return self.place(F32R, *dims)


def build_program(nc, io):
    ctx = ExitStack()
    with ctx:
        semnames = []

        def newsem(name):
            semnames.append(name)
            return ctx.enter_context(nc.semaphore("s_" + name))

        V, A, T = Queue(nc.vector, "V"), Queue(nc.scalar, "A"), Queue(nc.tensor, "T")
        G, Y = Queue(nc.gpsimd, "G"), Queue(nc.sync, "Y")
        slots = {}

        def slot(name):
            if name not in slots:
                slots[name] = Slot(newsem("d_" + name))
            return slots[name]

        M = Memory(nc)
        ti = M.place(I32, 96)
        bank = [ctx.enter_context(nc.psum_tensor(f"b{i}", [P, 512], F32)) for i in range(8)]
        pf = [None] * 8

        H2 = nc.dram_tensor("s_h2", [S, D], F32).ap()
        GT = nc.dram_tensor("s_gt", [16, P, S], F32).ap()
        Y2 = nc.dram_tensor("s_y2", [2 * S, D], F32).ap()

        def phase(name):
            ends = [q.last() for q in (V, A, T, G)]
            for q in (V, A, T, G):
                q.wait(*[t for t in ends if t and t[0] != q.sem], q.last())
                q.sem, q.n = newsem(f"{q.name}_{name}"), 0
            return ends

        def fr(ap):
            return ap.bitcast(F32)

        phase("init")

        ident = M.f(P)
        zeros = M.f(256)
        mneg = M.f(4)
        eps = M.f(4)
        raw = [M.f(1024) for _ in range(RAW)]
        DUP = [M.f(512) for _ in range(2)]
        dupf, ndup = [None, None], [0]

        def doubled(src, n, rep, *toks):
            i = ndup[0] % 2
            ndup[0] += 1
            d = DUP[i][:, 0:4 * rep * n].rearrange("p (t r n) -> p t r n", t=4, r=rep)
            tk = G.do(lambda e: e.tensor_scalar(d, src.unsqueeze(2).broadcast_to([P, 4, rep, n]), 1.0, 1.0, ALU.mult, ALU.mult), dupf[i], *toks)
            return i, DUP[i][:, 0:4 * rep * n].rearrange("p (t m) -> p t m", t=4), tk

        ring0 = M.pos
        whi = [M.r(1024) for _ in range(HL)]
        wlo = [M.r(1024) for _ in range(HL)]

        z0 = G.do(lambda e: e.memset(ident, 0.0))
        t_ident = G.do(lambda e: e.affine_select(out=ident, in_=ident, compare_op=ALU.not_equal, fill=1.0, base=0,
                                                 pattern=[[-1, P]], channel_multiplier=1), z0)
        t_zero = G.do(lambda e: e.memset(zeros, 0.0))
        m0 = G.do(lambda e: e.memset(mneg, 0.0))
        m0 = G.do(lambda e: e.memset(mneg[64:128, 0:1], -1.0), m0)
        m0 = G.do(lambda e: e.memset(mneg[32:64, 1:2], -1.0), m0)
        t_mneg = G.do(lambda e: e.memset(mneg[64:96, 2:3], -1.0), m0)
        t_eps = G.do(lambda e: e.memset(eps[:, 0:1], -0.5), t_mneg)

        chunks = []

        class Stream:
            def __init__(self):
                self.dmas = 0
                self.splits = 0
                self.used = 0
                self.rawfree = [None] * RAW
                self.hlfree = [None] * HL
                self.landed = {}
                self.ready = {}
                self.limit = 0
                self.plain = {}
                self.poolhi = False

            def load(self):
                i = self.dmas
                src, a, b = chunks[i]
                dst = raw[i % RAW][:, 0:a * b].rearrange("p (a b) -> p a b", a=a)
                self.landed[i] = dma(Y, slot(f"raw{i % RAW}"), dst, src, self.rawfree[i % RAW])
                self.dmas += 1

            def split(self):
                i = self.splits
                while self.dmas <= i:
                    self.load()
                n = chunks[i][1] * chunks[i][2]
                r, h, l = raw[i % RAW][:, 0:n], whi[i % HL][:, 0:n], wlo[i % HL][:, 0:n]
                if self.poolhi and i % 3 == 2:
                    th = G.do(lambda e: e.tensor_copy(h, r), self.landed[i], self.hlfree[i % HL])
                else:
                    th = A.do(lambda e: e.activation(h, r, ACT.Copy), self.landed[i], self.hlfree[i % HL])
                tl = V.do(lambda e: e.tensor_tensor(l, r, fr(h), ALU.subtract), th)
                self.ready[i] = [th, tl]
                self.rawfree[i % RAW] = [th, tl]
                self.splits += 1
                while self.dmas < min(i + 1 + RAW, len(chunks)):
                    self.load()

            def use(self, ahead=0):
                i = self.used + ahead
                while self.splits < min(self.used + HL, self.limit):
                    self.split()
                a, b = chunks[i][1:]
                view = lambda x: x[:, 0:a * b].rearrange("p (a b) -> p a b", a=a)
                return view(whi[i % HL]), view(wlo[i % HL]), self.ready[i]

            def used_by(self, tok):
                self.hlfree[self.used % HL] = tok
                self.used += 1

        W = Stream()

        def wchunks(w, kt, ks, cols, cw):
            v = w.rearrange("(k p) n -> p k n", p=P)
            for c in cols:
                for k in range(0, kt, ks):
                    chunks.append((v[:, k:k + ks, c:c + cw], ks, cw))

        wchunks(io["w_in"], 8, 2, range(0, 2240, 448), 448)
        wchunks(io["w_in"], 8, 4, range(2240, 4288, 256), 256)
        for c in range(0, 1024, 256):
            wchunks(io["w_br_a"], 4, 4, [c], 256)
            wchunks(io["w_br_b"], 4, 4, [c], 256)
        wchunks(io["w_out"], 8, 2, (0, 512), 512)
        for e in range(NEXP + 1):
            if e < NEXP:
                wchunks(io["w_gate_up"][e], 8, 2, [0], 512)
            if e > 0:
                wchunks(io["w_down"][e - 1], 2, 1, [0], 1024)
        for l in range(2):
            wchunks(io["w_in_2"][l], 8, 4, (1536, 1792), 256)
            wchunks(io["c_cos"], 4, 2, [0], 512)
            wchunks(io["c_sin"], 4, 2, [0], 512)
            wchunks(io["w_in_2"][l], 8, 2, (0, 512, 1024), 512)
            wo = io["w_o_2"][l].rearrange("(k p) n -> p k n", p=P)
            for c in (0, 512):
                for k in (4, 6, 0, 2):
                    chunks.append((wo[:, k:k + 2, c:c + 512], 2, 512))
            for f in range(0, 2816, 256):
                wchunks(io["w_gu_2"][l], 8, 4, [f], 256)
                wchunks(io["w_gu_2"][l], 8, 4, [2816 + f], 256)
            wchunks(io["w_down_2"][l], 22, 2, (0, 512), 512)

        def mm3(b, pairs, start, stop, *toks):
            (xh, xl), (yh, yl) = pairs
            T.wait(*toks)
            T.go(lambda e: e.matmul(b, xh, yh, start=start, stop=False, skip_group_check=True))
            T.go(lambda e: e.matmul(b, xh, yl, start=False, stop=False, skip_group_check=True))
            return T.do(lambda e: e.matmul(b, xl, yh, start=False, stop=stop, skip_group_check=True))

        def gemm_tok(xhi, xlo, kt, ks, width, nblocks, banks, evac, xready, hook=None):
            for j in range(nblocks):
                bs = banks[j % len(banks)]
                for s in range(kt // ks):
                    hi, lo, ready = W.use()
                    for kk in range(ks):
                        k = s * ks + kk
                        for t in range(NT):
                            sl = slice(t * P, t * P + P)
                            tk = mm3(bank[bs[t]][:, 0:width], ((xhi[:, k, sl], xlo[:, k, sl]), (hi[:, kk, :], lo[:, kk, :])),
                                     k == 0, k == kt - 1, ready, xready, pf[bs[t]] if k == 0 else None)
                            if k == kt - 1:
                                pf[bs[t]] = evac(j, t, bank[bs[t]], tk)
                    W.used_by(tk)
                    if hook:
                        hook()

        def gemm_feat(xhi, xlo, kt, banks, fdone, xready, hook=None):
            for s in range(kt // 4):
                hi, lo, ready = W.use()
                for kk in range(4):
                    k = s * 4 + kk
                    for f in range(2):
                        sl = slice(f * P, f * P + P)
                        tk = mm3(bank[banks[f]][:, :], ((hi[:, kk, sl], lo[:, kk, sl]), (xhi[:, k, :], xlo[:, k, :])),
                                 k == 0, k == kt - 1, ready, xready, pf[banks[f]] if k == 0 else None)
                        fdone[f] = tk
                W.used_by(tk)
                if hook:
                    hook()

        def feat_halves(xhi, xlo, banks, fdone, done):
            ws = [W.use(0), W.use(1)]
            for half in range(2):
                c = slice(256 * half, 256 * half + 256)
                for k in range(8):
                    hi, lo, ready = ws[k // 4]
                    for f in range(2):
                        sl = slice(f * P, f * P + P)
                        fdone[f] = tk = mm3(bank[banks[f]][:, c], ((hi[:, k % 4, sl], lo[:, k % 4, sl]), (xhi[:, k, c], xlo[:, k, c])),
                                            k == 0, k == 7, ready, done[2 * half + 1][1], pf[banks[f]] if k == 0 else None)
            W.used_by(tk)
            W.used_by(tk)

        def skew(n, *stages):
            for i in range(n + len(stages) - 1):
                for k, f in enumerate(stages):
                    if 0 <= i - k < n:
                        f(i - k)

        def turning(src, hi, lo, ready, done, banks=(0, 1, 2, 3)):
            def flip(t):
                for g in range(2):
                    b = banks[2 * (t % 2) + g]
                    T.wait(pf[b], t_ident, ready[t])
                    for k in range(4):
                        tt = T.do(lambda e: e.transpose(bank[b][:, k * P:k * P + P], src(t)[:, (4 * g + k) * P:(4 * g + k + 1) * P], ident))
                    done[t] = (tt, None)

            def halve(t):
                for g in range(2):
                    b = banks[2 * (t % 2) + g]
                    pv = bank[b][:, :].rearrange("p (k n) -> p k n", k=4)
                    h, l = hi[:, 4 * g:4 * g + 4, t * P:t * P + P], lo[:, 4 * g:4 * g + 4, t * P:t * P + P]
                    th = A.do(lambda e: e.activation(h, pv, ACT.Copy), done[t][0])
                    pf[b] = tl = V.do(lambda e: e.tensor_tensor(l, pv, fr(h), ALU.subtract), th)
                done[t] = (done[t][0], tl)
            return flip, halve

        def rms_stages(x, st, scr, ready, rs):
            sqd = [None] * NT

            def square(t):
                sqd[t] = A.do(lambda e: e.activation(scr, x[:, t, :], ACT.Square, accum_out=st[:, 8 + t:9 + t]), ready[t], A.last())

            def root(t):
                tv = V.do(lambda e: e.tensor_scalar(st[:, 4 + t:5 + t], st[:, 8 + t:9 + t], 1.0 / D, 1e-6, ALU.mult, ALU.add), sqd[t])
                rs[t] = G.do(lambda e: e.tensor_tensor(st[:, t:t + 1], st[:, 4 + t:5 + t], eps[:, 0:1], ALU.pow), tv, t_eps)
            return square, root

        def ln_stages(x, gb, bb, ln, ready, gtoks, out, half0=False):
            bn = ln[:, 0:48].rearrange("p (t s w) -> p t s w", t=4, s=2)
            mv = ln[:, 48:56].rearrange("p (t w) -> p t w", t=4)
            rs, nm = ln[:, 56:60], ln[:, 60:64]
            tk = {}

            def stats(t):
                v = None
                for s_ in ((1,) if half0 else (0, 1)):
                    v = V.do(lambda e: e.bn_stats(bn[:, t, s_, :], x[:, t, 512 * s_:512 * s_ + 512]), ready[t])
                v = V.do(lambda e: e.bn_aggr(mv[:, t, :], bn[:, t, :, :].rearrange("p s w -> p (s w)")), v)
                v = V.do(lambda e: e.tensor_scalar(nm[:, t:t + 1], mv[:, t, 1:2], 1e-5, None, ALU.add), v)
                tk[t] = G.do(lambda e: e.tensor_tensor(rs[:, t:t + 1], nm[:, t:t + 1], eps[:, 0:1], ALU.pow), v, t_eps)

            def apply(t):
                v = V.do(lambda e: e.tensor_scalar(nm[:, t:t + 1], mv[:, t, 0:1], rs[:, t:t + 1], -1.0, ALU.mult, ALU.mult), tk[t])
                tk[t] = A.do(lambda e: e.activation(x[:, t, :], x[:, t, :], ACT.Identity, bias=nm[:, t:t + 1], scale=rs[:, t:t + 1]), v)

            def gain(t):
                tk[t] = V.do(lambda e: e.tensor_tensor(x[:, t, :], x[:, t, :], gb, ALU.mult), tk[t], gtoks)

            def offset(t):
                g = G.do(lambda e: e.tensor_tensor(x[:, t, 0:384], x[:, t, 0:384], bb[:, 0:384], ALU.add), tk[t], gtoks)
                v = V.do(lambda e: e.tensor_tensor(x[:, t, 384:1024], x[:, t, 384:1024], bb[:, 384:1024], ALU.add), tk[t])
                out[t] = [g, v]
            return stats, apply, gain, offset

        def ln_half0(x, ln, t, tok):
            bn = ln[:, 0:48].rearrange("p (t s w) -> p t s w", t=4, s=2)
            return V.do(lambda e: e.bn_stats(bn[:, t, 0, :], x[:, t, 0:512]), tok)

        FX = M.pos
        PJ = M.f(4, 2240)
        RT = M.f(12, 128)
        invf = M.f(32)
        posf = M.f(4)
        M8 = M.f(3, 8)
        Mc = M.f(512)
        DM = M.f(3, 512)
        GNS = M.f(4, 24)
        PTC = [M.f(512) for _ in range(2)]
        BD = M.f(2, 2, 128)
        AT0 = M.pos
        TM = M.f(4, 1024)
        TM1 = M.pos
        HThi, HTlo = M.r(8, 512), M.r(8, 512)
        HT1 = M.pos
        X = M.f(4, 1024)
        XN = [PJ[:, 0, 0:1024], PJ[:, 1, 0:1024]]
        gB = PJ[:, 2, 0:1024]
        st = M.f(16)
        scr = PJ[:, 3, 0:1024]
        xv = io["x"].rearrange("(t p) n -> p t n", p=P)
        tx = [dma((A, Y)[t % 2], slot(f"x{t}"), X[:, t, :], xv[:, t, :]) for t in range(NT)]
        tg = dma(A, slot("g"), gB, io["norm_mix"].partition_broadcast(P))
        W.limit = 20
        for _ in range(RAW):
            W.load()
        rs_, nrm, done = [None] * NT, [None] * NT, [None] * NT

        def scale1(t):
            nrm[t] = V.do(lambda e: e.scalar_tensor_tensor(out=XN[t % 2], in0=X[:, t, :], scalar=st[:, t:t + 1], in1=gB,
                                                           op0=ALU.mult, op1=ALU.mult), rs_[t], tg, done[t - 2][0] if t > 1 else None)

        skew(NT, *rms_stages(X, st, scr, tx, rs_), scale1, *turning(lambda t: XN[t % 2], HThi, HTlo, nrm, done))
        phase("proj")
        M.pos = HT1

        def ev_proj(j, t, b, tk):
            dst = PJ[:, t, 448 * j:448 * j + 448]
            if t % 2:
                return V.do(lambda e: e.tensor_copy(dst, b[:, 0:448]), tk)
            return A.do(lambda e: e.activation(dst, b[:, 0:448], ACT.Copy), tk)

        QA, KA, VA, QI, KI, WI, QB, KVB, GB = 0, 512, 576, 640, 896, 928, 936, 1448, 2216

        RTr = [RT[:, i, :].rearrange("p (t d) -> p t d", t=4) for i in range(12)]
        WK = [M.f(3, 512)]
        tp = dma(A, slot("pos"), ti[:, 0:4], io["c_pos"])
        ti_ = dma(A, slot("invf"), invf, io["c_invf"])
        v = V.do(lambda e: e.tensor_copy(posf, ti[:, 0:4]), tp)
        for t in range(NT):
            v = V.do(lambda e, t=t: e.tensor_scalar(RTr[0][:, t, :], invf, posf[:, t:t + 1], None, ALU.mult), v, ti_)
        MAGIC = 12582912.0
        C1 = 6.28125
        C2 = float(np.float32(2 * math.pi - C1))
        C2 = float(np.frombuffer(np.uint32(np.frombuffer(np.float32(C2).tobytes(), np.uint32)[0] & 0xFFFFF000).tobytes(), np.float32)[0])
        C3 = float(np.float32(2 * math.pi - C1 - C2))
        for which, dst, off, add in (("sin", 2, 0.0, 0.0), ("cos", 3, 0.25, math.pi / 2)):
            v = V.do(lambda e, off=off: e.tensor_scalar(RT[:, 1, :], RT[:, 0, :], 1.0 / (2 * math.pi), off, ALU.mult, ALU.add), v)
            v = V.do(lambda e: e.tensor_scalar(RT[:, 1, :], RT[:, 1, :], MAGIC, None, ALU.add), v)
            v = V.do(lambda e: e.tensor_scalar(RT[:, 1, :], RT[:, 1, :], -MAGIC, None, ALU.add), v)
            v = V.do(lambda e, dst=dst: e.scalar_tensor_tensor(out=RT[:, dst, :], in0=RT[:, 1, :], scalar=-C1, in1=RT[:, 0, :], op0=ALU.mult, op1=ALU.add), v)
            v = V.do(lambda e, dst=dst: e.scalar_tensor_tensor(out=RT[:, dst, :], in0=RT[:, 1, :], scalar=-C2, in1=RT[:, dst, :], op0=ALU.mult, op1=ALU.add), v)
            v = V.do(lambda e, dst=dst: e.scalar_tensor_tensor(out=RT[:, dst, :], in0=RT[:, 1, :], scalar=-C3, in1=RT[:, dst, :], op0=ALU.mult, op1=ALU.add), v)
            v = V.do(lambda e, dst=dst, add=add: e.tensor_scalar(RT[:, dst, :], RT[:, dst, :], add, 3.1415925, ALU.add, ALU.min), v)
            v = V.do(lambda e, dst=dst: e.tensor_scalar(RT[:, dst, :], RT[:, dst, :], -3.1415925, None, ALU.max), v)
        SN, CS, NSN, NCS = RTr[4], RTr[5], RTr[6], RTr[7]
        a = A.do(lambda e: e.activation(RT[:, 4, :], RT[:, 2, :], ACT.Sin), v)
        a = A.do(lambda e: e.activation(RT[:, 5, :], RT[:, 3, :], ACT.Sin), v)
        trt = V.do(lambda e: e.tensor_scalar(RT[:, 6:8, :], RT[:, 4:6, :], -0.125, None, ALU.mult), a)
        c0 = G.do(lambda e: e.memset(Mc, 0.0))
        t_mc = G.do(lambda e: e.affine_select(out=Mc[:, 384:512], in_=Mc[:, 384:512], compare_op=ALU.is_ge, fill=BIG, base=0,
                                              pattern=[[-1, P]], channel_multiplier=1), c0)

        def rope(E, src, dst, nh, half, cs, sn, tm, *toks):
            n = 4 * nh * half
            tmp = [tm[:, i, 0:n].rearrange("p (t h d) -> p t h d", t=4, h=nh) for i in range(4)]
            sv = src.rearrange("p t (h two d) -> p t h two d", h=nh, two=2)
            dv = dst.rearrange("p t (h two d) -> p t h two d", h=nh, two=2)
            c = cs.unsqueeze(2).broadcast_to([P, 4, nh, half])
            s = sn.unsqueeze(2).broadcast_to([P, 4, nh, half])
            x1, x2 = sv[:, :, :, 0, :], sv[:, :, :, 1, :]
            for i, (x, y) in enumerate(((x1, c), (x2, s), (x1, s), (x2, c))):
                tk = E.do(lambda e, i=i, x=x, y=y: e.tensor_tensor(tmp[i], x, y, ALU.mult), *toks)
            E.do(lambda e: e.tensor_tensor(dv[:, :, :, 0, :], tmp[0], tmp[1], ALU.subtract), tk)
            return E.do(lambda e: e.tensor_tensor(dv[:, :, :, 1, :], tmp[2], tmp[3], ALU.add), tk)

        cs16, sn16 = CS[:, :, 0:32:2], SN[:, :, 0:32:2]
        kI = M.r(512)
        qI = [M.r(512) for _ in range(2)]
        hI = [M.r(512) for _ in range(2)]
        RL = [TM[:, 2, 0:512], TM[:, 3, 0:512], TM[:, 2, 512:1024], TM[:, 3, 512:1024]]
        rlf = [None] * 4
        AC = WK[0]

        def stack_steps(res, src, n, nrow, b, tmp, tmpfree, out, outfree, mcol, *toks):
            di, d, td = doubled(src, n, nrow // n, *toks)
            yield
            T.wait(pf[b], t_ident, td)
            for t in range(NT):
                tt = T.do(lambda e, t=t: e.transpose(bank[b][0:nrow, t * P:t * P + P], d[:, t, :], ident))
            dupf[di] = tt
            yield
            th = A.do(lambda e: e.activation(tmp[0:nrow, :], bank[b][0:nrow, :], ACT.Copy), tt, tmpfree() if callable(tmpfree) else tmpfree)
            yield
            tl = V.do(lambda e: e.scalar_tensor_tensor(out=out[0:nrow, :], in0=fr(tmp[0:nrow, :]), scalar=mneg[0:nrow, mcol:mcol + 1],
                                                       in1=bank[b][0:nrow, :], op0=ALU.mult, op1=ALU.add), th, outfree() if callable(outfree) else outfree, t_mneg)
            pf[b] = tl
            res.append(tl)

        def stack(*a):
            res = []
            for _ in stack_steps(res, *a):
                pass
            return None, res[0]

        acc = {}

        def index_steps():
            t_ki = rope(V, PJ[:, :, KI:KI + 32], PJ[:, :, KI:KI + 32], 1, 16, cs16, sn16, TM, [V.last(), A.last()], trt)
            t_qi = rope(V, PJ[:, :, QI:QI + 256], PJ[:, :, QI:QI + 256], 8, 16, cs16, sn16, TM, t_ki)
            for i in range(4):
                rlf[i] = t_qi
            n_rl = 0
            hf, gens, got, qf = [None, None], {}, {-1: []}, [None, None]

            def copies(h):
                got[h] = []
                if h < 0:
                    gens[h] = stack_steps(got[h], PJ[:, :, KI:KI + 32], 32, 96, 1, hI[1], lambda: hf[1], kI, None, 2, t_ki)
                else:
                    gens[h] = stack_steps(got[h], PJ[:, :, QI + 32 * h:QI + 32 * h + 32], 32, 96, h % 2, hI[h % 2], lambda: hf[h % 2], qI[h % 2],
                                          lambda: qf[h % 2], 1, t_qi)
                next(gens[h])

            def halves_(h):
                for _ in gens[h]:
                    pass
                hf[h % 2] = got[h][0]

            for i in range(-1, 13, 2):
                for h in (i - 4, i - 3):
                    if not 0 <= h < 8:
                        continue
                    for qt in (1, 2, 3):
                        n = (qt + 1) * P
                        b = 2 + n_rl % 2
                        ts = T.do(lambda e: e.matmul(bank[b][:, 0:n], qI[h % 2][0:96, qt * P:qt * P + P], kI[0:96, 0:n], start=True, stop=True),
                                  got[h], got[-1], pf[b])
                        r = n_rl % 4
                        pf[b] = ta = A.do(lambda e: e.activation(RL[r][:, 0:n], bank[b][:, 0:n], ACT.Relu), ts, rlf[r])
                        wcol = PJ[:, qt, WI + h:WI + h + 1]
                        if h == 0:
                            tv = V.do(lambda e: e.tensor_scalar(AC[:, qt - 1, 0:n], RL[r][:, 0:n], wcol, None, ALU.mult), ta)
                        else:
                            tv = V.do(lambda e: e.scalar_tensor_tensor(out=AC[:, qt - 1, 0:n], in0=RL[r][:, 0:n], scalar=wcol,
                                                                       in1=AC[:, qt - 1, 0:n], op0=ALU.mult, op1=ALU.add), ta, acc[qt])
                        acc[qt] = rlf[r] = tv
                        n_rl += 1
                    qf[h % 2] = ts
                for h in (i - 2, i - 1):
                    if -1 <= h < 8:
                        halves_(h)
                for h in (i, i + 1):
                    if -1 <= h < 8:
                        copies(h)
                yield
            for qt in (1, 2, 3):
                d = slice(qt * P, qt * P + P)
                acc[qt] = V.do(lambda e: e.tensor_tensor(AC[:, qt - 1, d], AC[:, qt - 1, d], Mc[:, 384:512], ALU.subtract), acc[qt], t_mc)

        isteps = index_steps()

        def index_hook():
            if W.used >= 12:
                next(isteps, None)

        Q4 = (4, 5, 6, 7)
        gemm_tok(HThi, HTlo, 8, 2, 448, 5, [(0, 1, 2, 3), Q4, (0, 1, 2, 3), Q4, Q4], ev_proj, None, hook=index_hook)
        tproj = [V.last(), A.last()]
        for _ in isteps:
            pass

        WA = {qt: AC[:, qt - 1, 0:(qt + 1) * P] for qt in (1, 2, 3)}
        WB = {qt: TM[:, qt - 1, 0:(qt + 1) * P] for qt in (1, 2, 3)}

        def topk_steps():
            tk = dict(acc)
            for r in range(TOPK // 8):
                for qt in (1, 2, 3):
                    src, dst = (WA, WB) if r % 2 == 0 else (WB, WA)
                    tk[qt] = V.do(lambda e, qt=qt, src=src: e.max(M8[:, qt - 1, :], src[qt]), tk[qt])
                for qt in (1, 2, 3):
                    src, dst = (WA, WB) if r % 2 == 0 else (WB, WA)
                    tk[qt] = V.do(lambda e, qt=qt, src=src, dst=dst: e.match_replace(dst[qt], M8[:, qt - 1, :], src[qt], -3e38), tk[qt],
                                  [tk[q] for q in tk])
                yield
            for qt in (1, 2, 3):
                tk[qt] = V.do(lambda e, qt=qt: e.tensor_scalar(DM[:, qt - 1, 0:(qt + 1) * P], WA[qt], -2e38, BIG, ALU.is_gt, ALU.mult), tk[qt])
            yield

        steps = topk_steps()

        GS = [M.f(512) for _ in range(4)]
        W1 = [M.f(16, 128) for _ in range(2)]
        TG = M.f(4, 512)
        KV2 = [M.f(512), M.f(512)]
        Zt = M.f(16, 64)
        hid = M.f(2, 64)
        kcT = M.f(2, 64)
        w2 = M.f(3, 64)
        peT = M.f(2, 16)
        twl = [dma(A, slot("w1k"), W1[0], io["w1_k"].rearrange("(j p) c -> p j c", p=P)),
               dma(A, slot("w1v"), W1[1], io["w1_v"].rearrange("(j p) c -> p j c", p=P))]
        wl = [dma(A, slot("w2"), w2[:, 0, :], io["w2_k"]), dma(A, slot("w2"), w2[:, 1, :], io["w2_k"]), dma(A, slot("w2"), w2[:, 2, :], io["w2_v"]),
              dma(A, slot("pe"), peT[:, 0, :], io["pe_k"]), dma(A, slot("pe"), peT[:, 1, :], io["pe_v"])]
        wl = [*twl, wl[2], wl[4]]

        def compress_steps():
            v0 = V.do(lambda e: e.memset(Zt[:, :, 31:32], 0.0))
            tk0 = V.do(lambda e: e.memset(kcT, 0.0))
            tb0 = V.do(lambda e: e.memset(BD, 0.0))
            kvf, zf = [None, None], None
            for s_, col in enumerate((KVB, KVB + 128)):
                dd = [doubled(PJ[:, :, col + 64 * kvh:col + 64 * kvh + 64], 64, 2, tproj) for kvh in range(2)]
                yield None
                for kvh in range(2):
                    di, d, td = dd[kvh]
                    b = kvh
                    T.wait(pf[b], td)
                    for t in range(NT):
                        tt = T.do(lambda e: e.transpose(bank[b][:, t * P:t * P + P], d[:, t, :], ident))
                    dupf[di] = tt
                    x = KV2[kvh]
                    V.do(lambda e: e.tensor_copy(x[0:64, :], bank[b][0:64, :]), tt, kvf[kvh])
                    pf[b] = tv = V.do(lambda e: e.tensor_copy(x[64:128, 0:511], bank[b][64:128, 1:512]), tt)
                    z = Zt[:, :, 32 * kvh:32 * kvh + 31]
                    for j0 in (0, 8):
                        pb = peT[:, s_, j0:j0 + 8].unsqueeze(2).broadcast_to([P, 8, 31])
                        sx = x[:, 2 * j0:2 * j0 + 496].rearrange("p (n j two) -> p j two n", j=8, two=2)[:, :, 0, :]
                        tzv = V.do(lambda e: e.tensor_tensor(z[:, j0:j0 + 8, :], sx, pb, ALU.add), tv, wl, zf)
                    kvf[kvh] = tzv
                yield None
                T.wait(tzv, wl)
                for j in range(16):
                    th = T.do(lambda e: e.matmul(bank[3][:, 0:63], W1[s_][:, j, :], Zt[:, j, 0:63], start=j == 0, stop=j == 15), pf[3] if j == 0 else None, v0)
                zf = th
                pf[3] = ta = A.do(lambda e: e.activation(hid[:, s_, 0:63], bank[3][:, 0:63], ACT.Silu), th)
                yield None
                T.wait(pf[2], ta)
                if s_ == 0:
                    for kvh in range(2):
                        w2d = w2[:, 0:2, :].rearrange("p a b -> p (a b)")
                        tt = T.do(lambda e: e.matmul(bank[2][:, 32 * kvh:32 * kvh + 31], w2d, hid[:, 0, 32 * kvh:32 * kvh + 31], start=True, stop=True,
                                                     skip_group_check=True))
                    for kvh in range(2):
                        for r in (0, 64):
                            pf[2] = tkc = V.do(lambda e: e.tensor_copy(kcT[r:r + 64, kvh, r // 2:r // 2 + 31], bank[2][r:r + 64, 32 * kvh:32 * kvh + 31]), tt, tk0)
                else:
                    for kvh in range(2):
                        tt = T.do(lambda e: e.matmul(bank[2][0:31, 64 * kvh:64 * kvh + 64], hid[:, 1, 32 * kvh:32 * kvh + 31], w2[:, 2, :], start=True, stop=True,
                                                     skip_group_check=True))
                    for kvh in range(2):
                        for h in range(4):
                            pf[2] = tbd = V.do(lambda e: e.tensor_copy(BD[32 * h:32 * h + 31, kvh, h // 2, 64 * (h % 2):64 * (h % 2) + 64],
                                                                       bank[2][0:31, 64 * kvh:64 * kvh + 64]), tt, tb0)

        csteps = compress_steps()
        next(csteps)
        t_qa = rope(G, PJ[:, :, QA:QA + 256], PJ[:, :, QA:QA + 256], 4, 32, NCS, NSN, TG, tproj, trt)
        roped = [t_qa]

        def ropes():
            yield
            yield
            for c, nh, cs, sn in ((QA + 256, 4, NCS, NSN), (KA, 1, CS, SN), (KVB + 256, 2, CS, SN), (KVB + 512, 2, CS, SN)):
                roped[0] = rope(G, PJ[:, :, c:c + 64 * nh], PJ[:, :, c:c + 64 * nh], nh, 32, cs, sn, TG, roped[0])
                yield

        rsteps = ropes()

        def gates_hook():
            next(csteps, None)
            next(steps, None)
            next(rsteps, None)

        gsf = [None] * 4
        W.limit = 20 + 16
        n = 0
        for fp in range(8):
            bs = [(4, 5), (6, 7)][fp % 2]
            fd = [None, None]
            gemm_feat(HThi, HTlo, 8, bs, fd, None, hook=gates_hook)
            for f in range(2):
                i = n % 4
                ta = A.do(lambda e, i=i, b=bs[f]: e.activation(GS[i], bank[b][:, :], ACT.Sigmoid), fd[f], gsf[i])
                pf[bs[f]] = ta
                gsf[i] = dma(A, slot(f"gs{i}"), GT[2 * fp + f], GS[i], ta)
                n += 1
        for _ in steps:
            pass
        tsg = A.do(lambda e: e.activation(GNS, PJ[:, :, GB:GB + 24], ACT.Sigmoid))
        phase("cmp")
        for q in (A, V, G):
            q.wait(*gsf)

        M.pos = TM1
        VE = [(M.r(4, 192), M.r(4, 192)) for _ in range(3)]
        VE1 = M.pos
        CM = TM[:, 0, 0:128]
        c0 = G.do(lambda e: e.memset(CM, 0.0))
        CMv = CM.rearrange("p (t n) -> p t n", t=4)
        t_cm = G.do(lambda e: e.affine_select(out=CMv, in_=CMv, compare_op=ALU.is_ge, fill=BIG, base=-31,
                                              pattern=[[P, 4], [-16, 32]], channel_multiplier=1), c0)
        RV = TM[:, 0, 128:132]
        c0 = G.do(lambda e: e.memset(RV, 1.0))
        t_rv = G.do(lambda e: e.affine_select(out=RV, in_=RV, compare_op=ALU.is_ge, fill=0.0, base=-31,
                                              pattern=[[P, 4]], channel_multiplier=1), c0)
        QN = [TM[:, 1, 0:512], TM[:, 1, 512:1024]]
        SC = TM[:, 2, :].rearrange("p (t h n) -> p t h n", t=4, h=8)
        cst = TM[:, 3, 0:256].rearrange("p (a t h) -> p a t h", a=8, t=4)
        qnf, tqn = [None, None], {}

        def queries(pr):
            b = pr % 2
            T.wait(pf[b])
            for t in range(NT):
                tt = T.do(lambda e: e.transpose(bank[b][:, t * P:t * P + P], PJ[:, t, QB + P * pr:QB + P * pr + P], ident))
            pf[b] = tqn[pr] = V.do(lambda e: e.tensor_scalar(QN[pr % 2], bank[b][:, :], -0.125, None, ALU.mult), tt, qnf[pr % 2])

        queries(0)
        queries(1)
        tsc0 = V.do(lambda e: e.memset(SC, 0.0))
        for pr in range(4):
            for t in range(NT):
                ts = T.do(lambda e: e.matmul(bank[2 + t][:, 64 * pr:64 * pr + 64], QN[pr % 2][:, t * P:t * P + P], kcT[:, pr // 2, :],
                                             start=True, stop=True, skip_group_check=True), tqn[pr], pf[2 + t] if pr == 0 else None)
            qnf[pr % 2] = ts
            if pr + 2 < 4:
                queries(pr + 2)
        for t in range(NT):
            bv = bank[2 + t][:, 0:256].rearrange("p (h n) -> p h n", h=8)[:, :, 0:31]
            cm = CMv[:, t, 0:31].unsqueeze(1).broadcast_to([P, 8, 31])
            tsc = V.do(lambda e, t=t, bv=bv, cm=cm: e.tensor_tensor(SC[:, t, :, 0:31], bv, cm, ALU.add), ts, tsc0, t_cm)
            pf[2 + t] = tsc
        SCf = SC.rearrange("p t h n -> p (t h) n")[:, :, 0:31]
        cf = lambda i: cst[:, i, :, :].rearrange("p t h -> p (t h)")
        v = V.do(lambda e: e.tensor_reduce(cf(0), SCf, AX, ALU.min), tsc)
        v = V.do(lambda e: e.tensor_tensor(SCf, SCf, cf(0).unsqueeze(2).broadcast_to([P, 32, 31]), ALU.subtract), v)
        a = A.do(lambda e: e.activation(SCf, SCf, ACT.Exp, scale=-1.0), v)
        for hi_, lo_ in VE:
            for x in (hi_, lo_):
                for c in (0, 128):
                    tz = V.do(lambda e, x=x, c=c: e.tensor_copy(x[:, :, c:c + 64], zeros.rearrange("p (a b) -> p a b", a=4)), t_zero)
        v = V.do(lambda e: e.tensor_reduce(cf(1), SCf, AX, ALU.add), a)
        v = V.do(lambda e: e.reciprocal(cf(2), cf(1)), v)
        v = V.do(lambda e: e.tensor_tensor(cst[:, 3], cst[:, 2], GNS[:, :, 0:8], ALU.mult), v, tsg)
        v = V.do(lambda e: e.tensor_tensor(cst[:, 4], cst[:, 3], RV.unsqueeze(2).broadcast_to([P, 4, 8]), ALU.mult), v, t_rv)
        v = V.do(lambda e: e.tensor_tensor(SCf, SCf, cf(4).unsqueeze(2).broadcast_to([P, 32, 31]), ALU.mult), v)
        for kvh in range(2):
            b = kvh
            T.wait(pf[b], v)
            for t in range(NT):
                tt = T.do(lambda e, t=t, kvh=kvh, b=b: e.transpose(bank[b][:, t * P:t * P + P], SC[:, t, 4 * kvh:4 * kvh + 4, :].rearrange("p h n -> p (h n)"), ident))
            tptc = V.do(lambda e, kvh=kvh, b=b: e.tensor_copy(PTC[kvh], bank[b][:, :]), tt)
            pf[b] = tptc
        tmdone = [v, tt, qnf[0], qnf[1]]
        rope(G, PJ[:, :, QB + 384:QB + 512], PJ[:, :, QB + 384:QB + 512], 2, 32, NCS, NSN, TG, tmdone)
        rope(V, PJ[:, :, QB:QB + 384], PJ[:, :, QB:QB + 384], 6, 32, NCS, NSN, TM, tmdone)
        phase("att")

        M.pos = AT0
        PTb = [(M.r(4, 512), M.r(4, 512))]
        assert M.pos <= TM1
        M.pos = VE1
        KS = [(M.r(512), M.r(512)) for _ in range(3)]
        qH = [M.r(512) for _ in range(2)]
        qS = [M.r(512) for _ in range(3)]
        Ebuf = [M.f(512) for _ in range(4)]
        sm = M.f(3, 8)
        OAB = M.size - 8192
        assert M.pos <= OAB
        M.pos = OAB
        OA = (M.r(4, 512), M.r(4, 512))
        OB = (M.r(4, 512), M.r(4, 512))
        M.pos = ring0
        PTb.append((M.r(4, 512), M.r(4, 512)))
        branches = []
        for h in range(8):
            branches.append(dict(q=("a", h), kv=0, mask="sel", gate=None, par=h % 2, o=OA, pr=h // 2,
                                 first=h % 2 == 0, last=h % 2 == 1, cmp=None))
        for h in range(8):
            for br in range(2):
                branches.append(dict(q=("b", h), kv=1 + 2 * (h // 4) + br, mask="causal", gate=(1 + br) * 8 + h, par=h % 2, o=OB, pr=h // 2,
                                     first=False, last=(h % 2 == 1 and br == 1), cmp=(h // 4, (h % 4) // 2) if (h % 2 == 0 and br == 0) else None))
        kvsrc = [(KA, VA), (KVB + 256, KVB + 384), (KVB + 512, KVB + 640), (KVB + 320, KVB + 448), (KVB + 576, KVB + 704)]
        kvset = [0, 1, 2, 0, 1]
        kvtok, kvfree, kvasked = {}, [None] * 3, set()
        qtok, qfree, qhf = {}, [None] * 3, [None, None]
        qasked = {}
        jobs = []

        def prep_kv(i):
            s = kvset[i]
            kc, vc = kvsrc[i]
            b = 7
            di, d, td = doubled(PJ[:, :, kc:kc + 64], 64, 2)
            yield
            T.wait(pf[b], td)
            for t in range(NT):
                tt = T.do(lambda e, t=t: e.transpose(bank[b][:, t * P:t * P + P], d[:, t, :], ident))
            dupf[di] = tt
            yield
            kh, kl = KS[s]
            vh, vl = VE[s]
            src = PJ[:, :, vc:vc + 64]
            th = A.do(lambda e: e.activation(kh, bank[b][:, :], ACT.Copy), tt, kvfree[s])
            th2 = A.do(lambda e: e.activation(vh[:, :, 64:128], src, ACT.Copy))
            yield
            pf[b] = V.do(lambda e: e.tensor_tensor(kl, bank[b][:, :], fr(kh), ALU.subtract), th, kvfree[s])
            kvtok[i] = V.do(lambda e: e.tensor_tensor(vl[:, :, 64:128], src, fr(vh[:, :, 64:128]), ALU.subtract), th2)

        def prep_q(key):
            i = qasked[key]
            c = (QA if key[0] == "a" else QB) + 64 * key[1]
            res = []
            yield from stack_steps(res, PJ[:, :, c:c + 64], 64, 128, 7, qH[i % 2], qhf[i % 2], qS[i % 3], qfree[i % 3], 0)
            qhf[i % 2] = res[0]
            qtok[key] = (i % 3, res[0])

        def ask(B_):
            if B_["kv"] not in kvasked:
                kvasked.add(B_["kv"])
                jobs.append([prep_kv(B_["kv"]), 0])
            if B_["q"] not in qasked:
                qasked[B_["q"]] = len(qasked)
                jobs.append([prep_q(B_["q"]), 0])
            start()

        def start():
            for j in jobs[0:2]:
                if j[1] == 0 and (j is jobs[0] or jobs[0][1] > 1):
                    j[1] = 1
                    age[0] = 0
                    next(j[0])

        age = [0]

        def work(n):
            age[0] += 1
            for _ in range(n):
                if jobs and (jobs[0][1] > 1 or age[0] > 2 or n > 1):
                    jobs[0][1] += 1
                    if next(jobs[0][0], 0) == 0:
                        jobs.pop(0)
                    start()

        SBK, TBK, OBK = [0, 1], [2, 3, 4], [5, 6]
        nbr = len(branches)
        todo = [(i, qt) for i in range(nbr) for qt in range(NT)]
        NS = len(todo)
        ef = [None] * 4
        tS, tM, tX, tP, tT, tH = {}, {}, {}, {}, {}, {}
        ptf = {}
        pvs = [0]

        def pv_to(n):
            while pvs[0] < min(n, NS):
                pv_part(pvs[0] // 4, pvs[0] % 4)
                pvs[0] += 1

        def pv_part(bi, kt):
            B_ = branches[bi]
            ob = OBK[B_["pr"] % 2]
            ph, pl = PTb[bi % 2]
            vh, vl = VE[kvset[B_["kv"]]]
            sl = slice(64, 192) if B_["par"] == 0 else slice(0, 128)
            T.wait(tH[4 * bi + 3])
            started = kt > 0
            if kt == 0 and (B_["first"] or B_["cmp"]):
                T.wait(pf[ob])
            if kt == 0 and B_["cmp"]:
                kvh, pp = B_["cmp"]
                T.go(lambda e: e.matmul(bank[ob][:, :], BD[:, kvh, pp, :], PTC[kvh], start=True, stop=False, skip_group_check=True), tptc)
                started = True
            cs_ = slice(kt * P, 512)
            for a_, b_ in ((vh, ph), (vl, ph), (vh, pl)):
                st_ = B_["first"] and not started
                started = True
                fin = B_["last"] and kt == 3 and b_ is pl
                tpv = T.do(lambda e: e.matmul(bank[ob][:, cs_], a_[:, kt, sl], b_[:, kt, cs_], start=st_, stop=fin, skip_group_check=True))
            ptf[bi % 2, kt] = tpv
            if kt < 3:
                return
            kvfree[kvset[B_["kv"]]] = tpv
            if B_["last"]:
                oh, ol = B_["o"]
                pr = B_["pr"]
                th = A.do(lambda e: e.activation(oh[:, pr, :], bank[ob][:, :], ACT.Copy), tpv)
                pf[ob] = V.do(lambda e: e.tensor_tensor(ol[:, pr, :], bank[ob][:, :], fr(oh[:, pr, :]), ALU.subtract), th)

        for B_ in branches[0:2]:
            ask(B_)
        work(99)

        for i in range(NS + 11):
            k = i - 1
            if 0 <= k < NS:
                bi, qt = todo[k]
                B_ = branches[bi]
                n = (qt + 1) * P
                sb_ = SBK[k % 2]
                m = DM[:, qt - 1, 0:n] if (B_["mask"] == "sel" and qt > 0) else Mc[:, 384 - qt * P:512]
                E = Ebuf[k % 4]
                c = k % 8
                tM[k] = V.do(lambda e: e.tensor_tensor_reduce(E[:, 0:n], bank[sb_][:, 0:n], m, 1.0, 3e38, ALU.add, ALU.min, sm[:, 0, c:c + 1]),
                             tS[k], ef[k % 4])
                pf[sb_] = tM[k]
            k = i - 5
            if 0 <= k < NS:
                bi, qt = todo[k]
                ph, pl = PTb[bi % 2]
                dh, pv_ = ph[:, 0:qt + 1, qt * P:qt * P + P], bank[TBK[k % 3]][:, 0:(qt + 1) * P].rearrange("p (k n) -> p k n", n=P)
                th5 = A.do(lambda e: e.activation(dh, pv_, ACT.Copy), tT[k], ptf.get((bi % 2, qt)))
            k = i - 1
            if 0 <= k < NS:
                n = (todo[k][1] + 1) * P
                E = Ebuf[k % 4]
                c = k % 8
                tX[k] = A.do(lambda e: e.activation(E[:, 0:n], E[:, 0:n], ACT.Exp, bias=sm[:, 0, c:c + 1], scale=-1.0, accum_out=sm[:, 1, c:c + 1]), tM[k])
            k = i - 2
            if 0 <= k < NS:
                bi, qt = todo[k]
                n = (qt + 1) * P
                E = Ebuf[k % 4]
                c = k % 8
                gate = branches[bi]["gate"]
                tr2 = V.do(lambda e: e.reciprocal(sm[:, 2, c:c + 1], sm[:, 1, c:c + 1]), tX[k])
                g2 = 1.0 if gate is None else GNS[:, qt, gate:gate + 1]
                tP[k] = G.do(lambda e: e.tensor_scalar(E[:, 0:n], E[:, 0:n], sm[:, 2, c:c + 1], g2, ALU.mult, ALU.mult), tr2)
            k = i - 5
            if 0 <= k < NS:
                bi, qt = todo[k]
                ph, pl = PTb[bi % 2]
                dh, dl = ph[:, 0:qt + 1, qt * P:qt * P + P], pl[:, 0:qt + 1, qt * P:qt * P + P]
                pv_ = bank[TBK[k % 3]][:, 0:(qt + 1) * P].rearrange("p (k n) -> p k n", n=P)
                pf[TBK[k % 3]] = tH[k] = V.do(lambda e: e.tensor_tensor(dl, pv_, fr(dh), ALU.subtract), th5)
            if i < NS and todo[i][1] == 0 and branches[todo[i][0]]["kv"] not in kvasked:
                pv_to(4 * (todo[i][0] - 2))
            if i < NS:
                bi, qt = todo[i]
                B_ = branches[bi]
                if qt == 0:
                    ask(B_)
                    while B_["q"] not in qtok or B_["kv"] not in kvtok:
                        work(2)
                    if bi + 2 < nbr and branches[bi + 2]["kv"] < 4:
                        ask(branches[bi + 2])
                n = (qt + 1) * P
                sb_ = SBK[i % 2]
                kh, kl = KS[kvset[B_["kv"]]]
                qs, tq = qtok[B_["q"]]
                T.wait(pf[sb_], tq, kvtok[B_["kv"]])
                T.go(lambda e: e.matmul(bank[sb_][:, 0:n], qS[qs][:, qt * P:qt * P + P], kh[:, 0:n], start=True, stop=False))
                tS[i] = T.do(lambda e: e.matmul(bank[sb_][:, 0:n], qS[qs][:, qt * P:qt * P + P], kl[:, 0:n], start=False, stop=True))
                if qt == 3:
                    qfree[qs] = tS[i]
            k = i - 4
            if 0 <= k < NS:
                qt = todo[k][1]
                E = Ebuf[k % 4]
                tb_ = TBK[k % 3]
                T.wait(pf[tb_], tP[k])
                for kt in range(qt + 1):
                    ef[k % 4] = tT[k] = T.do(lambda e, kt=kt: e.transpose(bank[tb_][:, kt * P:kt * P + P], E[:, kt * P:kt * P + P], ident))
            pv_to(i - 9)
            work(1)
        phase("merge")

        M.pos = FX
        X1 = M.f(4, 1024)
        X1E = M.pos
        MThi, MTlo = M.r(8, 512), M.r(8, 512)
        GL = [M.f(4, 512) for _ in range(2)]
        MM = [M.f(2, 512) for _ in range(2)]
        assert M.pos <= OAB
        W.limit = len(chunks)
        glf = [None, None]
        glt = {}

        def load_gates(i):
            g = GL[i % 2]
            s_ = slot(f"gl{i % 2}")
            dma(A, s_, g[:, 0:2, :], GT[2 * i:2 * i + 2].rearrange("f p n -> p f n"), glf[i % 2])
            glt[i] = dma(A, s_, g[:, 2:4, :], GT[8 + 2 * i:10 + 2 * i].rearrange("f p n -> p f n"))

        load_gates(0)
        load_gates(1)
        for i in range(4):
            fa, fb = [None, None], [None, None]
            o = 4 * (i % 2)
            gemm_feat(OA[0], OA[1], 4, (o, o + 1), fa, None)
            gemm_feat(OB[0], OB[1], 4, (o + 2, o + 3), fb, None)
            for f in range(2):
                ta = V.do(lambda e, f=f, o=o, i=i: e.tensor_tensor(MM[f][:, 0, :], bank[o + f][:, :], GL[i % 2][:, f, :], ALU.mult), fa[f], glt[i])
                pf[o + f] = ta
                tb = V.do(lambda e, f=f, o=o, i=i: e.tensor_tensor(MM[f][:, 1, :], bank[o + 2 + f][:, :], GL[i % 2][:, 2 + f, :], ALU.mult), fb[f])
                pf[o + 2 + f] = tb
                tc = V.do(lambda e, f=f: e.tensor_tensor(MM[f][:, 0, :], MM[f][:, 0, :], MM[f][:, 1, :], ALU.add), tb)
                k = 2 * i + f
                th = V.do(lambda e, f=f, k=k: e.tensor_copy(MThi[:, k, :], MM[f][:, 0, :]), tc)
                tl = V.do(lambda e, f=f, k=k: e.tensor_tensor(MTlo[:, k, :], MM[f][:, 0, :], fr(MThi[:, k, :]), ALU.subtract), th)
            glf[i % 2] = tb
            if i < 2:
                load_gates(i + 2)
        tx = [dma(A, slot("x"), X1, io["x"].rearrange("(t p) n -> p t n", p=P))]

        def ev_out(j, t, b, tk):
            return V.do(lambda e: e.tensor_tensor(X1[:, t, 512 * j:512 * j + 512], b[:, :], X1[:, t, 512 * j:512 * j + 512], ALU.add), tk, tx)

        gemm_tok(MThi, MTlo, 8, 2, 512, 2, [(0, 1, 2, 3), (4, 5, 6, 7)], ev_out, tl)
        phase("route")

        M.pos = X1E
        HThi, HTlo = M.r(8, 512), M.r(8, 512)
        XN = [M.f(1024) for _ in range(2)]
        gB = M.f(1024)
        st = M.f(16)
        scr = M.f(1024)
        wr = M.f(8, 36)
        wrh, wrl = M.r(8, 36), M.r(8, 36)
        br = M.f(36)
        tg = dma(A, slot("g"), gB, io["norm_ffn"].partition_broadcast(P))
        twr = [dma(A, slot("wr"), wr[:, :, 0:4], io["w_group"].rearrange("(k p) n -> p k n", p=P)),
               dma(A, slot("wr"), wr[:, :, 4:36], io["w_expert"].rearrange("(k p) n -> p k n", p=P))]
        tbr = [dma(A, slot("br"), br[:, 0:4], io["b_group"].partition_broadcast(P)),
               dma(A, slot("br"), br[:, 4:36], io["b_expert"].partition_broadcast(P))]
        rs_, nrm, done, th2 = [None] * NT, [None] * NT, [None] * NT, [None] * NT

        def scale2(t):
            nrm[t] = V.do(lambda e: e.scalar_tensor_tensor(out=XN[t % 2], in0=X1[:, t, :], scalar=st[:, t:t + 1], in1=gB,
                                                           op0=ALU.mult, op1=ALU.mult), rs_[t], tg, [done[t - 2][0], th2[t - 2]] if t > 1 else None)
            th2[t] = dma(Y, slot(f"h2{t % 2}"), H2[t * P:t * P + P, :], XN[t % 2], nrm[t])

        skew(NT, *rms_stages(X1, st, scr, [None] * NT, rs_), scale2, *turning(lambda t: XN[t % 2], HThi, HTlo, nrm, done))
        t_h2 = [th2[2], th2[3]]
        tht = [done[t][1] for t in range(NT)]
        t1 = V.do(lambda e: e.tensor_copy(wrh, wr), twr[1])
        t1 = V.do(lambda e: e.tensor_tensor(wrl, wr, fr(wrh), ALU.subtract), t1)
        LG = M.f(4, 36)
        LT_ = M.f(512)
        for k in range(8):
            tk = mm3(bank[4][0:36, :], ((wrh[:, k, :], wrl[:, k, :]), (HThi[:, k, :], HTlo[:, k, :])), k == 0, k == 7, tht, t1, pf[4] if k == 0 else None)
        pf[4] = ta = A.do(lambda e: e.activation(LT_[0:36, :], bank[4][0:36, :], ACT.Copy), tk)
        T.wait(ta, pf[5])
        for t in range(NT):
            tt = T.do(lambda e: e.transpose(bank[5][:, 64 * t:64 * t + 36], LT_[0:36, t * P:t * P + P], ident[0:36, 0:36]))
        tlg = pf[5] = V.do(lambda e: e.tensor_tensor(LG, bank[5][:, 0:256].rearrange("p (t n) -> p t n", t=4)[:, :, 0:36],
                                                     br.unsqueeze(1).broadcast_to([P, 4, 36]), ALU.add), tt, tbr[1])

        RS = M.f(16, 128)
        s4 = M.f(24, 4)
        IO128 = M.f(128)
        UT, ON = M.f(128), M.f(128)
        UTr, ONr, ASr = M.r(128), M.r(128), M.r(4, 32)
        YS = [M.f(1024) for _ in range(2)]
        gi = G.do(lambda e: e.iota(IO128.bitcast(I32), pattern=[[1, 128]], base=0, channel_multiplier=0))
        gi = G.do(lambda e: e.tensor_copy(IO128, IO128.bitcast(I32)), gi)
        gt = G.do(lambda e: e.iota(ti[:, 4:8], pattern=[[P, 4]], base=0, channel_multiplier=1))
        go_ = G.do(lambda e: e.memset(ON, 1.0))
        gu = G.do(lambda e: e.affine_select(out=UT, in_=ON, compare_op=ALU.is_gt, fill=0.0, base=0, pattern=[[1, P]], channel_multiplier=-1), go_)

        def r3(i, n=32):
            return RS[:, i, 0:4 * n].rearrange("p (t n) -> p t n", t=4)

        def bc(x, n):
            return x.unsqueeze(2).broadcast_to([P, 4, n])

        def i3(n):
            return IO128[:, 0:n].unsqueeze(1).broadcast_to([P, 4, n])

        def chain(*fns, first=None):
            v = first
            for f in fns:
                v = V.do(f, v)
            return v

        def first_of(src, n, mx, idx, oh, tmp):
            return [
                lambda e: e.tensor_reduce(mx, src, AX, ALU.max),
                lambda e: e.tensor_tensor(tmp, src, bc(mx, n), ALU.is_equal),
                lambda e: e.tensor_scalar(tmp, tmp, -1000.0, 1000.0, ALU.mult, ALU.add),
                lambda e: e.tensor_tensor(tmp, tmp, i3(n), ALU.add),
                lambda e: e.tensor_reduce(idx, tmp, AX, ALU.min),
                lambda e: e.tensor_tensor(oh, i3(n), bc(idx, n), ALU.is_equal),
            ]

        gl, el = LG[:, :, 0:4], LG[:, :, 4:36]
        goh, oh1, oh2, tmp, em, e2, RK = r3(0, 4), r3(1), r3(2), r3(3), r3(4), r3(5), r3(7)
        gx, gidx, gsum, gp, m1, i1, m2, i2, ex, w1_, w2_, tokf = [s4[:, i, :] for i in range(12)]
        sl_, cl_ = [s4[:, 12 + i, :] for i in range(2)], [s4[:, 14 + i, :] for i in range(2)]
        tr2_ = V.do(lambda e: e.tensor_copy(UTr, UT), gu)
        tr2_ = V.do(lambda e: e.tensor_copy(ONr, ON))
        v = V.do(lambda e: e.tensor_copy(tokf, ti[:, 4:8]), gt)
        v = chain(*first_of(gl, 4, gx, gidx, goh, r3(3, 4)), first=[tlg, gi])
        v = chain(lambda e: e.tensor_tensor(r3(3, 4), gl, bc(gx, 4), ALU.subtract), first=v)
        a = A.do(lambda e: e.activation(r3(11, 4), r3(3, 4), ACT.Exp), v)
        v = chain(lambda e: e.tensor_reduce(gsum, r3(11, 4), AX, ALU.add),
                  lambda e: e.reciprocal(gp, gsum), first=a)
        g8 = goh.unsqueeze(3).broadcast_to([P, 4, 4, 8])
        e4 = lambda x: x.rearrange("p t (g i) -> p t g i", g=4)
        v = chain(lambda e: e.tensor_tensor(e4(em), e4(el), g8, ALU.mult),
                  lambda e: e.tensor_scalar(e4(tmp), g8, BIG, -BIG, ALU.mult, ALU.add),
                  lambda e: e.tensor_tensor(em, em, tmp, ALU.add),
                  *first_of(em, 32, m1, i1, oh1, tmp),
                  lambda e: e.tensor_scalar(tmp, oh1, -3e30, None, ALU.mult),
                  lambda e: e.tensor_tensor(e2, em, tmp, ALU.add),
                  *first_of(e2, 32, m2, i2, oh2, tmp),
                  lambda e: e.tensor_tensor(ASr, oh1, oh2, ALU.add), first=v)
        t_as = v
        v = chain(lambda e: e.tensor_tensor(w1_, m2, m1, ALU.subtract), first=v)
        a = A.do(lambda e: e.activation(ex, w1_, ACT.Exp), v)
        v = chain(lambda e: e.tensor_scalar(w2_, ex, 1.0, None, ALU.add),
                  lambda e: e.reciprocal(w1_, w2_),
                  lambda e: e.tensor_tensor(w1_, w1_, gp, ALU.mult),
                  lambda e: e.tensor_tensor(w2_, w1_, ex, ALU.mult), first=a)
        T.wait(pf[6], pf[7], t_as)
        asf = ASr.rearrange("p t n -> p (t n)")
        T.do(lambda e: e.matmul(bank[6][:, 0:128], UTr, asf, start=True, stop=False, skip_group_check=True))
        for u in (1, 2, 3):
            tk = T.do(lambda e: e.matmul(bank[6][:, 32 * u:128], ONr, asf[:, 0:128 - 32 * u], start=False, stop=u == 3, skip_group_check=True))
        for u in range(NT):
            tk2 = T.do(lambda e: e.matmul(bank[7][:, 0:32], ONr, ASr[:, u, :], start=u == 0, stop=u == 3))
        OV = M.f(8, 32)
        cnt, ovn, s_a, s_b, cex = [OV[:, i, :] for i in range(5)]
        v = chain(lambda e: e.tensor_copy(RK, bank[6][:, 0:128].rearrange("p (t n) -> p t n", t=4)),
                  lambda e: e.tensor_copy(cnt, bank[7][:, 0:32]),
                  lambda e: e.tensor_scalar(ovn, cnt, CAP + 0.5, None, ALU.is_gt),
                  *[f for x in (1, 2, 3) for f in (
                      lambda e, x=x: e.tensor_scalar(s_a, cnt, CAP + 128.0 * x + 0.5, None, ALU.is_gt),
                      lambda e: e.tensor_tensor(ovn, ovn, s_a, ALU.add))],
                  lambda e: e.tensor_copy(s_a, ovn), first=[tk2])
        cur, oth = s_a, s_b
        for sh in (1, 2, 4, 8, 16):
            v = chain(lambda e, c=cur, o=oth, sh=sh: e.tensor_copy(o[:, 0:sh], c[:, 0:sh]),
                      lambda e, c=cur, o=oth, sh=sh: e.tensor_tensor(o[:, sh:32], c[:, sh:32], c[:, 0:32 - sh], ALU.add), first=v)
            cur, oth = oth, cur
        incl = cur
        v = chain(lambda e: e.tensor_tensor(cex, incl, ovn, ALU.subtract), first=v)
        full = r3(12)
        j_ = r3(13)
        fl = r3(14)
        v = chain(lambda e: e.tensor_scalar(tmp, RK, CAP - 0.5, None, ALU.is_gt),
                  lambda e: e.tensor_copy(fl, tmp),
                  *[f for x in (1, 2, 3) for f in (
                      lambda e, x=x: e.tensor_scalar(j_, RK, CAP + 128.0 * x - 0.5, None, ALU.is_gt),
                      lambda e: e.tensor_tensor(fl, fl, j_, ALU.add))],
                  lambda e: e.tensor_scalar(j_, tmp, float(128 - CAP), None, ALU.mult),
                  lambda e: e.tensor_tensor(full, RK, j_, ALU.add),
                  lambda e: e.tensor_scalar(j_, fl, -128.0, None, ALU.mult),
                  lambda e: e.tensor_tensor(full, full, j_, ALU.add),
                  lambda e: e.tensor_tensor(j_, fl, cex.unsqueeze(1).broadcast_to([P, 4, 32]), ALU.add),
                  lambda e: e.tensor_scalar(j_, j_, 31.0, None, ALU.add),
                  lambda e: e.tensor_tensor(j_, j_, i3(32), ALU.subtract),
                  lambda e: e.tensor_tensor(j_, j_, tmp, ALU.mult),
                  lambda e: e.tensor_tensor(j_, j_, i3(32), ALU.add), first=v)
        OHS = YS[0].rearrange("p (k t s) -> p k t s", k=2, t=4)
        RH = [x[:, 0:16 * TCOLS].rearrange("p (t c n) -> p t c n", t=4, c=4) for x in (YS[1], scr)]
        T.wait(pf[5])
        for k, (oh, w) in enumerate(((oh1, w1_), (oh2, w2_))):
            tm2 = r3(8 + k)
            c40 = RH[k][:, :, 3, :]
            v = chain(lambda e: e.tensor_tensor(tmp, full, oh, ALU.mult),
                      lambda e: e.tensor_tensor(tm2, j_, oh, ALU.mult),
                      lambda e: e.tensor_reduce(sl_[k], tmp, AX, ALU.add),
                      lambda e: e.tensor_reduce(cl_[k], tm2, AX, ALU.add),
                      lambda e: e.tensor_tensor(OHS[:, k], i3(128), bc(sl_[k], 128), ALU.is_equal),
                      lambda e: e.tensor_tensor(c40, i3(TCOLS), bc(cl_[k], TCOLS), ALU.is_equal),
                      lambda e: e.tensor_tensor(RH[k][:, :, 0, :], c40, bc(tokf, TCOLS), ALU.mult),
                      lambda e: e.scalar_tensor_tensor(out=RH[k][:, :, 1, :], in0=c40, scalar=float(k * S), in1=RH[k][:, :, 0, :], op0=ALU.mult, op1=ALU.add),
                      lambda e: e.tensor_tensor(RH[k][:, :, 2, :], c40, bc(w, TCOLS), ALU.mult), first=v)
            for t in range(NT):
                tk = T.do(lambda e: e.matmul(bank[5][:, 0:4 * TCOLS], OHS[:, k, t, :], RH[k][:, t].rearrange("p c n -> p (c n)"), start=k == 0 and t == 0,
                                             stop=k == 1 and t == 3), v)
        TBF = M.f(4, TCOLS)
        TBI = M.f(2, TCOLS).bitcast(I32)
        v = V.do(lambda e: e.tensor_copy(TBF, bank[5][:, 0:4 * TCOLS].rearrange("p (c n) -> p c n", c=4)), tk)
        pf[5] = v
        v = chain(lambda e: e.tensor_scalar(TBF[:, 3, :], TBF[:, 3, :], -float(FAR), float(FAR), ALU.mult, ALU.add),
                  lambda e: e.tensor_tensor(TBF[:, 0:2, :], TBF[:, 0:2, :], TBF[:, 3, :].unsqueeze(1).broadcast_to([P, 2, TCOLS]), ALU.add),
                  lambda e: e.tensor_copy(TBI, TBF[:, 0:2, :]), first=v)
        t_tab = v
        OE = M.f(16)
        OI = M.f(16, 10)
        v = V.last()
        for j in range(NOVER):
            v = V.do(lambda e, j=j: e.tensor_scalar(s_b if incl is s_a else s_a, incl, j + 0.5, None, ALU.is_lt), v)
            v = V.do(lambda e, j=j: e.tensor_reduce(OE[:, j:j + 1], s_b if incl is s_a else s_a, AX, ALU.add), v)
        v = V.do(lambda e: e.tensor_scalar(OE[:, 0:NOVER], OE[:, 0:NOVER], 31.0, None, ALU.min), v)
        v = V.do(lambda e: e.tensor_copy(ti[:, 60:61], incl[:, 31:32]), v)
        gi2 = G.do(lambda e: e.iota(ti[:, 48:58], pattern=[[P, 10]], base=0, channel_multiplier=1))
        IOF = M.f(10)
        v = V.do(lambda e: e.tensor_copy(IOF, ti[:, 48:58]), v, gi2)
        v = V.do(lambda e: e.tensor_scalar(IOF[:, 8:10], IOF[:, 8:10], -1024.0, None, ALU.add), v)
        toi = []
        for j in range(NOVER):
            v = V.do(lambda e, j=j: e.scalar_tensor_tensor(out=OI[:, j, 0:8], in0=OE[:, j:j + 1].to_broadcast([P, 8]), scalar=1024.0, in1=IOF[:, 0:8], op0=ALU.mult, op1=ALU.add), v)
            v = V.do(lambda e, j=j: e.scalar_tensor_tensor(out=OI[:, j, 8:10], in0=OE[:, j:j + 1].to_broadcast([P, 2]), scalar=256.0, in1=IOF[:, 8:10], op0=ALU.mult, op1=ALU.add), v)
        OIi = M.f(16, 10).bitcast(I32)
        t_oi = V.do(lambda e: e.tensor_copy(OIi[:, 0:NOVER, :], OI[:, 0:NOVER, :]), v)

        XG = [M.f(1024) for _ in range(2)]
        XT = [(M.r(8, 128), M.r(8, 128)) for _ in range(2)]
        SG = [M.f(256) for _ in range(2)]
        AT = [(M.r(2, 128), M.r(2, 128)) for _ in range(2)]
        xz = [G.do(lambda e, x=x: e.memset(x, 0.0)) for x in XG]
        xgf, ysf = list(xz), [None, None]
        xtf, atf, sgf = [None, None], [None, None], [None, None]
        gtok = {}

        def rows(c):
            return CAP if c < NEXP else P

        def gather(c):
            i = c % 2
            n = rows(c)
            s_ = slot(f"xg{i}")
            G.wait(xgf[i], t_tab, t_h2)
            s_.n += 16
            G.put(lambda e: e.indirect_dma_start(XG[i][0:n, :], None, H2, bass.IndirectOffsetOnAxis(TBI[0:n, 0, c:c + 1].bitcast(U32), 0),
                                                 bounds_check=S - 1, oob_is_err=False).then_inc(s_.key, 16))
            gtok[c] = (s_.key, s_.n)

        tyall = []

        def tokens_in(c):
            i = c % 2
            n = rows(c)
            hi, lo = XT[i]
            w = 512 // n
            for g in range(8 // w):
                b = 4 + (c + g) % 2
                T.wait(pf[b], gtok[c])
                for k in range(w):
                    tt = T.do(lambda e, k=k, g=g, b=b: e.transpose(bank[b][:, k * n:k * n + n], XG[i][0:n, (w * g + k) * P:(w * g + k + 1) * P], ident[0:n, 0:n]))
                pv = bank[b][:, :].rearrange("p (k n) -> p k n", k=w)
                h, l = hi[:, w * g:w * g + w, 0:n], lo[:, w * g:w * g + w, 0:n]
                th = A.do(lambda e, h=h, pv=pv: e.activation(h, pv, ACT.Copy), tt, xtf[i])
                tl = V.do(lambda e, h=h, l=l, pv=pv: e.tensor_tensor(l, pv, fr(h), ALU.subtract), th)
                pf[b] = tl
            xgf[i] = tt
            return tl

        def expert(c, getw, xready):
            i = c % 2
            m = rows(c)
            hi, lo = XT[i]
            b = i
            for s_ in range(4):
                wh, wl_, ready, done = getw()
                for kk in range(2):
                    k = 2 * s_ + kk
                    tk = mm3(bank[b][0:m, :], ((hi[:, k, 0:m], lo[:, k, 0:m]), (wh[:, kk, :], wl_[:, kk, :])), k == 0, k == 7, ready, xready, pf[b] if k == 0 else None)
                done(tk)
                if s_ == 1:
                    yield
            xtf[i] = tk
            ta = A.do(lambda e: e.activation(SG[i][0:m, :], bank[i][0:m, 0:256], ACT.Silu), tk, sgf[i])
            tv = V.do(lambda e: e.tensor_tensor(SG[i][0:m, :], SG[i][0:m, :], bank[i][0:m, 256:512], ALU.mult), ta)
            pf[i] = tv
            yield
            b = 6
            T.wait(pf[b], tv)
            for f in range(2):
                tt = T.do(lambda e, f=f, b=b: e.transpose(bank[b][:, f * m:f * m + m], SG[i][0:m, f * P:f * P + P], ident[0:m, 0:m]))
            sgf[i] = tt
            pv = bank[b][:, 0:2 * m].rearrange("p (k n) -> p k n", k=2)
            ah, al = [x[:, :, 0:m] for x in AT[i]]
            th = A.do(lambda e: e.activation(ah, pv, ACT.Copy), tt, atf[i])
            tl = V.do(lambda e: e.tensor_tensor(al, pv, fr(ah), ALU.subtract), th)
            pf[b] = tl
            yield
            for f in range(2):
                wh, wl_, ready, done = getw()
                for n in range(2):
                    tk = mm3(bank[2 + n][0:m, :], ((ah[:, f, :], al[:, f, :]), (wh[:, 0, 512 * n:512 * n + 512], wl_[:, 0, 512 * n:512 * n + 512])),
                             f == 0, f == 1, ready, tl, pf[2 + n] if f == 0 else None)
                done(tk)
            atf[i] = tk
            wt = TBF[0:m, 2, c:c + 1]
            ty0 = A.do(lambda e: e.activation(YS[i][0:m, 0:512], bank[2][0:m, :], ACT.Copy, scale=wt), tk, ysf[i])
            pf[2] = ty0
            ty1 = A.do(lambda e: e.activation(YS[i][0:m, 512:1024], bank[3][0:m, :], ACT.Copy, scale=wt))
            pf[3] = ty1
            s_ = slot(f"ys{i}")
            G.wait(ty1)
            s_.n += 16
            G.put(lambda e: e.indirect_dma_start(Y2, bass.IndirectOffsetOnAxis(TBI[0:m, 1, c:c + 1].bitcast(U32), 0), YS[i][0:m, :], None,
                                                 bounds_check=2 * S - 1, oob_is_err=False).then_inc(s_.key, 16))
            ysf[i] = (s_.key, s_.n)
            yield

        def ring():
            hi, lo, ready = W.use()
            return hi, lo, ready, W.used_by

        top = M.pos
        M.pos = M.size - 3072
        assert top <= M.pos, (top, M.pos)
        gF, gB, bB = M.f(1024), M.f(1024), M.f(1024)
        tgf = dma(A, slot("g"), gF, io["norm_final"].partition_broadcast(P))
        tgl = [dma(A, slot("lg"), gB, io["ln_in_g_2"].partition_broadcast(P)),
               dma(A, slot("lb"), bB, io["ln_in_b_2"].partition_broadcast(P))]
        M.pos = top
        gather(0)
        gather(1)
        xr = tokens_in(0)
        gather(2)
        before = None
        for c in range(NEXP + 1):
            now = expert(c, ring, xr) if c < NEXP else None
            if now:
                next(now)
            if before:
                next(before)
            if now:
                next(now)
            if c + 1 < NEXP:
                xr = tokens_in(c + 1)
            if c + 3 < NEXP:
                gather(c + 3)
            if before:
                next(before)
            before = now
        phase("over")
        for q in (V, A, G):
            q.wait(*ysf)

        wg_rows = io["w_gate_up"].rearrange("e k n -> (e k) n")
        wd_rows = io["w_down"].rearrange("e k n -> (e k) n")
        OW = [M.f(2, 512) for _ in range(2)]
        OWR = [(M.r(2, 512), M.r(2, 512)) for _ in range(2)]
        assert M.pos <= M.size - 3072
        owf = [[None, None], [None, None]]
        now = [0]

        def over_w(j):
            s = [0]

            def get():
                i = now[0] % 2
                now[0] += 1
                sl_ = slot(f"ow{i}")
                G.wait(owf[i][0], t_oi)
                if s[0] < 4:
                    for kk in range(2):
                        k = 2 * s[0] + kk
                        sl_.n += 16
                        G.put(lambda e, k=k, kk=kk: e.indirect_dma_start(
                            OW[i][:, kk, :], None, wg_rows, bass.IndirectOffsetOnAxis(OIi[:, j, k:k + 1].bitcast(U32), 0)).then_inc(sl_.key, 16))
                    a_, b_ = 2, 512
                else:
                    f = s[0] - 4
                    sl_.n += 16
                    G.put(lambda e: e.indirect_dma_start(
                        OW[i].rearrange("p a b -> p (a b)"), None, wd_rows, bass.IndirectOffsetOnAxis(OIi[:, j, 8 + f:9 + f].bitcast(U32), 0)).then_inc(sl_.key, 16))
                    a_, b_ = 1, 1024
                s[0] += 1
                hi, lo = OWR[i]
                th = A.do(lambda e: e.activation(hi, OW[i], ACT.Copy), (sl_.key, sl_.n), owf[i][1])
                tl = V.do(lambda e: e.tensor_tensor(lo, OW[i], fr(hi), ALU.subtract), th)
                owf[i][0] = tl
                vw = lambda x: x.rearrange("p a b -> p (a b)").rearrange("p (a b) -> p a b", a=a_)

                def done(tk):
                    owf[i][1] = tk
                return vw(hi), vw(lo), [th, tl], done
            return get

        engines = (V, A, T, G)
        novr = ti[0:1, 60:61]
        seen = {q.name: dict(q.seen) for q in engines}
        rows_out = list(ysf)
        many = {q.name: q.eng.value_load(novr, min_val=0, max_val=NOVER) for q in engines}
        kept = {q.name: [] for q in engines}
        for j in range(NOVER):
            for q in engines:
                q.kept = []
            c = NEXP + j
            gather(c)
            for _ in expert(c, over_w(j), tokens_in(c)):
                pass
            ends = [q.last() for q in engines]
            for q in engines:
                q.wait(*[t for t in ends if t], *ysf)
                kept[q.name].append(q.kept)
        for q in engines:
            q.kept = None
            with q.eng.If(many[q.name] > 0):
                for j in range(NOVER):
                    with ExitStack() as also:
                        if j:
                            also.enter_context(q.eng.If(many[q.name] > j))
                        for fn in kept[q.name][j]:
                            fn(q.eng)
            q.seen = seen[q.name]
            q.sem, q.n = newsem(f"{q.name}_join"), 1
            q.eng.sem_inc(q.sem, 1)
        pf[:] = [None] * 8
        Y.wait(*phase("final"), *rows_out)
        M.pos = X1E
        lnb = M.f(64)
        small = M.f(64)
        bdo = M.f(4, 8)
        sel8 = M.f(4, 128)
        TOE = M.f(896)
        lamb = M.f(8)
        LPm = M.f(4, 32)
        subg = M.f(4)
        bfc = M.f(8)
        HThi, HTlo = M.r(8, 512), M.r(8, 512)
        LAY = M.pos
        st = small[:, 0:16]

        YA = [M.f(1024) for _ in range(8)]
        scr = M.f(1024)
        tya = {}
        for t in range(NT):
            for k in range(2):
                tya[t, k] = dma((A, Y)[k], slot(f"ya{t}{k}"), YA[2 * t + k], Y2[k * S + t * P:k * S + t * P + P, :])
        tsum, rs_, nrm, out_, done = ([None] * NT for _ in range(5))

        def pair(t):
            tsum[t] = G.do(lambda e: e.tensor_tensor(YA[2 * t], YA[2 * t], YA[2 * t + 1], ALU.add), tya[t, 0], tya[t, 1])

        def total(t):
            tsum[t] = V.do(lambda e: e.tensor_tensor(X1[:, t, :], X1[:, t, :], YA[2 * t], ALU.add), tsum[t])

        def scale3(t):
            nrm[t] = V.do(lambda e: e.scalar_tensor_tensor(out=X1[:, t, :], in0=X1[:, t, :], scalar=st[:, t:t + 1], in1=gF,
                                                           op0=ALU.mult, op1=ALU.mult), rs_[t], tgf)

        skew(NT, pair, total, *rms_stages(X1, st, scr, tsum, rs_), scale3, *ln_stages(X1, gB, bB, lnb, nrm, tgl, out_),
             *turning(lambda t: X1[:, t, :], HThi, HTlo, out_, done))
        fd0 = [None, None]
        feat_halves(HThi, HTlo, (4, 5), fd0, done)
        phase("lay")

        Hs = X1
        g0 = G.do(lambda e: e.memset(bdo, 0.0))
        g0b = G.do(lambda e: e.memset(sel8, 0.0))
        for pr in range(4):
            for hh in range(2):
                tbo = G.do(lambda e, pr=pr, hh=hh: e.memset(bdo[64 * hh:64 * hh + 64, pr, 2 * pr + hh:2 * pr + hh + 1], 1.0 / 64), G.last())
        tse = G.do(lambda e: e.memset(sel8[0:8, :, :], 1.0), tbo)
        sv = sel8[0:8, :, :].rearrange("p r (h d) -> p r h d", h=2)
        tse = G.do(lambda e: e.affine_select(out=sv, in_=sv, compare_op=ALU.is_equal, fill=0.0, base=0,
                                             pattern=[[-2, 4], [-1, 2], [0, 64]], channel_multiplier=1), tse)
        tio = G.do(lambda e: e.iota(TOE.bitcast(I32), pattern=[[-1, 896]], base=384, channel_multiplier=1))
        SC32 = 32.0 ** -0.5
        ov = io["out"].rearrange("(t p) n -> p t n", p=P)
        tout = []

        for l in range(2):
            lam_init = 0.8 - 0.6 * math.exp(-0.3 * l)
            M.pos = LAY
            CT0 = M.pos
            CThi, CTlo = M.r(8, 512), M.r(8, 512)
            CT1 = M.pos
            tlp = dma(A, slot("lp"), LPm, io["lam_params_2"][l].partition_broadcast(P))
            tsg_ = dma(A, slot("sg"), subg[:, 0:1], io["subln_g_2"][l])
            tbf = dma(A, slot("bf"), bfc[:, 0:4], io["b_f_2"][l])
            tht = None

            uT = (M.r(4, 512), M.r(4, 512))
            AB = (M.r(4, 4, 256), M.r(4, 4, 256))
            C1s = (M.r(256), M.r(256))
            wfR = (M.r(4, 128), M.r(4, 128))
            c1 = M.f(256)
            wf = M.f(4, 128)
            tc1 = dma(A, slot("c1"), c1, io["c_c128"])
            twf = dma(A, slot("wf"), wf, io["w_f_2"][l].rearrange("g c d -> c g d"))
            tu = {}

            def halves(b, hi, lo, tk, *toks):
                th = A.do(lambda e: e.activation(hi, b, ACT.Copy), tk, *toks)
                return V.do(lambda e: e.tensor_tensor(lo, b, fr(hi), ALU.subtract), th)

            for fp in range(2):
                fd = [None, None]
                bs = (4, 5) if fp == 0 else (6, 7)
                if fp == 0:
                    fd = fd0
                else:
                    gemm_feat(HThi, HTlo, 8, bs, fd, tht)
                for f in range(2):
                    g = 2 * fp + f
                    pf[bs[f]] = tu[g] = halves(bank[bs[f]][:, :], uT[0][:, g, :], uT[1][:, g, :], fd[f])
            v = V.do(lambda e: e.tensor_copy(C1s[0], c1), tc1)
            tc1 = V.do(lambda e: e.tensor_tensor(C1s[1], c1, fr(C1s[0]), ALU.subtract), v)
            v = V.do(lambda e: e.tensor_copy(wfR[0], wf), twf)
            twf = V.do(lambda e: e.tensor_tensor(wfR[1], wf, fr(wfR[0]), ALU.subtract), v)
            v = V.do(lambda e: e.tensor_tensor(LPm[:, 0:4:2, :], LPm[:, 0:4:2, :], LPm[:, 1:4:2, :], ALU.mult), tlp)
            v = V.do(lambda e: e.tensor_reduce(lamb[:, 0:2], LPm[:, 0:4:2, :], AX, ALU.add), v)
            a = A.do(lambda e: e.activation(lamb[:, 2:4], lamb[:, 0:2], ACT.Exp), v)
            v = V.do(lambda e: e.tensor_tensor(lamb[:, 4:5], lamb[:, 3:4], lamb[:, 2:3], ALU.subtract), a)
            tlam = V.do(lambda e, li=lam_init: e.tensor_scalar(lamb[:, 5:6], lamb[:, 4:5], -li, None, ALU.add), v)
            tsub = V.do(lambda e, li=lam_init: e.tensor_scalar(subg[:, 1:2], subg[:, 0:1], 1.0 - li, None, ALU.mult), tsg_)
            if l == 0:
                v = V.do(lambda e: e.tensor_copy(TOE, TOE.bitcast(I32)), tio)
                ttoe = V.do(lambda e: e.scalar_tensor_tensor(out=TOE, in0=TOE, scalar=-1.0, in1=TOE, op0=ALU.mult, op1=ALU.max), v)
            n = 0
            for g in range(4):
                for t2 in range(2):
                    b = n % 4
                    n += 1
                    for tt_ in range(2):
                        t = 2 * t2 + tt_
                        sl = slice(t * P, t * P + P)
                        tk = mm3(bank[b][:, 256 * tt_:256 * tt_ + 256], ((uT[0][:, g, sl], uT[1][:, g, sl]), C1s), True, True, tu[g], tc1, pf[b] if tt_ == 0 else None)
                    bv = bank[b][:, :].rearrange("p (t c) -> p t c", t=2)
                    pf[b] = tab = halves(bv, AB[0][:, 2 * t2:2 * t2 + 2, g, :], AB[1][:, 2 * t2:2 * t2 + 2, g, :], tk)
            for cs_ in range(2):
                for s_ in range(2):
                    hi, lo, ready = W.use()
                    for kk in range(2):
                        t = 2 * s_ + kk
                        for g in range(4):
                            c = slice(128 * cs_, 128 * cs_ + 128)
                            tk = mm3(bank[4 + g][:, :], ((AB[0][:, t, g, c], AB[1][:, t, g, c]), (hi[:, kk, :], lo[:, kk, :])),
                                     cs_ == 0 and t == 0, cs_ == 1 and t == 3, ready, tab, pf[4 + g] if (cs_ == 0 and t == 0) else None)
                    W.used_by(tk)
            for g in range(4):
                pf[4 + g] = tu[g] = halves(bank[4 + g][:, :], uT[0][:, g, :], uT[1][:, g, :], tk)
            for g in range(4):
                tk = mm3(bank[g][:, :], ((wfR[0][:, g, :], wfR[1][:, g, :]), (uT[0][:, g, :], uT[1][:, g, :])), True, True, tu[g], twf, pf[g])
                bias = bfc[:, g:g + 1]
                th = V.do(lambda e, g=g, bias=bias: e.tensor_scalar(CThi[:, 4 + g, :], bank[g][:, :], bias, None, ALU.add), tk, tbf)
                pf[g] = V.do(lambda e, g=g, bias=bias: e.scalar_tensor_tensor(out=CTlo[:, 4 + g, :], in0=bank[g][:, :], scalar=bias, in1=fr(CThi[:, 4 + g, :]),
                                                                             op0=ALU.add, op1=ALU.subtract), th)
            phase(f"qkv{l}")
            M.pos = CT1
            QK = M.f(4, 1024)
            VV = (M.r(4, 4, 192), M.r(4, 4, 192))
            for x in VV:
                for t in range(NT):
                    tz = V.do(lambda e, x=x, t=t: e.tensor_copy(x[:, t, :, 64:128], zeros.rearrange("p (a b) -> p a b", a=4)), t_zero)

            A_qk = [None]

            def ev_qkv(j, t, b, tk):
                if j < 2:
                    sc_ = -SC32 if j == 0 else 1.0
                    A_qk[0] = A.do(lambda e: e.activation(QK[:, t, 512 * j:512 * j + 512], b[:, :], ACT.Copy, scale=sc_), tk)
                    return A_qk[0]
                bv = b[:, :].rearrange("p (r h d) -> p r h d", r=4, h=2)
                vv = [x[:, t, :, :].rearrange("p r (c d) -> p r c d", c=3)[:, :, 0:3:2, :] for x in VV]
                return halves(bv, vv[0], vv[1], tk)


            PT2 = [(HThi[:, 0:4, :], HTlo[:, 0:4, :]), (HThi[:, 4:8, :], HTlo[:, 4:8, :])]
            SH = M.r(512)
            QI2 = [CThi[:, i, :] for i in range(4)]
            KI2 = [CTlo[:, i, :] for i in range(4)]
            Eb = [M.f(2, 512) for _ in range(4)]
            AB2 = [M.f(896) for _ in range(2)]
            OO = M.f(4, 512)
            sm2 = M.f(4, 16)
            SQ = [QK[:, t, 0:512] for t in range(NT)]
            gB, bB = Eb[0].rearrange("p a b -> p (a b)"), Eb[1].rearrange("p a b -> p (a b)")
            shf, qif, kif = [None], [None] * 4, [None] * 4
            abf = [None, None]
            gens, prept, tbias = {}, {}, {}

            def part(n):
                if not 0 <= n < 32:
                    return
                if n not in gens:
                    h, c, kind = n // 4, (n // 2) % 2, n % 2
                    dst, fl, mc = ((QI2, qif, 1), (KI2, kif, 2))[kind]
                    i = (2 * h + c) % 4
                    col = 512 * kind + 64 * h + 32 * c

                    def run():
                        res = []
                        yield from stack_steps(res, QK[:, :, col:col + 32], 32, 96, 7, SH, lambda: shf[0], dst[i], lambda: fl[i], mc, tqk[0])
                        shf[0] = prept[n] = res[0]
                    gens[n] = run()
                next(gens[n], None)

            todo = [(h, qt) for h in range(8) for qt in range(NT)]
            NS = len(todo)
            ef = [None] * 4
            ptf = {}
            tS, tM, tX, tL, tR, tE, tT, tH = {}, {}, {}, {}, {}, {}, {}, {}
            SBK, TBK, OBK = [0, 1, 2, 3], [4, 5], 6

            def pv_part(h, kt):
                pr, hh = h // 2, h % 2
                ph, pl = PT2[h % 2]
                sl = slice(64 * hh, 64 * hh + 128)
                T.wait(tH[4 * h + 3])
                if hh == 0 and kt == 0:
                    T.wait(pf[OBK])
                for x_, (a_, b_) in enumerate(((VV[0], ph), (VV[1], ph), (VV[0], pl))):
                    tpv = T.do(lambda e: e.matmul(bank[OBK][:, :], a_[:, kt, pr, sl], b_[:, kt, :], start=(hh == 0 and kt == 0 and x_ == 0),
                                                  stop=(hh == 1 and kt == 3 and x_ == 2), skip_group_check=True))
                ptf[h % 2, kt] = tpv
                if kt < 3:
                    return
                if hh == 1:
                    pf[OBK] = A.do(lambda e: e.activation(OO[:, pr, :], bank[OBK][:, :], ACT.Copy), tpv)

            tqk, early = [None], [-6]

            def late(i):
                part(i + 5)
                part(i + 5)
                if (i + 3) % 4 == 0 and (i + 3) // 4 < 8:
                    h = (i + 3) // 4
                    tbias[h] = A.do(lambda e: e.activation(AB2[h % 2], TOE, ACT.Copy, scale=2.0 ** (-8.0 * (h + 1) / 8)), ttoe, abf[h % 2])

            def before(i):
                part(i + 4)
                part(i + 6)
                late(i)

            def while_values():
                if W.used - w0 > 8:
                    tqk[0] = A_qk[0]
                    before(early[0])
                    early[0] += 1

            w0 = W.used
            gemm_tok(HThi, HTlo, 8, 2, 512, 3, [(0, 1, 2, 3), (4, 5, 6, 7)], ev_qkv, None, hook=while_values)
            for i in range(early[0], NS + 9):
                k = i - 1
                if 0 <= k < NS:
                    h, qt = todo[k]
                    m = AB2[h % 2][:, 384 - qt * P:896 - qt * P]
                    for c in range(2):
                        w = (2 * k + c) % 16
                        sb_ = SBK[(2 * k + c) % 4]
                        tM[k, c] = V.do(lambda e: e.tensor_tensor_reduce(Eb[k % 4][:, c, :], bank[sb_][:, :], m, 1.0, 3e38, ALU.add, ALU.min, sm2[:, 0, w:w + 1]),
                                        tS[k, c], ef[k % 4], tbias[h])
                        pf[sb_] = tM[k, c]
                    if qt == 3:
                        abf[h % 2] = tM[k, 1]
                part(i + 4)
                k = i - 5
                if 0 <= k < NS:
                    h, qt = todo[k]
                    ph, pl = PT2[h % 2]
                    dh, dl = ph[:, :, qt * P:qt * P + P], pl[:, :, qt * P:qt * P + P]
                    pv_ = bank[TBK[k % 2]][:, :].rearrange("p (k n) -> p k n", n=P)
                    tH0 = A.do(lambda e: e.activation(dh, pv_, ACT.Copy), tT[k], [ptf.get((h % 2, x)) for x in range(NT)] if qt == 0 else None)
                k = i - 1
                if 0 <= k < NS:
                    for c in range(2):
                        w = (2 * k + c) % 16
                        tX[k] = A.do(lambda e: e.activation(Eb[k % 4][:, c, :], Eb[k % 4][:, c, :], ACT.Exp, bias=sm2[:, 0, w:w + 1], scale=-1.0,
                                                            accum_out=sm2[:, 1, w:w + 1]), tM[k, c])
                k = i - 2
                if 0 <= k < NS:
                    w = (2 * k) % 16
                    E = Eb[k % 4]
                    tR[k] = V.do(lambda e: e.reciprocal(sm2[:, 2, w:w + 2], sm2[:, 1, w:w + 2]), tX[k])
                    tL[k] = G.do(lambda e: e.tensor_scalar(E[:, 1, :], E[:, 1, :], sm2[:, 2, w + 1:w + 2], lamb[:, 5:6], ALU.mult, ALU.mult), tR[k], tlam)
                    if k % 2:
                        tL[k] = G.do(lambda e: e.tensor_scalar(E[:, 0, :], E[:, 0, :], sm2[:, 2, w:w + 1], 1.0, ALU.mult, ALU.mult))
                k = i - 3
                if 0 <= k < NS:
                    w2_ = (2 * k) % 16
                    E2 = Eb[k % 4]
                    if k % 2:
                        tE[k] = G.do(lambda e: e.tensor_tensor(E2[:, 0, :], E2[:, 0, :], E2[:, 1, :], ALU.add), tL[k])
                    else:
                        tE[k] = V.do(lambda e: e.scalar_tensor_tensor(out=E2[:, 0, :], in0=E2[:, 0, :], scalar=sm2[:, 2, w2_:w2_ + 1], in1=E2[:, 1, :], op0=ALU.mult, op1=ALU.add), tL[k])
                k = i - 5
                if 0 <= k < NS:
                    pf[TBK[k % 2]] = tH[k] = V.do(lambda e: e.tensor_tensor(dl, pv_, fr(dh), ALU.subtract), tH0)
                part(i + 6)
                if 0 <= i < NS:
                    h, qt = todo[i]
                    for c in range(2):
                        sb_ = SBK[(2 * i + c) % 4]
                        qi_ = (2 * h + c) % 4
                        tS[i, c] = T.do(lambda e: e.matmul(bank[sb_][:, :], QI2[qi_][0:96, qt * P:qt * P + P], KI2[qi_][0:96, :], start=True, stop=True),
                                        pf[sb_], prept[4 * h + 3])
                        if qt == 3:
                            qif[qi_] = kif[qi_] = tS[i, c]
                k = i - 4
                if 0 <= k < NS:
                    T.wait(pf[TBK[k % 2]], tE[k])
                    for kt in range(4):
                        ef[k % 4] = tT[k] = T.do(lambda e: e.transpose(bank[TBK[k % 2]][:, kt * P:kt * P + P], Eb[k % 4][:, 0, kt * P:kt * P + P], ident))
                late(i)
                if 9 <= i:
                    pv_part((i - 9) // 4, (i - 9) % 4)
            hadd = {}

            def ev_res(j, t, b, tk):
                d = Hs[:, t, 512 * j:512 * j + 512]
                hadd[t] = tk = V.do(lambda e: e.scalar_tensor_tensor(out=d, in0=d, scalar=ALPHA, in1=b[:, :], op0=ALU.mult, op1=ALU.add), tk)
                if j == 0:
                    ln_half0(Hs, lnb, t, tk)
                return tk

            def wo_chunk(j, k0, first, last, ready_rows):
                hi, lo, ready = W.use()
                for kk in range(2):
                    k = k0 + kk
                    for t in range(NT):
                        sl = slice(t * P, t * P + P)
                        b = 4 + t - 4 * j
                        tk = mm3(bank[b][:, :], ((CThi[:, k, sl], CTlo[:, k, sl]), (hi[:, kk, :], lo[:, kk, :])), first and kk == 0, last and kk == 1,
                                 ready, ready_rows.get(k), pf[b] if first and kk == 0 else None)
                        if last and kk == 1:
                            pf[b] = ev_res(j, t, bank[b], tk)
                W.used_by(tk)

            too = pf[OBK]
            wo_chunk(0, 4, True, False, {})
            for pr in range(4):
                ta = A.do(lambda e: e.activation(SQ[pr], OO[:, pr, :], ACT.Square), too)
                tk = T.do(lambda e: e.matmul(bank[0][0:8, :], bdo[:, pr, :], SQ[pr], start=pr == 0, stop=pr == 3, skip_group_check=True), ta, pf[0], tbo)
            ms, y_, z_ = [Eb[2][0:8, i, :] for i in range(2)] + [Eb[3][0:8, 0, :]]
            v = V.do(lambda e: e.tensor_scalar(ms, bank[0][0:8, :], 1e-5, None, ALU.add), tk)
            pf[0] = v
            a = A.do(lambda e: e.activation(z_, ms, ACT.Sqrt), v)
            v = V.do(lambda e: e.reciprocal(y_, z_), a)
            v = V.do(lambda e: e.tensor_tensor(z_, y_, y_, ALU.mult), v)
            v = V.do(lambda e: e.tensor_tensor(z_, z_, ms, ALU.mult), v)
            v = V.do(lambda e: e.tensor_scalar(z_, z_, -0.5, 1.5, ALU.mult, ALU.add), v)
            g = V.do(lambda e: e.tensor_tensor(y_, y_, z_, ALU.mult), v)
            wo_chunk(0, 6, False, False, {})
            rows = {}
            for pr in range(4):
                b = 1 + pr % 2
                tk = T.do(lambda e: e.matmul(bank[b][:, :], sel8[0:8, pr, :], y_, start=True, stop=True), g, pf[b], tse)
                pf[b] = v = V.do(lambda e: e.scalar_tensor_tensor(out=OO[:, pr, :], in0=OO[:, pr, :], scalar=subg[:, 1:2], in1=bank[b][:, :], op0=ALU.mult, op1=ALU.mult), tk, tsub)
                a = A.do(lambda e: e.activation(CThi[:, pr, :], OO[:, pr, :], ACT.Copy), v)
                rows[pr] = V.do(lambda e: e.tensor_tensor(CTlo[:, pr, :], OO[:, pr, :], fr(CThi[:, pr, :]), ALU.subtract), a)
            wo_chunk(0, 0, False, False, rows)
            wo_chunk(0, 2, False, True, rows)
            tg1 = [dma(A, slot("lg"), gB, io["ln1_g_2"][l:l + 1, :].rearrange("a n -> (a n)").partition_broadcast(P)),
                   dma(A, slot("lb"), bB, io["ln1_b_2"][l:l + 1, :].rearrange("a n -> (a n)").partition_broadcast(P))]
            for n_, k in enumerate((4, 6, 0, 2)):
                wo_chunk(1, k, n_ == 0, n_ == 3, rows)
            out_, done = [None] * NT, [None] * NT
            skew(NT, *ln_stages(Hs, gB, bB, lnb, hadd, tg1, out_, True), *turning(lambda t: Hs[:, t, :], HThi, HTlo, out_, done, (4, 5, 6, 7)))
            fa0 = [None, None]
            feat_halves(HThi, HTlo, (0, 1), fa0, done)
            phase(f"ffn{l}")
            M.pos = LAY
            FAh, FAl = M.r(22, 512), M.r(22, 512)
            gB, bB = M.f(1024), M.f(1024)
            SL = [M.f(512) for _ in range(2)]
            UP = [M.f(512) for _ in range(2)]
            tg1 = [dma(A, slot("lg"), gB, io["ln2_g_2"][l:l + 1, :].rearrange("a n -> (a n)").partition_broadcast(P)),
                   dma(A, slot("lb"), bB, io["ln2_b_2"][l:l + 1, :].rearrange("a n -> (a n)").partition_broadcast(P))]
            tht = None
            slf, upf = [None] * 2, [None] * 2
            for i in range(11):
                o = 4 * (i % 2)
                fa, fb = [None, None], [None, None]
                if i == 0:
                    fa = fa0
                else:
                    gemm_feat(HThi, HTlo, 8, (o, o + 1), fa, tht)
                s2 = []
                for f in range(2):
                    k = f
                    ta = A.do(lambda e, k=k, b=o + f: e.activation(SL[k], bank[b][:, :], ACT.Silu), fa[f], slf[k])
                    pf[o + f] = ta
                    s2.append((k, ta))
                gemm_feat(HThi, HTlo, 8, (o + 2, o + 3), fb, tht)
                for f in range(2):
                    k, ta = s2[f]
                    u = UP[f]
                    tv = V.do(lambda e, k=k, b=o + 2 + f, u=u: e.tensor_tensor(u, bank[b][:, :], SL[k], ALU.mult), fb[f], ta, upf[f])
                    pf[o + 2 + f] = tv
                    slf[k] = tv
                    th = A.do(lambda e, u=u, i=i, f=f: e.activation(FAh[:, 2 * i + f, :], u, ACT.Copy), tv)
                    tl = G.do(lambda e, u=u, i=i, f=f: e.tensor_tensor(FAl[:, 2 * i + f, :], u, fr(FAh[:, 2 * i + f, :]), ALU.subtract), th)
                    upf[f] = tl
            gemm_tok(FAh, FAl, 22, 2, 512, 2, [(0, 1, 2, 3), (4, 5, 6, 7)], ev_res, tl)
            out_, done = [None] * NT, [None] * NT
            lns = ln_stages(Hs, gB, bB, lnb, hadd, tg1, out_, True)
            if l == 0:
                skew(NT, *lns, *turning(lambda t: Hs[:, t, :], HThi, HTlo, out_, done))
                fd0 = [None, None]
                feat_halves(HThi, HTlo, (4, 5), fd0, done)
            else:
                skew(NT, *lns, lambda t: tout.append(dma(Y, slot(f"out{t}"), ov[:, t, :], Hs[:, t, :], out_[t])))
            phase(f"end{l}")
        Y.wait(*tout)

        assert W.used == len(chunks), (W.used, len(chunks))


_INS = ["x", "c_pos", "c_invf", "norm_mix", "w_in", "pe_k", "w1_k", "w2_k", "pe_v", "w1_v", "w2_v", "w_br_a", "w_br_b", "w_out",
        "norm_ffn", "w_group", "b_group", "w_expert", "b_expert", "w_gate_up", "w_down", "norm_final", "ln_in_g_2", "ln_in_b_2",
        "w_in_2", "lam_params_2", "subln_g_2", "w_f_2", "b_f_2", "w_o_2", "ln1_g_2", "ln1_b_2", "w_gu_2", "w_down_2", "ln2_g_2",
        "ln2_b_2", "c_cos", "c_sin", "c_c128"]


def constants():
    inv = (10000.0 ** (-np.arange(32, dtype=np.float64) / 32)).astype(np.float32)
    s = np.arange(S)
    w = 2 * np.pi * ((s[:, None] * s[None, :]) % S) / S
    c = np.arange(P)
    v = 2 * np.pi * ((c[:, None] * c[None, :]) % P) / P
    return {
        "c_invf": np.ascontiguousarray(np.broadcast_to(inv, (P, 32))),
        "c_cos": (np.cos(w) / np.sqrt(S)).astype(np.float32),
        "c_sin": (np.sin(w) / np.sqrt(S)).astype(np.float32),
        "c_c128": np.concatenate([np.cos(v), -np.sin(v)], axis=1).astype(np.float32) * np.float32(1.0) / np.float32(np.sqrt(P)),
    }


def lay_out(inputs):
    a = {k: np.asarray(v) for k, v in inputs.items()}
    for n in ("norm_mix", "w_in", "w1_k", "w2_k", "w1_v", "w2_v", "w_br_a", "w_br_b", "w_out", "norm_ffn", "w_group",
              "b_group", "w_expert", "b_expert", "w_gate_up", "w_down"):
        a[n] = a[n][0]
    a["x"] = a["x"][0]
    a["c_pos"] = a.pop("positions").reshape(NT, P).T
    for n in ("pe_k", "pe_v"):
        a[n] = a[n][0].reshape(16, P).T
    a["subln_g_2"] = np.tile(a["subln_g_2"], (1, 2)).reshape(2, P, 1)
    a["b_f_2"] = a["b_f_2"].reshape(2, 4, P).transpose(0, 2, 1)
    a.update(constants())
    return {n: np.ascontiguousarray(a[n]) for n in _INS}


def kernel(**inputs):
    import concourse.bacc as bacc
    from concourse.bass_utils import run_bass_kernel_spmd

    nc = bacc.Bacc("TRN2", target_bir_lowering=False, num_devices=1)
    arrays = lay_out(inputs)
    io = {n: nc.dram_tensor("in_" + n, a.shape, mybir.dt.from_np(a.dtype), kind="ExternalInput").ap() for n, a in arrays.items()}
    io["out"] = nc.dram_tensor("out_y", (S, D), F32, kind="ExternalOutput").ap()
    build_program(nc, io)
    r = run_bass_kernel_spmd(nc, [{"in_" + n: a for n, a in arrays.items()}], core_ids=[0])
    return r.results[0]["out_y"].reshape(1, S, D)
```
